# Optimizing a Trainium2 kernel written in Bass

```python
import math
import jax, jax.numpy as jnp
from jax import lax
import numpy as np

D_MODEL = 1024
BATCH = 1
SEQ = 256
DEPTH = 2

D_SSD = D_MODEL
SSD_HEADDIM = 64
SSD_HEADS = D_SSD // SSD_HEADDIM
SSD_GROUPS = 4
HEADS_PER_GROUP = SSD_HEADS // SSD_GROUPS
SSD_STATE = 128
CHUNK = 128
CONV_WIDTH = 3
CONV_XBC = D_SSD + 2 * SSD_GROUPS * SSD_STATE
D_SC = D_MODEL
SC_GROUPS = 16
D_MIX = D_SSD + D_SC
D_FF = ((8 * D_MODEL // 3 + 255) // 256) * 256
RMS_EPS = 1e-5
DT_MIN = 1e-3
DT_MAX = 1e-1
IN_COLS = D_SSD + CONV_XBC + 2 * SSD_HEADS + 3 * D_SC
SPLIT_POINTS = (D_SSD,
                D_SSD + CONV_XBC,
                D_SSD + CONV_XBC + SSD_HEADS,
                D_SSD + CONV_XBC + 2 * SSD_HEADS,
                D_SSD + CONV_XBC + 2 * SSD_HEADS + D_SC,
                D_SSD + CONV_XBC + 2 * SSD_HEADS + 2 * D_SC)


def rms_norm(x, w):
    xf = x.astype(jnp.float32)
    y = xf * lax.rsqrt(jnp.mean(xf * xf, axis=-1, keepdims=True) + RMS_EPS)
    return (y * w.astype(jnp.float32)).astype(x.dtype)

def dwconv_centred(u, w, b=None):
    k = w.shape[0]
    half = k // 2
    length = u.shape[1]
    up = jnp.pad(u, ((0, 0), (half, half), (0, 0)))
    out = up[:, 0:length] * w[0]
    for i in range(1, k):
        out = out + up[:, i:i + length] * w[i]
    if b is not None:
        out = out + b
    return out

def ssd_chunked(xdt, a, bm, cm):
    bsz, length, g, r, p = xdt.shape
    n = bm.shape[-1]
    c = length // CHUNK
    xdt = xdt.reshape(bsz, c, CHUNK, g, r, p)
    a = a.reshape(bsz, c, CHUNK, g, r)
    bm = bm.reshape(bsz, c, CHUNK, g, n)
    cm = cm.reshape(bsz, c, CHUNK, g, n)
    a_cs = jnp.cumsum(a, axis=2)
    seg = a_cs[:, :, :, None] - a_cs[:, :, None, :]
    mask = jnp.tril(jnp.ones((CHUNK, CHUNK), dtype=bool))[:, :, None, None]
    decay_ls = jnp.exp(jnp.where(mask, seg, -jnp.inf))
    scores = jnp.einsum('bclgn,bcsgn->bclsg', cm, bm)
    y_diag = jnp.einsum('bclsgr,bcsgrp->bclgrp', scores[..., None] * decay_ls, xdt)
    decay_to_end = jnp.exp(a_cs[:, :, -1:] - a_cs)
    states = jnp.einsum('bclgn,bclgrp->bcgrpn', bm, xdt * decay_to_end[..., None])
    chunk_decay = jnp.exp(a_cs[:, :, -1])

    def step(hstate, inp):
        s_c, d_c = inp
        return hstate * d_c[..., None, None] + s_c, hstate

    h0 = jnp.zeros((bsz, g, r, p, n), dtype=xdt.dtype)
    _, h_prev = lax.scan(step, h0, (jnp.moveaxis(states, 1, 0), jnp.moveaxis(chunk_decay, 1, 0)))
    h_prev = jnp.moveaxis(h_prev, 0, 1)
    y_off = jnp.einsum('bclgn,bcgrpn->bclgrp', cm, h_prev) * jnp.exp(a_cs)[..., None]
    return (y_diag + y_off).reshape(bsz, length, g, r, p)

def ssd_branch(z, xbc, dt_f_raw, dt_b_raw, conv_w, conv_b, dt_bias_f, dt_bias_b,
               a_log_f, a_log_b, d_skip, norm_w):
    f32 = jnp.float32
    bsz, length, _ = z.shape
    xbc = jax.nn.silu(dwconv_centred(xbc, conv_w, conv_b))
    xs, bm, cm = jnp.split(xbc, [D_SSD, D_SSD + SSD_GROUPS * SSD_STATE], axis=-1)
    xs = xs.astype(f32).reshape(bsz, length, SSD_GROUPS, HEADS_PER_GROUP, SSD_HEADDIM)
    bm = bm.astype(f32).reshape(bsz, length, SSD_GROUPS, SSD_STATE)
    cm = cm.astype(f32).reshape(bsz, length, SSD_GROUPS, SSD_STATE)

    def discretise(dt_raw, dt_bias, a_log):
        dt = jax.nn.softplus(dt_raw.astype(f32) + dt_bias.astype(f32))
        dt = dt.reshape(bsz, length, SSD_GROUPS, HEADS_PER_GROUP)
        a = -jnp.exp(a_log.astype(f32)).reshape(SSD_GROUPS, HEADS_PER_GROUP) * dt
        return xs * dt[..., None], a

    xdt_f, a_f = discretise(dt_f_raw, dt_bias_f, a_log_f)
    xdt_b, a_b = discretise(dt_b_raw, dt_bias_b, a_log_b)
    flip = lambda t: jnp.flip(t, axis=1)
    y_f = ssd_chunked(xdt_f, a_f, bm, cm)
    y_b = flip(ssd_chunked(flip(xdt_b), flip(a_b), flip(bm), flip(cm)))
    y = y_f + y_b + xs * d_skip.astype(f32).reshape(SSD_GROUPS, HEADS_PER_GROUP)[..., None]
    y = y.reshape(bsz, length, D_SSD) * jax.nn.silu(z.astype(f32))
    yg = y.reshape(bsz, length, SSD_GROUPS, D_SSD // SSD_GROUPS)
    yg = yg * lax.rsqrt(jnp.mean(yg * yg, axis=-1, keepdims=True) + RMS_EPS)
    return (yg.reshape(bsz, length, D_SSD) * norm_w.astype(f32)).astype(z.dtype)

def short_conv_branch(sc_b, sc_c, sc_v, conv_w):
    return sc_b * dwconv_centred(sc_c * sc_v, conv_w)

def conv_ffn(n, w_up, conv_w, conv_b, w_down):
    u = jnp.einsum('bld,df->blf', n, w_up)
    u = dwconv_centred(u, conv_w, conv_b)
    gate, up = jnp.split(u, 2, axis=-1)
    return jnp.einsum('blf,fd->bld', jax.nn.silu(gate) * up, w_down)

def _dt_bias_init(k, shape):
    u = jax.random.uniform(k, shape, jnp.float32)
    dt = jnp.exp(u * (math.log(DT_MAX) - math.log(DT_MIN)) + math.log(DT_MIN))
    return dt + jnp.log(-jnp.expm1(-dt))

def first_inputs(seed: int = 0) -> dict:
    key = jax.random.key(seed)
    ks = jax.random.split(key, 20)
    f32 = jnp.float32
    nrm = lambda k, shape, scale: jax.random.normal(k, shape, f32) * scale
    gain = lambda k, shape: 1.0 + 0.01 * jax.random.normal(k, shape, f32)
    return {
        'x': jax.random.normal(ks[0], (BATCH, SEQ, D_MODEL), f32),
        'w_in': nrm(ks[1], (DEPTH, D_MODEL, IN_COLS), D_MODEL ** -0.5),
        'conv_xbc_w': nrm(ks[2], (DEPTH, CONV_WIDTH, CONV_XBC), CONV_WIDTH ** -0.5),
        'conv_xbc_b': nrm(ks[3], (DEPTH, CONV_XBC), 0.01),
        'dt_bias_f': _dt_bias_init(ks[4], (DEPTH, SSD_HEADS)),
        'dt_bias_b': _dt_bias_init(ks[5], (DEPTH, SSD_HEADS)),
        'a_log_f': jnp.log(jax.random.uniform(ks[6], (DEPTH, SSD_HEADS), f32, 1.0, 16.0)),
        'a_log_b': jnp.log(jax.random.uniform(ks[7], (DEPTH, SSD_HEADS), f32, 1.0, 16.0)),
        'd_skip': gain(ks[8], (DEPTH, SSD_HEADS)),
        'ssd_norm_w': gain(ks[9], (DEPTH, D_SSD)),
        'sc_conv_w': nrm(ks[10], (DEPTH, CONV_WIDTH, D_SC), CONV_WIDTH ** -0.5),
        'w_out': nrm(ks[11], (DEPTH, D_MIX, D_MODEL), D_MIX ** -0.5),
        'norm1_w': gain(ks[12], (DEPTH, D_MODEL)),
        'norm2_w': gain(ks[13], (DEPTH, D_MODEL)),
        'w_ffn_up': nrm(ks[14], (DEPTH, D_MODEL, 2 * D_FF), D_MODEL ** -0.5),
        'ffn_conv_w': nrm(ks[15], (DEPTH, CONV_WIDTH, 2 * D_FF), CONV_WIDTH ** -0.5),
        'ffn_conv_b': nrm(ks[16], (DEPTH, 2 * D_FF), 0.01),
        'w_ffn_down': nrm(ks[17], (DEPTH, D_FF, D_MODEL), D_FF ** -0.5),
        'final_norm_w': gain(ks[18], (D_MODEL,)),
    }

def first_block(x, w_in, conv_xbc_w, conv_xbc_b, dt_bias_f, dt_bias_b, a_log_f, a_log_b,
              d_skip, ssd_norm_w, sc_conv_w, w_out, norm1_w, norm2_w, w_ffn_up,
              ffn_conv_w, ffn_conv_b, w_ffn_down, final_norm_w):
    h = x
    for l in range(DEPTH):
        n = rms_norm(h, norm1_w[l])
        proj = jnp.einsum('bld,de->ble', n, w_in[l])
        z, xbc, dt_f, dt_b, sc_b, sc_c, sc_v = jnp.split(proj, SPLIT_POINTS, axis=-1)
        y_ssd = ssd_branch(z, xbc, dt_f, dt_b, conv_xbc_w[l], conv_xbc_b[l],
                           dt_bias_f[l], dt_bias_b[l], a_log_f[l], a_log_b[l],
                           d_skip[l], ssd_norm_w[l])
        y_sc = short_conv_branch(sc_b, sc_c, sc_v, sc_conv_w[l])
        mix = jnp.concatenate([y_ssd, y_sc], axis=-1)
        h = h + jnp.einsum('ble,ed->bld', mix, w_out[l])
        n = rms_norm(h, norm2_w[l])
        h = h + conv_ffn(n, w_ffn_up[l], ffn_conv_w[l], ffn_conv_b[l], w_ffn_down[l])
    return rms_norm(h, final_norm_w)


_first_inputs = first_inputs


def first_inputs(seed=0):
    import zlib

    import numpy as np

    out = dict(_first_inputs(seed))
    spreads = {}
    factors = {'conv_xbc_b': 36.408,
     'd_skip': 64.0,
     'ssd_norm_w': 55.792,
     'norm1_w': 3.165,
     'norm2_w': 20.19,
     'ffn_conv_b': 20.331,
     'final_norm_w': 33.875}
    for name, (base, spread) in spreads.items():
        noise = np.random.default_rng([zlib.crc32(name.encode()), seed]).standard_normal(out[name].shape)
        drawn = base * np.exp(spread * noise) if base else spread * noise
        out[name] = __import__('jax').numpy.asarray(drawn.astype(out[name].dtype))
    for name, factor in factors.items():
        out[name] = (out[name] * factor).astype(out[name].dtype)
    return out


_narrow_inputs = first_inputs


def first_inputs(seed=0):

    out = dict(_narrow_inputs(seed))
    wider = {'d_skip': 11.95,
     'ssd_norm_w': 4.17,
     'norm2_w': 3.09,
     'ffn_conv_b': 3.08,
     'final_norm_w': 6.53}
    for name, times in wider.items():
        mean = out[name].mean()
        out[name] = (mean + times * (out[name] - mean)).astype(out[name].dtype)
    return out


HEAD_DIM = 64
POOL_WIDTH = D_MODEL // 4
POOL_WINDOWS = (2, 4, 8, 16)
N_POOL_GROUPS = len(POOL_WINDOWS)
POOL_GROUP_DIM = POOL_WIDTH // N_POOL_GROUPS
CONV_WIDTH_2 = (3 * D_MODEL) // 8
CONV_KERNEL = 31
SGU_WIDTH = D_MODEL - POOL_WIDTH - CONV_WIDTH_2
SGU_HEADS = SGU_WIDTH // HEAD_DIM
D_MIX_2 = POOL_WIDTH + CONV_WIDTH_2 + SGU_WIDTH
D_IN = POOL_WIDTH + 2 * CONV_WIDTH_2 + 2 * SGU_WIDTH
D_FF_2 = ((8 * D_MODEL // 3 + 127) // 128) * 128
N_EXPERTS = 8
TOP_K = 2
D_FF_EXPERT = 7 * D_MODEL // 2
N_MOD = 6
EPS = 1e-6


def rms_norm_2(x, g):
    xf = x.astype(jnp.float32)
    y = xf * lax.rsqrt(jnp.mean(xf * xf, axis=-1, keepdims=True) + EPS)
    return (y * g.astype(jnp.float32)).astype(x.dtype)

def layer_norm(x, g, b):
    xf = x.astype(jnp.float32)
    mu = jnp.mean(xf, axis=-1, keepdims=True)
    var = jnp.mean(jnp.square(xf - mu), axis=-1, keepdims=True)
    y = (xf - mu) * lax.rsqrt(var + EPS) * g.astype(jnp.float32) + b.astype(jnp.float32)
    return y.astype(x.dtype)

def multiscale_pool(a, pool_w, pool_scale):
    S = a.shape[1]
    af = a.astype(jnp.float32)
    cs = jnp.pad(jnp.cumsum(af, axis=1), ((0, 0), (1, 0), (0, 0)))
    t = jnp.arange(S)
    outs = []
    for g, w in enumerate(POOL_WINDOWS):
        half = w // 2
        hi = jnp.clip(t + half, 0, S)
        lo = jnp.clip(t - half, 0, S)
        sl = slice(g * POOL_GROUP_DIM, (g + 1) * POOL_GROUP_DIM)
        cs_g = cs[:, :, sl]
        win_sum = jnp.take(cs_g, hi, axis=1) - jnp.take(cs_g, lo, axis=1)
        count = (hi - lo).astype(jnp.float32)[None, :, None]
        diff = (win_sum / count - af[:, :, sl]).astype(a.dtype)
        outs.append(jnp.einsum('bsc,cd->bsd', diff, pool_w[g]))
    return jnp.concatenate(outs, axis=-1) * pool_scale

def conformer_conv(p, conv_w, conv_b, ln_g, ln_b):
    val, gate = jnp.split(p, 2, axis=-1)
    glu = val * jax.nn.sigmoid(gate)
    y = lax.conv_general_dilated(
        glu, conv_w[:, None, :], window_strides=(1,),
        padding=[(CONV_KERNEL // 2, CONV_KERNEL // 2)],
        dimension_numbers=('NWC', 'WIO', 'NWC'),
        feature_group_count=CONV_WIDTH_2) + conv_b
    return jax.nn.silu(layer_norm(y, ln_g, ln_b))

def spatial_gating(p, ln_g, ln_b, sgu_w, sgu_b):
    B, S, _ = p.shape
    u, v = jnp.split(p, 2, axis=-1)
    v = layer_norm(v, ln_g, ln_b).reshape(B, S // CHUNK, CHUNK, SGU_HEADS, HEAD_DIM)
    mixed = jnp.einsum('hpq,bnqhd->bnphd', sgu_w, v) + sgu_b.T[:, :, None]
    return u * mixed.reshape(B, S, SGU_WIDTH)

def swiglu(h, w_gate, w_up, w_down):
    return (jax.nn.silu(h @ w_gate) * (h @ w_up)) @ w_down

def moe_swiglu(h, router_w, router_b, w_gate, w_up, w_down):
    logits = jnp.einsum('bsd,de->bse', h.astype(jnp.float32), router_w.astype(jnp.float32)) \
        + router_b.astype(jnp.float32)
    top_vals, top_idx = lax.top_k(logits, TOP_K)
    top_w = jax.nn.softmax(top_vals, axis=-1)
    combine = jnp.sum(jax.nn.one_hot(top_idx, N_EXPERTS, dtype=jnp.float32) * top_w[..., None], axis=-2)
    combine = combine.astype(h.dtype)
    y = jnp.zeros_like(h)
    for e in range(N_EXPERTS):
        y = y + combine[..., e:e + 1] * swiglu(h, w_gate[e], w_up[e], w_down[e])
    return y

def second_inputs(seed: int = 0) -> dict:
    key = jax.random.key(seed)
    ks = jax.random.split(key, 32)
    n_dense = (DEPTH + 1) // 2
    n_moe = DEPTH // 2

    def nrm(k, shape, fan_in):
        return jax.random.normal(k, shape, jnp.float32) * (fan_in ** -0.5)

    def near_one(k, shape):
        return 1.0 + 0.1 * jax.random.normal(k, shape, jnp.float32)

    def small(k, shape):
        return 0.02 * jax.random.normal(k, shape, jnp.float32)

    return {
        "x": jax.random.normal(ks[0], (BATCH, SEQ, D_MODEL), jnp.float32),
        "c": jax.random.normal(ks[1], (BATCH, D_MODEL), jnp.float32),
        "ada_w": nrm(ks[2], (DEPTH, D_MODEL, N_MOD * D_MODEL), D_MODEL),
        "ada_b": small(ks[3], (DEPTH, N_MOD * D_MODEL)),
        "mix_norm_g": near_one(ks[4], (DEPTH, D_MODEL)),
        "ffn_norm_g": near_one(ks[5], (DEPTH, D_MODEL)),
        "w_in": nrm(ks[6], (DEPTH, D_MODEL, D_IN), D_MODEL),
        "pool_w": nrm(ks[7], (DEPTH, N_POOL_GROUPS, POOL_GROUP_DIM, POOL_GROUP_DIM), POOL_GROUP_DIM),
        "pool_scale": near_one(ks[8], (DEPTH, POOL_WIDTH)),
        "conv_w": nrm(ks[9], (DEPTH, CONV_KERNEL, CONV_WIDTH_2), CONV_KERNEL),
        "conv_b": small(ks[10], (DEPTH, CONV_WIDTH_2)),
        "conv_ln_g": near_one(ks[11], (DEPTH, CONV_WIDTH_2)),
        "conv_ln_b": small(ks[12], (DEPTH, CONV_WIDTH_2)),
        "sgu_ln_g": near_one(ks[13], (DEPTH, SGU_WIDTH)),
        "sgu_ln_b": small(ks[14], (DEPTH, SGU_WIDTH)),
        "sgu_w": nrm(ks[15], (DEPTH, SGU_HEADS, CHUNK, CHUNK), CHUNK),
        "sgu_b": near_one(ks[16], (DEPTH, SGU_HEADS, CHUNK)),
        "w_out": nrm(ks[17], (DEPTH, D_MIX_2, D_MODEL), D_MIX_2),
        "ffn_w_gate": nrm(ks[18], (n_dense, D_MODEL, D_FF_2), D_MODEL),
        "ffn_w_up": nrm(ks[19], (n_dense, D_MODEL, D_FF_2), D_MODEL),
        "ffn_w_down": nrm(ks[20], (n_dense, D_FF_2, D_MODEL), D_FF_2),
        "router_w": nrm(ks[21], (n_moe, D_MODEL, N_EXPERTS), D_MODEL),
        "router_b": 0.01 * jax.random.normal(ks[22], (n_moe, N_EXPERTS), jnp.float32),
        "moe_w_gate": nrm(ks[23], (n_moe, N_EXPERTS, D_MODEL, D_FF_EXPERT), D_MODEL),
        "moe_w_up": nrm(ks[24], (n_moe, N_EXPERTS, D_MODEL, D_FF_EXPERT), D_MODEL),
        "moe_w_down": nrm(ks[25], (n_moe, N_EXPERTS, D_FF_EXPERT, D_MODEL), D_FF_EXPERT),
        "final_norm_g": near_one(ks[26], (D_MODEL,)),
    }

def second_block(x, c, ada_w, ada_b, mix_norm_g, ffn_norm_g, w_in, pool_w, pool_scale,
              conv_w, conv_b, conv_ln_g, conv_ln_b, sgu_ln_g, sgu_ln_b, sgu_w, sgu_b, w_out,
              ffn_w_gate, ffn_w_up, ffn_w_down, router_w, router_b,
              moe_w_gate, moe_w_up, moe_w_down, final_norm_g):
    cond = jax.nn.silu(c)
    for l in range(DEPTH):
        mod = cond @ ada_w[l] + ada_b[l]
        mods = jnp.split(mod[:, None, :], N_MOD, axis=-1)
        shift_m, scale_m, gate_m, shift_f, scale_f, gate_f = mods

        h = rms_norm_2(x, mix_norm_g[l]) * (1.0 + scale_m) + shift_m
        proj = h @ w_in[l]
        p_pool, p_conv, p_sgu = jnp.split(proj, [POOL_WIDTH, POOL_WIDTH + 2 * CONV_WIDTH_2], axis=-1)
        out_a = multiscale_pool(p_pool, pool_w[l], pool_scale[l])
        out_b = conformer_conv(p_conv, conv_w[l], conv_b[l], conv_ln_g[l], conv_ln_b[l])
        out_c = spatial_gating(p_sgu, sgu_ln_g[l], sgu_ln_b[l], sgu_w[l], sgu_b[l])
        mixed = jnp.concatenate([out_a, out_b, out_c], axis=-1)
        x = x + gate_m * (mixed @ w_out[l])

        h = rms_norm_2(x, ffn_norm_g[l]) * (1.0 + scale_f) + shift_f
        i = l // 2
        if l % 2 == 0:
            y = swiglu(h, ffn_w_gate[i], ffn_w_up[i], ffn_w_down[i])
        else:
            y = moe_swiglu(h, router_w[i], router_b[i], moe_w_gate[i], moe_w_up[i], moe_w_down[i])
        x = x + gate_f * y
    return rms_norm_2(x, final_norm_g)


def setup_inputs(seed=0):
    out = dict(first_inputs(seed))
    for name, value in second_inputs(seed + 1).items():
        if name != "x":
            out[name + "_2"] = value
    return out


def reference(
    x, w_in, conv_xbc_w, conv_xbc_b, dt_bias_f, dt_bias_b, a_log_f, a_log_b, d_skip, ssd_norm_w,
    sc_conv_w, w_out, norm1_w, norm2_w, w_ffn_up, ffn_conv_w, ffn_conv_b, w_ffn_down,
    final_norm_w, c_2, ada_w_2, ada_b_2, mix_norm_g_2, ffn_norm_g_2, w_in_2, pool_w_2,
    pool_scale_2, conv_w_2, conv_b_2, conv_ln_g_2, conv_ln_b_2, sgu_ln_g_2, sgu_ln_b_2, sgu_w_2,
    sgu_b_2, w_out_2, ffn_w_gate_2, ffn_w_up_2, ffn_w_down_2, router_w_2, router_b_2,
    moe_w_gate_2, moe_w_up_2, moe_w_down_2, final_norm_g_2,
):
    x = first_block(
        x, w_in, conv_xbc_w, conv_xbc_b, dt_bias_f, dt_bias_b, a_log_f, a_log_b, d_skip,
        ssd_norm_w, sc_conv_w, w_out, norm1_w, norm2_w, w_ffn_up, ffn_conv_w, ffn_conv_b,
        w_ffn_down, final_norm_w,
    )
    return second_block(
        x, c_2, ada_w_2, ada_b_2, mix_norm_g_2, ffn_norm_g_2, w_in_2, pool_w_2, pool_scale_2,
        conv_w_2, conv_b_2, conv_ln_g_2, conv_ln_b_2, sgu_ln_g_2, sgu_ln_b_2, sgu_w_2, sgu_b_2,
        w_out_2, ffn_w_gate_2, ffn_w_up_2, ffn_w_down_2, router_w_2, router_b_2, moe_w_gate_2,
        moe_w_up_2, moe_w_down_2, final_norm_g_2,
    )


_drawn_inputs = setup_inputs


def setup_inputs(seed=0):
    import zlib

    import numpy as np

    out = dict(_drawn_inputs(seed))
    spreads = {}
    factors = {'ada_b_2': 8.0,
     'mix_norm_g_2': 8.0,
     'ffn_norm_g_2': 8.0,
     'pool_w_2': 4.392,
     'pool_scale_2': 8.0,
     'conv_w_2': 6.397,
     'conv_b_2': 64.0,
     'conv_ln_g_2': 51.566,
     'conv_ln_b_2': 64.0,
     'sgu_ln_g_2': 8.0,
     'sgu_ln_b_2': 8.0,
     'sgu_w_2': 2.691,
     'sgu_b_2': 8.0,
     'ffn_w_gate_2': 2.953,
     'ffn_w_up_2': 2.68,
     'ffn_w_down_2': 2.701,
     'router_w_2': 4.314,
     'router_b_2': 59.905,
     'moe_w_gate_2': 4.295,
     'moe_w_up_2': 3.96,
     'moe_w_down_2': 3.96}
    for name, (base, spread) in spreads.items():
        noise = np.random.default_rng([zlib.crc32(name.encode()), seed]).standard_normal(out[name].shape)
        drawn = base * np.exp(spread * noise) if base else spread * noise
        out[name] = __import__('jax').numpy.asarray(drawn.astype(out[name].dtype))
    for name, factor in factors.items():
        out[name] = (out[name] * factor).astype(out[name].dtype)
    return out
```

```python
from contextlib import ExitStack

import numpy as np

import concourse.bass as bass
from concourse import mybir

F32, F32R = mybir.dt.float32, mybir.dt.float32r
ACT, ALU = mybir.ActivationFunctionType, mybir.AluOpType
AX = mybir.AxisListType

P = 128
T = 256
D = 1024
KB = D // P
DEPTH = 2
HALF = T // 2
HEADS = 16
XBC = 16
NFF = 2816 // P
NEXP = 8
NFE = 3584 // P
NMOE = NEXP * NFE
TAPS = 31
CB = 3
UW = KB * P
SLOTS = 6
PAIRS = SLOTS // 2
LEAD = 4
ADA = DEPTH * 48
UNITS = DEPTH * (48 + 16 + 3 * NFF) + DEPTH * (14 + 8) + 3 * NFF + 3 * NMOE
EPS1, EPS2 = 1e-5, 1e-6

COLS = {}


def _columns():
    at = 0

    def add(name, width):
        nonlocal at
        COLS[name] = (at, width)
        at += width
    for l in range(DEPTH):
        for name, width in (("norm1", 8), ("norm2", 8), ("xw", 3 * XBC), ("xb", XBC), ("sw", 3 * 8),
                            ("gn", 8), ("skip", 8), ("fw", 3 * 2 * NFF), ("fb", 2 * NFF),
                            ("dtb", 32), ("alog", 32), ("wdt", KB * 32)):
            add(f"{name}{l}", width)
        for name, width in (("mixg", 8), ("ffng", 8), ("pscale", 2), ("cw", CB * TAPS), ("cb", CB),
                            ("clg", CB), ("clb", CB), ("slg", CB), ("slb", CB), ("adab", 48),
                            ("pw", 2 * P), ("sguw", 6 * P), ("sgub", CB * P)):
            add(f"{name}{l}", width)
    for name, width in (("final1", 8), ("final2", 8), ("cond", 8), ("rw", 64), ("rb", 8), ("ident", P),
                        ("ones", P), ("triu", P), ("tril", P), ("rcount", 2 * T), ("before", 64)):
        add(name, width)
    return at


NCOLS = _columns()


def build(nc, w_hbm, ada_hbm, x_hbm, par_hbm, out_hbm):
    with ExitStack() as ctx:
        def sb(name, shape, dt=F32):
            return ctx.enter_context(nc.sbuf_tensor(name, shape, dt))

        def sem(name):
            return ctx.enter_context(nc.semaphore(name))

        par = sb("par", [P, NCOLS])
        raw = sb("raw", [P, SLOTS, UW])
        whi = sb("whi", [P, SLOTS, UW], F32R)
        wlo = sb("wlo", [P, SLOTS, UW], F32R)
        h = sb("h", [P, KB, T])
        nhi = sb("nhi", [P, KB, T], F32R)
        nlo = sb("nlo", [P, KB, T], F32R)
        mhi = sb("mhi", [P, 2 * KB, T], F32R)
        mlo = sb("mlo", [P, 2 * KB, T], F32R)
        area = sb("area", [P, 24, T])
        work = sb("work", [P, 15, T])
        ring = sb("ring", [P, 7, T])
        mod = sb("mod", [P, ADA])
        modg = sb("modg", [P, 4, KB])
        cond = sb("cond", [P, KB])
        sml = sb("sml", [P, 12, 64])
        nF = sb("nF", [P, 2, 32])
        rowF = sb("rowF", [HEADS, 2, T])
        row1 = sb("row1", [P, T])
        rstd = sb("rstd", [P, T])
        bank = [ctx.enter_context(nc.psum_tensor(f"bank{b}", [P, 2, T], F32)) for b in range(8)]

        def cols(name):
            a, width = COLS[name]
            return par[:, a:a + width]

        def col(name, k=0, width=1):
            a = COLS[name][0] + k
            return par[:, a:a + width]

        def spreader(rows, k):
            a = COLS["ident"][0] + k
            return par[0:rows, a:a + 1].to_broadcast([rows, P])

        xs, Bt, Ct, nf = area[:, 0:8, :], area[:, 8:12, :], area[:, 12:16, :], area[:, 16:24, :]
        adaring = area[:, :, :].rearrange("p (s a) t -> p s (a t)", s=PAIRS)
        y1 = nf
        fg, fu, fs, fa = (area[:, 2 * a:2 * a + 2, :] for a in range(4))
        cw = area[:, 8:16, :]
        ahi, alo = mhi[:, 0:2, :], mlo[:, 0:2, :]
        dec = work[:, 0:6, :].rearrange("p (r a) (b c) -> p r (a b) c", r=2, b=2)
        prod = work[:, 6:12, :].rearrange("p (r a) (b c) -> p r (a b) c", r=2, b=2)
        s6 = work[:, 12:15, :].rearrange("p a (b c) -> p (a b) c", b=2)
        xtok = ring[:, 0:2, :].rearrange("p r (c x) -> p r c x", c=2)
        short_c, short_p, short_q, short_m = ring[:, 2, :], ring[:, 3, :], ring[:, 4, :], ring[:, 5:7, :]
        PADW = T + 32
        flat = area[:, 0:11, :].rearrange("p a t -> p (a t)")
        glu = flat[:, 0:CB * PADW].rearrange("p (b t) -> p b t", b=CB)
        pl = flat[:, CB * PADW:(CB + 6) * PADW].rearrange("p (b t) -> p b t", b=6)
        cv, pmix = area[:, 11:14, :], area[:, 14:16, :]
        vtok = work[:, 0:3, :].rearrange("p a t -> p (a t)").rearrange("p (c x) -> p c x", c=2)
        gated, sq3, sgate, nmean, vv = (work[:, 3:6, :], work[:, 6:9, :], work[:, 9:11, :],
                                        work[:, 11, :], work[:, 12:15, :])

        s = {}
        for name in """par_in x_in cond_ready ada_done mod_ready hi_ready lo_ready unit_done psum_free
                h_ready sq_ready ssq_ready var_ready root_ready n_ready nhi_ready nlo_ready fin_ready
                flin_ready silu_ready hid_ready ahi_ready alo_ready
                xlin_ready xbc_ready dt_ready dtv_ready dta_ready a_ready cum_ready cumv_ready
                score_ready s6_ready bc_ready clamp_ready xtp_ready xtok_ready dec_ready prod_ready y_ready y1_ready
                scq_ready mhi_ready mlo_ready zs_ready ysq_ready gssq_ready groot_ready gy_ready
                gate_ready conv_ready sum_ready cen_ready csq_ready cssq_ready croot_ready cn_ready
                cs_ready vn_ready vtp_ready vtok_ready smix_ready diff_ready pool_ready poolv_ready
                logit_ready rsub_ready rexp_ready comb_ready combt_ready combv_ready cwp_ready cw_ready
                out_stored""".split():
            s[name] = sem(name)
        loaded = [sem(f"loaded{k}") for k in range(PAIRS)]
        ada_in = [sem(f"ada_in{k}") for k in range(PAIRS)]
        block = ctx.enter_context(nc.Block())

        class At:

            def __init__(self, u, n, j, i=0, rolled=False):
                self.cu, self.cn, self.cj, self.i, self.rolled = u, n, j, i, rolled
                self.u, self.n, self.j = u + 6 * i, n + 4 * i, j + 2 * i
                self.slot, self.bank, self.par = u % SLOTS, bank[4 + n % 4], j % 2

            def ahead(self, k):
                return At(self.cu + k, self.cn, self.cj, self.i, self.rolled)

        class Chain:

            def __init__(self, eng, name):
                self.eng, self.sem, self.n, self.i, self.step = eng, sem(name), 0, 0, 0

            def mark(self, ins):
                ins.then_inc(self.sem, 1)
                self.n += 1

            def wait(self):
                self.eng.wait_ge(self.sem, self.n + self.step * self.i)

            def link(self, ins):
                self.mark(ins)
                self.wait()

        XBC_ORDER = [8, 9, 10, 11, 12, 13, 14, 15, 0, 1, 2, 3, 4, 5, 6, 7]
        MIX1_ORDER = [(k + 8) % 16 for k in range(16)]
        MIX2_ORDER = [5, 0, 6, 1, 7, 2, 3, 4]
        MIX2 = 16 * DEPTH

        def walk(eng, split, do, chain=None):
            u = n = j = m = 0

            def unit(kind, at, *args):
                if at.rolled or at.cu + LEAD < UNITS:
                    split(at.ahead(LEAD))
                do[kind](at, *args)

            def one(kind, *args):
                nonlocal u, n
                unit(kind, At(u, n, 0), *args)
                u, n = u + 1, n + (kind != "mixdown")

            def ffn(kind, count, l, links, spread=False, last=0):
                nonlocal u, n, j

                def pair(du, i, rolled):
                    for k in range(2):
                        a, b, c = u + 3 * k, n + 2 * k, j + k
                        unit(kind + "_gate", At(a, b, c, i, rolled), l)
                        unit(kind + "_up", At(a + 1, b + 1, c, i, rolled), l)
                        unit("down", At(a + 2, b + 2, c - 1, i, rolled), False, False)
                        do[kind + "_hid"](At(a + 2, b + 2, c, i, rolled), l)

                unit(kind + "_gate", At(u, n, j), l)
                if spread:
                    do["route_spread"]()
                unit(kind + "_up", At(u + 1, n + 1, j), l)
                do[kind + "_hid"](At(u + 2, n + 2, j), l)
                unit(kind + "_gate", At(u + 2, n + 2, j + 1), l)
                unit(kind + "_up", At(u + 3, n + 3, j + 1), l)
                unit("down", At(u + 4, n + 4, j), True, False)
                do[kind + "_hid"](At(u + 4, n + 4, j + 1), l)
                u, n, j = u + 5, n + 4, j + 2
                loops = (count - 2) // 2 - last
                with eng.Fori(0, loops) as i:
                    if chain is not None:
                        chain.i, chain.step, n0 = i, links, chain.n
                    pair(0, i, True)
                if chain is not None:
                    assert chain.n - n0 == links
                    chain.n, chain.i = n0 + links * loops, 0
                u, n, j = u + 6 * loops, n + 4 * loops, j + 2 * loops
                for _ in range(last):
                    pair(0, 0, False)
                    u, n, j = u + 6, n + 4, j + 2
                unit("down", At(u, n, j - 1), False, True)
                u += 1

            for v in range(LEAD):
                split(At(v, 0, 0))
            do["norm"](0, EPS1, "first")
            m = 1
            for l in range(DEPTH):
                for k, b in enumerate(XBC_ORDER):
                    one("xbc", l, k, b)
                    if k == 2:
                        do["dt"](l)
                do["xbc_last"](n, l)
                for t in range(KB):
                    one("sc_c", l, t)
                    do["ssd_scores"](l, t)
                    one("sc_v", l, t)
                    one("sc_b", l, t)
                    do["ssd_out"](l, t)
                for t in range(KB):
                    one("z", l, t)
                for k, b in enumerate(MIX1_ORDER):
                    one("mixdown", 16 * l + k, b, k == 0, k == 15)
                    if k == 0:
                        do["group_norm"](At(u, n, 0), l)
                        n += 2
                do["residual"](u, None)
                do["norm"](m, EPS1, "split")
                m += 1
                ffn("f", NFF, l, 4)
                do["residual"](u, None)
                if l < DEPTH - 1:
                    do["norm"](m, EPS1, "split")
                    m += 1
            do["norm"](m, EPS1, "plain")
            m += 1
            for l in range(DEPTH):
                do["norm"](m, EPS2, "shift")
                m += 1
                for b in range(CB):
                    one("sv", l, b)
                ln = At(u, n, 0)
                do["sums"](ln, 2 * l + 1, vv)
                n += 1
                one("cgate", l, 0)
                do["squares"](ln, 2 * l + 1, vv)
                do["sgu_norm"](l)
                one("cval", l, 0)
                do["sgu_turn"](l)
                one("cgate", l, 1)
                do["sgu_mix"](l)
                one("cval", l, 1)
                one("cgate", l, 2)
                one("cval", l, 2)
                for b in range(2):
                    one("pool", l, b)
                for b in range(CB):
                    one("su", l, b)
                for k, b in enumerate(MIX2_ORDER):
                    one("mixdown", MIX2 + 8 * l + k, b, k == 0, k == 7)
                    if k == 0:
                        ln = At(u, n, 0)
                        do["sums"](ln, 2 * l + 2, cv)
                        n += 1
                    if k == 1:
                        do["squares"](ln, 2 * l + 2, cv)
                        do["conv_norm"](l)
                do["residual"](u, 48 * l + 16)
                do["norm"](m, EPS2, "shift")
                m += 1
                if l == DEPTH - 1:
                    do["route"]()
                    ffn("e", NMOE, l, 0, spread=True, last=1)
                else:
                    ffn("d", NFF, l, 0)
                do["residual"](u, 48 * l + 40)
            do["norm"](m, EPS2, "last")
            assert u == UNITS, u

        SPLIT_BEFORE = [0, 1, 2, 3, 4, 4, 5, 6, 7, 8]

        def gain(m, k):
            if m < 5:
                return col(("norm10", "norm20", "norm11", "norm21", "final1")[m], k)
            return col("final2", k) if m == 9 else modg[:, m - 5, k:k + 1]

        def shift(m, k):
            a = 48 * ((m - 5) // 2) + 24 * ((m - 5) % 2) + k
            return mod[:, a:a + 1]

        def nothing(*args):
            pass

        @block.sync
        def _(sp):
            def load(k, src):
                sp.dma_start(raw[:, 2 * k:2 * k + 2, :].rearrange("p a t -> p (a t)"), src).then_inc(loaded[k], 16)

            for k in range(PAIRS):
                load(k, w_hbm[k])
                sp.dma_start(adaring[:, k, :], ada_hbm[k]).then_inc(ada_in[k], 16)
            with sp.Fori(0, ADA // SLOTS - 1) as i:
                for k in range(PAIRS):
                    src = ada_hbm[PAIRS * i + (PAIRS + k)]
                    used = sp.snap(SLOTS * i + (2 * k + 2))
                    sp.wait_ge(s["ada_done"], used)
                    sp.dma_start(adaring[:, k, :], src).then_inc(ada_in[k], 16)
            pairs = UNITS // 2
            turns = (pairs - PAIRS) // PAIRS
            with sp.Fori(0, turns) as i:
                for k in range(PAIRS):
                    src = w_hbm[PAIRS * i + (PAIRS + k)]
                    used = sp.snap(SLOTS * i + (2 * k + 2))
                    sp.wait_ge(s["lo_ready"], used)
                    load(k, src)
            for p in range(PAIRS * (turns + 1), pairs):
                sp.wait_ge(s["lo_ready"], 2 * (p - PAIRS) + 2)
                load(p % PAIRS, w_hbm[p])
            sp.wait_ge(s["fin_ready"], KB)
            sp.dma_start(out_hbm, nf.rearrange("p k t -> p (k t)")).then_inc(s["out_stored"], 16)
            sp.wait_ge(s["out_stored"], 16)

        @block.tensor
        def _(pe):
            mm = nc.tensor.matmul
            fresh = [0]

            def three(out, slot, tile, xh, xl, start, stop):
                w = slice(tile * P, tile * P + P)
                mm(out, whi[:, slot, w], xh, start=start, stop=False, skip_group_check=True)
                mm(out, wlo[:, slot, w], xh, start=False, stop=False, skip_group_check=True)
                return mm(out, whi[:, slot, w], xl, start=False, stop=stop, skip_group_check=True)

            def up(at, *args):
                pe.wait_ge(s["lo_ready"], at.u + 1)
                if at.cn >= 4:
                    pe.wait_ge(s["psum_free"], at.n - 3)
                for k in range(KB):
                    if fresh[0]:
                        pe.wait_ge(s["nlo_ready"], KB * (fresh[0] - 1) + k + 1)
                    last = three(at.bank[:, 0, :], at.slot, k, nhi[:, k, :], nlo[:, k, :],
                                 k == 0, k == KB - 1)
                fresh[0] = 0
                last.then_inc(s["unit_done"], 1)

            def down_tiles(at, xh, xl, first, final):
                for o in range(KB):
                    last = three(bank[o // 2][:, o % 2, :], at.slot, o, xh, xl, first and o % 2 == 0, final)
                last.then_inc(s["unit_done"], 1)

            def mixdown(at, order, b, first, final):
                pe.wait_ge(s["lo_ready"], at.u + 1)
                pe.wait_ge(s["mlo_ready"], order + (4 if first and order >= MIX2 else 1))
                down_tiles(at, mhi[:, b, :], mlo[:, b, :], first, final)

            def down(at, first, final):
                pe.wait_ge(s["lo_ready"], at.u + 1)
                pe.wait_ge(s["alo_ready"], at.j + 1)
                if first and at.cj == 3 * NFF:
                    pe.wait_ge(s["cw_ready"], 4)
                down_tiles(at, ahi[:, at.par, :], alo[:, at.par, :], first, final)

            def norm(m, eps, how):
                for k in range(KB):
                    if k % 2 == 0:
                        pe.wait_ge(s["sq_ready"], 4 * m + k // 2 + 1)
                    last = mm(bank[0][:, 0, :], cols("ones"), nf[:, k, :], start=k == 0, stop=k == KB - 1)
                last.then_inc(s["ssq_ready"], 1)
                if how in ("first", "split", "shift"):
                    fresh[0] = SPLIT_BEFORE[m] + 1

            def dt(l):
                for c in range(2):
                    for k in range(KB):
                        last = mm(bank[0][:, 0, 32 * c:32 * c + 32], nf[:, k, HALF * c:HALF * c + HALF],
                                  col(f"wdt{l}", 32 * k, 32), start=k == 0, stop=k == KB - 1)
                last.then_inc(s["dt_ready"], 1)
                pe.wait_ge(s["a_ready"], l + 1)
                a = sml[:, 0, :].rearrange("p (c h) -> p c h", c=2)
                triu, ones, tril = col("triu", 0, P), cols("ones"), cols("tril")
                o = bank[1][:, 0, 0:64].rearrange("p (c h) -> p c h", c=2)
                mm(o[:, 0, 0:16], triu, a[:, 0, 0:16], start=True, stop=True)
                mm(o[:, 0, 16:32], ones, a[:, 1, 16:32], start=True, stop=False)
                mm(o[:, 0, 16:32], tril, a[:, 0, 16:32], start=False, stop=True)
                mm(o[:, 1, 0:16], ones, a[:, 0, 0:16], start=True, stop=False)
                mm(o[:, 1, 0:16], triu, a[:, 1, 0:16], start=False, stop=True)
                mm(o[:, 1, 16:32], tril, a[:, 1, 16:32], start=True, stop=True)
                f, b = bank[2][0:16, 0, :], bank[3][0:16, 0, :]
                mm(f[:, 0:HALF], a[:, 0, 0:16], triu, start=True, stop=True)
                mm(f[:, HALF:T], a[:, 0, 0:16], ones, start=True, stop=False)
                mm(f[:, HALF:T], a[:, 1, 0:16], triu, start=False, stop=True)
                mm(b[:, 0:HALF], a[:, 1, 16:32], ones, start=True, stop=False)
                mm(b[:, 0:HALF], a[:, 0, 16:32], tril, start=False, stop=True)
                mm(b[:, HALF:T], a[:, 1, 16:32], tril, start=True, stop=True).then_inc(s["cum_ready"], 1)

            def ssd_scores(l, j):
                g, it = j // 2, 8 * l + j
                if j == 0:
                    pe.wait_ge(s["xbc_ready"], 16 * (l + 1))
                    pe.wait_ge(s["cumv_ready"], 3 * (l + 1))
                if j % 2 == 0:
                    if it:
                        pe.wait_ge(s["s6_ready"], 4 * l + g)
                    for c in range(2):
                        last = mm(bank[2][:, c, :], Bt[:, g, HALF * c:HALF * c + HALF], Ct[:, g, :],
                                  start=True, stop=True)
                    last.then_inc(s["score_ready"], 1)
                for r in range(2):
                    if it:
                        pe.wait_ge(s["clamp_ready"], 2 * it + r - 1)
                    for d in range(2):
                        last = mm(bank[r][:, d, :], spreader(16, 2 * j + r), rowF[:, d, :], start=True, stop=True)
                    last.then_inc(s["bc_ready"], 1)
                if it:
                    pe.wait_ge(s["xtok_ready"], it)
                    pe.wait_ge(s["y1_ready"], it)
                for c in range(2):
                    last = nc.tensor.transpose(bank[3][:, 1, HALF * c:HALF * c + HALF],
                                               xs[:, j, HALF * c:HALF * c + HALF], cols("ident"))
                last.then_inc(s["xtp_ready"], 1)

            def ssd_out(l, j):
                it = 8 * l + j
                pe.wait_ge(s["xtok_ready"], it + 1)
                for r in range(2):
                    pe.wait_ge(s["prod_ready"], 2 * it + r + 1)
                    for c in range(2):
                        last = mm(bank[3][64 * r:64 * r + 64, 0, :], xtok[:, it % 2, c, 64 * r:64 * r + 64],
                                  prod[:, r, 2 * c:2 * c + 2, :].rearrange("p a b -> p (a b)"),
                                  start=c == 0, stop=c == 1)
                last.then_inc(s["y_ready"], 1)

            def group_norm(at, l):
                for g in range(4):
                    if g % 2 == 0:
                        pe.wait_ge(s["psum_free"], at.n - 3 + g // 2)
                    pe.wait_ge(s["ysq_ready"], 8 * l + 2 * g + 2)
                    b = bank[4 + (at.cn + g // 2) % 4]
                    for k in range(2):
                        last = mm(b[:, g % 2, :], cols("ones"), xs[:, 2 * g + k, :], start=k == 0, stop=k == 1)
                    last.then_inc(s["gssq_ready"], 1)

            def sums(at, count, src):
                pe.wait_ge(s["psum_free"], at.n - 3)
                if count % 2:
                    pe.wait_ge(s["psum_free"], at.n)
                else:
                    pe.wait_ge(s["conv_ready"], count // 2)
                for b in range(CB):
                    last = mm(at.bank[:, 0, :], cols("ones"), src[:, b, :], start=b == 0, stop=b == CB - 1)
                last.then_inc(s["sum_ready"], 1)

            def squares(at, count, src):
                pe.wait_ge(s["csq_ready"], count)
                for b in range(CB):
                    last = mm(at.bank[:, 1, :], cols("ones"), sq3[:, b, :], start=b == 0, stop=b == CB - 1)
                last.then_inc(s["cssq_ready"], 1)

            def sgu_turn(l):
                pe.wait_ge(s["vn_ready"], l + 1)
                for c in range(2):
                    out = bank[1 + c][:, :, :].rearrange("p a t -> p (a t)")
                    for b in range(CB):
                        last = nc.tensor.transpose(out[:, P * b:P * b + P], vv[:, b, HALF * c:HALF * c + HALF],
                                                   cols("ident"))
                    last.then_inc(s["vtp_ready"], 1)

            def sgu_mix(l):
                pe.wait_ge(s["vtok_ready"], 2 * (l + 1))
                for b in range(CB):
                    o = (bank[1][:, 0, :], bank[1][:, 1, :], bank[2][:, 0, :])[b]
                    for r in range(2):
                        hd = 2 * b + r
                        for c in range(2):
                            last = mm(o[64 * r:64 * r + 64, HALF * c:HALF * c + HALF],
                                      vtok[:, c, 64 * hd:64 * hd + 64], col(f"sguw{l}", P * hd, P),
                                      start=True, stop=True)
                last.then_inc(s["smix_ready"], 1)

            def su(at, l, b):
                up(at)
                if b < 2:
                    pe.wait_ge(s["diff_ready"], 2 * l + b + 1)
                    mm(bank[(3, 0)[b]][:, 0, :], col(f"pw{l}", P * b, P), pl[:, 4 + b, 16:16 + T],
                       start=True, stop=True).then_inc(s["pool_ready"], 1)

            def route():
                pe.wait_ge(s["nlo_ready"], KB * fresh[0])
                for c in range(2):
                    for k in range(KB):
                        last = mm(bank[0][:, 0, 8 * c:8 * c + 8], nf[:, k, HALF * c:HALF * c + HALF],
                                  col("rw", 8 * k, 8), start=k == 0, stop=k == KB - 1)
                last.then_inc(s["logit_ready"], 1)

            def route_spread():
                pe.wait_ge(s["comb_ready"], 1)
                for c in range(2):
                    last = nc.tensor.transpose(bank[1][0:8, 0, HALF * c:HALF * c + HALF],
                                               sml[:, 6, 8 * c:8 * c + 8], cols("ident"))
                last.then_inc(s["combt_ready"], 1)
                pe.wait_ge(s["combv_ready"], 1)
                for e in range(NEXP):
                    last = mm(bank[e // 2][:, e % 2, :], spreader(8, e), rowF[0:8, 0, :], start=True, stop=True)
                    if e % 2:
                        last.then_inc(s["cwp_ready"], 1)

            pe.wait_ge(s["cond_ready"], 1)
            with pe.Fori(0, ADA // SLOTS) as i:
                for k in range(PAIRS):
                    pe.wait_ge(ada_in[k], 16 * i + 16)
                    for e in range(2):
                        for t in range(KB):
                            last = mm(bank[7][:, 0, bass.ds(SLOTS * i + (2 * k + e), 1)],
                                      adaring[:, k, e * UW + t * P:e * UW + t * P + P],
                                      cond[:, t:t + 1], start=t == 0, stop=t == KB - 1)
                        last.then_inc(s["ada_done"], 1)
            walk(pe, nothing, {
                "norm": norm, "xbc": up, "dt": dt, "xbc_last": nothing, "sc_c": up, "sc_v": up, "sc_b": up,
                "z": up, "ssd_scores": ssd_scores, "ssd_out": ssd_out, "mixdown": mixdown,
                "group_norm": group_norm, "residual": nothing, "f_gate": up, "f_up": up, "f_hid": nothing,
                "d_gate": up, "d_up": up, "d_hid": nothing, "e_gate": up, "e_up": up, "e_hid": nothing,
                "down": down, "sv": up, "cgate": up, "cval": up, "sums": sums, "squares": squares,
                "sgu_norm": nothing, "sgu_turn": sgu_turn, "sgu_mix": sgu_mix, "pool": up, "su": su,
                "conv_norm": nothing, "route": route, "route_spread": route_spread})

        @block.scalar
        def _(act):
            A, copy = nc.scalar.activation, nc.scalar.copy

            act.dma_start(par[:, :], par_hbm).then_inc(s["par_in"], 16)
            act.dma_start(h[:, :, :].rearrange("p k t -> p (k t)"), x_hbm).then_inc(s["x_in"], 16)
            act.wait_ge(s["par_in"], 16)
            A(cond[:, :], cols("cond"), ACT.Silu).then_inc(s["cond_ready"], 1)

            def split(at):
                act.wait_ge(loaded[at.slot // 2], 16 * (at.cu // SLOTS) + 16 + 16 * at.i)
                if at.cu >= SLOTS:
                    act.wait_ge(s["unit_done"], at.u - (SLOTS - 1))
                copy(whi[:, at.slot, :], raw[:, at.slot, :]).then_inc(s["hi_ready"], 1)

            def norm(m, eps, how):
                for q in range(4):
                    if m == 0:
                        act.wait_ge(s["x_in"], 16)
                        act.wait_ge(s["mod_ready"], 1)
                    else:
                        act.wait_ge(s["h_ready"], 4 * (m - 1) + q + 1)
                    A(nf[:, 2 * q:2 * q + 2, :], h[:, 2 * q:2 * q + 2, :], ACT.Square).then_inc(s["sq_ready"], 1)
                act.wait_ge(s["var_ready"], m + 1)
                A(row1[:, :], row1[:, :], ACT.Sqrt).then_inc(s["root_ready"], 1)
                if how in ("first", "split", "shift"):
                    for k in range(KB):
                        act.wait_ge(s["n_ready"], KB * SPLIT_BEFORE[m] + k + 1)
                        copy(nhi[:, k, :], nf[:, k, :]).then_inc(s["nhi_ready"], 1)

            def xbc(at, l, k, b):
                act.wait_ge(s["unit_done"], at.u + 1)
                if k >= 2:
                    act.wait_ge(s["xbc_ready"], 16 * l + k - 1)
                A(ring[:, k % 2, :], at.bank[:, 0, :], ACT.Identity, bias=col(f"xb{l}", b),
                  scale=col(f"xw{l}", 3 * b + 1)).then_inc(s["xlin_ready"], 1)
                if k:
                    xbc_silu(at.n, k - 1)

            def xbc_silu(done, k):
                act.wait_ge(s["psum_free"], done)
                A(area[:, XBC_ORDER[k], :], ring[:, k % 2, :], ACT.Silu).then_inc(s["xbc_ready"], 1)

            def xbc_last(n, l):
                xbc_silu(n, XBC - 1)

            def dt(l):
                act.wait_ge(s["dtv_ready"], 2 * l + 1)
                A(sml[:, 3, :], sml[:, 2, :], ACT.Exp).then_inc(s["dta_ready"], 1)
                A(sml[:, 7, 0:32], cols(f"alog{l}"), ACT.Exp).then_inc(s["dta_ready"], 1)
                act.wait_ge(s["dtv_ready"], 2 * l + 2)
                A(sml[:, 5, :], sml[:, 4, :], ACT.Ln).then_inc(s["dta_ready"], 1)

            def ssd_scores(l, j):
                it = 8 * l + j
                act.wait_ge(s["xtp_ready"], it + 1)
                copy(xtok[:, it % 2, :, :].rearrange("p c x -> p (c x)"),
                     bank[3][:, 1, :]).then_inc(s["xtok_ready"], 1)
                for r in range(2):
                    act.wait_ge(s["clamp_ready"], 2 * it + r + 1)
                    A(dec[:, r, :, :], dec[:, r, :, :], ACT.Exp).then_inc(s["dec_ready"], 1)

            def sc_v(at, l, j):
                act.wait_ge(s["psum_free"], at.n + 1)
                A(short_q, short_p, ACT.Copy, scale=col(f"sw{l}", 3 * j + 1)).then_inc(s["scq_ready"], 1)

            def sc_b(at, l, j):
                act.wait_ge(s["psum_free"], at.n + 1)
                copy(mhi[:, 8 + j, :], short_m[:, j % 2, :]).then_inc(s["mhi_ready"], 1)

            def z(at, l, j):
                act.wait_ge(s["unit_done"], at.u + 1)
                A(ring[:, j % 2, :], at.bank[:, 0, :], ACT.Silu).then_inc(s["zs_ready"], 1)
                act.wait_ge(s["psum_free"], at.n + 1)
                A(xs[:, j, :], y1[:, j, :], ACT.Square).then_inc(s["ysq_ready"], 1)

            def group_norm(at, l):
                for q in range(2):
                    act.wait_ge(s["psum_free"], at.n + q + 1)
                    A(work[:, 2 * q:2 * q + 2, :], work[:, 2 * q:2 * q + 2, :],
                      ACT.Sqrt).then_inc(s["groot_ready"], 1)
                for k in range(KB):
                    act.wait_ge(s["gy_ready"], 8 * l + k + 1)
                    copy(mhi[:, k, :], y1[:, k, :]).then_inc(s["mhi_ready"], 1)

            def f_lin(at, l, dst, b):
                act.wait_ge(s["unit_done"], at.u + 1)
                A(dst[:, at.par, :], at.bank[:, 0, :], ACT.Identity,
                  bias=par[:, bass.ds(b + COLS[f"fb{l}"][0], 1)],
                  scale=par[:, bass.ds(3 * b + (COLS[f"fw{l}"][0] + 1), 1)]).then_inc(s["flin_ready"], 1)

            def f_gate(at, l):
                f_lin(at, l, fg, at.j - NFF * l)

            def f_up(at, l):
                f_lin(at, l, fu, at.j + (NFF - NFF * l))
                act.wait_ge(s["psum_free"], at.n)
                A(fs[:, at.par, :], fg[:, at.par, :], ACT.Silu).then_inc(s["silu_ready"], 1)

            def f_hid(at, l):
                act.wait_ge(s["hid_ready"], at.j + 1)
                copy(ahi[:, at.par, :], fa[:, at.par, :]).then_inc(s["ahi_ready"], 1)

            def d_gate(at, l):
                act.wait_ge(s["unit_done"], at.u + 1)
                A(fs[:, at.par, :], at.bank[:, 0, :], ACT.Silu).then_inc(s["silu_ready"], 1)

            def d_hid(at, l):
                act.wait_ge(s["psum_free"], at.n)
                copy(ahi[:, at.par, :], fa[:, at.par, :]).then_inc(s["ahi_ready"], 1)

            def e_hid(at, l):
                act.wait_ge(s["hid_ready"], at.j - (NFF - 1))
                copy(ahi[:, at.par, :], fa[:, at.par, :]).then_inc(s["ahi_ready"], 1)

            def squares(at, count, src):
                for b in range(CB):
                    act.wait_ge(s["cen_ready"], CB * (count - 1) + b + 1)
                    last = A(sq3[:, b, :], src[:, b, :], ACT.Square)
                last.then_inc(s["csq_ready"], 1)
                act.wait_ge(s["psum_free"], at.n + 1)
                A(row1[:, :], row1[:, :], ACT.Sqrt).then_inc(s["croot_ready"], 1)

            def sgu_turn(l):
                for c in range(2):
                    act.wait_ge(s["vtp_ready"], 2 * l + c + 1)
                    copy(vtok[:, c, :], bank[1 + c][:, :, :].rearrange("p a t -> p (a t)")[:, 0:CB * P]
                         ).then_inc(s["vtok_ready"], 1)

            def cgate(at, l, b):
                act.wait_ge(s["unit_done"], at.u + 1)
                if b == 2:
                    act.wait_ge(s["psum_free"], at.n - 2)
                A(sgate[:, b % 2, :], at.bank[:, 0, :], ACT.Sigmoid).then_inc(s["gate_ready"], 1)

            def su(at, l, b):
                act.wait_ge(s["psum_free"], at.n + 1)
                copy(mhi[:, 5 + b, :], gated[:, b, :]).then_inc(s["mhi_ready"], 1)
                if b < 2:
                    act.wait_ge(s["poolv_ready"], 2 * l + b + 1)
                    copy(mhi[:, b, :], pmix[:, b, :]).then_inc(s["mhi_ready"], 1)

            def conv_norm(l):
                for b in range(CB):
                    act.wait_ge(s["cn_ready"], CB * l + b + 1)
                    A(cv[:, b, :], cv[:, b, :], ACT.Silu, bias=col(f"clb{l}", b)).then_inc(s["cs_ready"], 1)
                for b in range(CB):
                    act.wait_ge(s["cs_ready"], CB * l + b + 1)
                    copy(mhi[:, 2 + b, :], cv[:, b, :]).then_inc(s["mhi_ready"], 1)

            def route():
                act.wait_ge(s["rsub_ready"], 2)
                A(sml[:, 3, 0:16], sml[:, 2, 0:16], ACT.Exp).then_inc(s["rexp_ready"], 1)

            def route_spread():
                for q in range(4):
                    act.wait_ge(s["cwp_ready"], q + 1)
                    copy(cw[:, 2 * q:2 * q + 2, :], bank[q][:, :, :]).then_inc(s["cw_ready"], 1)

            walk(act, split, {
                "norm": norm, "xbc": xbc, "dt": dt, "xbc_last": xbc_last, "sc_c": nothing, "sc_v": sc_v,
                "sc_b": sc_b, "z": z, "ssd_scores": ssd_scores, "ssd_out": nothing, "mixdown": nothing,
                "group_norm": group_norm, "residual": nothing, "f_gate": f_gate, "f_up": f_up, "f_hid": f_hid,
                "d_gate": d_gate, "d_up": nothing, "d_hid": d_hid, "e_gate": d_gate, "e_up": nothing,
                "e_hid": e_hid, "down": nothing, "sv": nothing, "cgate": cgate, "cval": nothing,
                "sums": nothing, "squares": squares, "sgu_norm": nothing, "sgu_turn": sgu_turn,
                "sgu_mix": nothing, "pool": nothing, "su": su, "conv_norm": conv_norm, "route": route,
                "route_spread": route_spread})

        @block.vector
        def _(dve):
            TT, TS, STT, copy = (nc.vector.tensor_tensor, nc.vector.tensor_scalar,
                                 nc.vector.scalar_tensor_tensor, nc.vector.tensor_copy)
            MUL, ADD, SUB = ALU.mult, ALU.add, ALU.subtract
            ch = Chain(dve, "vchain")

            def split(at):
                dve.wait_ge(s["hi_ready"], at.u + 1)
                TT(wlo[:, at.slot, :], raw[:, at.slot, :], whi[:, at.slot, :].bitcast(F32),
                   SUB).then_inc(s["lo_ready"], 1)

            def rest(dst, src, hi, ready, count, done):
                dve.wait_ge(s[ready], count)
                TT(dst, src, hi.bitcast(F32), SUB).then_inc(s[done], 1)

            def mix_rest(order, b, src):
                rest(mlo[:, b, :], src, mhi[:, b, :], "mhi_ready", order + 1, "mlo_ready")

            def taps(dst, src, w):
                ch.link(STT(dst[:, 1:T], src[:, 0:T - 1], w(0), dst[:, 1:T], MUL, ADD))
                return STT(dst[:, 0:T - 1], src[:, 1:T], w(2), dst[:, 0:T - 1], MUL, ADD)

            def norm(m, eps, how):
                dve.wait_ge(s["ssq_ready"], m + 1)
                TS(row1[:, :], bank[0][:, 0, :], 1.0 / D, eps, MUL, ADD).then_inc(s["var_ready"], 1)
                dve.wait_ge(s["root_ready"], m + 1)
                ch.link(nc.vector.reciprocal(rstd[:, :], row1[:, :]))
                for k in range(KB):
                    dst = h if how == "plain" else nf
                    ins = STT(dst[:, k, :], h[:, k, :], gain(m, k), rstd[:, :], MUL, MUL)
                    if how == "plain":
                        if k % 2:
                            ins.then_inc(s["h_ready"], 1)
                    elif how == "last":
                        ins.then_inc(s["fin_ready"], 1)
                    else:
                        if how == "shift":
                            ch.link(ins)
                            ins = TS(nf[:, k, :], nf[:, k, :], shift(m, k), None, ADD)
                        ins.then_inc(s["n_ready"], 1)
                        if k:
                            norm_rest(m, k - 1)
                if how in ("first", "split", "shift"):
                    norm_rest(m, KB - 1)

            def norm_rest(m, k):
                rest(nlo[:, k, :], nf[:, k, :], nhi[:, k, :], "nhi_ready", KB * SPLIT_BEFORE[m] + k + 1, "nlo_ready")

            def xbc(at, l, k, b):
                dve.wait_ge(s["xlin_ready"], 16 * l + k + 1)
                taps(ring[:, k % 2, :], at.bank[:, 0, :],
                     lambda t: col(f"xw{l}", 3 * b + t)).then_inc(s["psum_free"], 1)

            def dt(l):
                a, x, nx, e, u, lnu, ea, t, r, d = (sml[:, k, :] for k in (0, 1, 2, 3, 4, 5, 7, 8, 9, 10))
                dve.wait_ge(s["dt_ready"], l + 1)
                for c in range(2):
                    w = slice(32 * c, 32 * c + 32)
                    ins = TT(x[:, w], bank[0][:, 0, w], cols(f"dtb{l}"), ADD)
                ch.link(ins)
                STT(nx, x, -1.0, x, MUL, ALU.min).then_inc(s["dtv_ready"], 1)
                dve.wait_ge(s["dta_ready"], 3 * l + 1)
                TS(u, e, 1.0, None, ADD).then_inc(s["dtv_ready"], 1)
                dve.wait_ge(s["dtv_ready"], 2 * l + 2)
                ch.link(TS(t, u, -1.0, 1.0, MUL, ADD))
                TT(t, t, e, ADD)
                ch.link(nc.vector.reciprocal(r, u))
                ch.link(TT(t, t, r, MUL))
                dve.wait_ge(s["dta_ready"], 3 * l + 3)
                ch.link(STT(d, x, 0.0, lnu, ALU.max, ADD))
                ch.link(TT(d, d, t, ADD))
                for c in range(2):
                    w = slice(32 * c, 32 * c + 32)
                    ins = STT(a[:, w], d[:, w], -1.0, ea[:, 0:32], MUL, MUL)
                ins.then_inc(s["a_ready"], 1)
                dve.wait_ge(s["cum_ready"], l + 1)
                TS(nF[:, :, :].rearrange("p c h -> p (c h)"), bank[1][:, 0, 0:64], -1.0, None,
                   MUL).then_inc(s["cumv_ready"], 1)
                copy(rowF[:, 0, :], bank[2][0:16, 0, :]).then_inc(s["cumv_ready"], 1)
                copy(rowF[:, 1, :], bank[3][0:16, 0, :]).then_inc(s["cumv_ready"], 1)

            def ssd_scores(l, j):
                g, it = j // 2, 8 * l + j
                triu, tril = col("triu", 0, P), cols("tril")
                if j % 2 == 0:
                    sc = bank[2][:, :, :].rearrange("p c (b t) -> p (c b) t", b=2)
                    dve.wait_ge(s["score_ready"], 4 * l + g + 1)
                    TT(s6[:, 0, :], sc[:, 0, :], triu, MUL)
                    copy(s6[:, 1:3, :], sc[:, 1:3, :])
                    TT(s6[:, 3, :], sc[:, 3, :], tril, MUL)
                    TT(s6[:, 4, :], sc[:, 0, :], tril, MUL)
                    TT(s6[:, 5, :], sc[:, 3, :], triu, MUL).then_inc(s["s6_ready"], 1)
                    dve.wait_ge(s["s6_ready"], 4 * l + g + 1)
                parts = ((0, 2, 0, 0, 0), (2, 4, 1, 1, 0), (4, 5, 0, 1, 0), (5, 6, 1, 0, HALF))
                dts = sml[:, 10, :].rearrange("p (c h) -> p c h", c=2)
                for r in range(2):
                    hd = 2 * j + r
                    dve.wait_ge(s["bc_ready"], 2 * it + r + 1)
                    if it:
                        dve.wait_ge(s["prod_ready"], 2 * it + r - 1)
                    for a, b, c, d, t in parts:
                        ins = TS(dec[:, r, a:b, :].rearrange("p a b -> p (a b)"),
                                 bank[r][:, d, t:t + HALF * (b - a)], nF[:, c, 16 * d + hd:16 * d + hd + 1],
                                 0.0, ADD, ALU.min)
                    ins.then_inc(s["clamp_ready"], 1)
                for r in range(2):
                    hd = 2 * j + r
                    dve.wait_ge(s["dec_ready"], 2 * it + r + 1)
                    for a, b, c, d, t in parts:
                        ins = STT(prod[:, r, a:b, :], dec[:, r, a:b, :], dts[:, c, 16 * d + hd:16 * d + hd + 1],
                                  s6[:, a:b, :], MUL, MUL)
                    ch.link(ins)
                    TT(prod[:, r, 0:4:3, :], prod[:, r, 0:4:3, :], prod[:, r, 4:6, :], ADD).then_inc(s["prod_ready"], 1)

            def ssd_out(l, j):
                it = 8 * l + j
                mix_rest(16 * l + j, 8 + j, short_m[:, j % 2, :])
                dve.wait_ge(s["y_ready"], it + 1)
                STT(y1[:, j, :], xs[:, j, :], col(f"skip{l}", j), bank[3][:, 0, :], MUL, ADD).then_inc(s["y1_ready"], 1)

            def sc_c(at, l, j):
                dve.wait_ge(s["unit_done"], at.u + 1)
                copy(short_c, at.bank[:, 0, :]).then_inc(s["psum_free"], 1)

            def sc_v(at, l, j):
                dve.wait_ge(s["unit_done"], at.u + 1)
                dve.wait_ge(s["psum_free"], at.n)
                TT(short_p, short_c, at.bank[:, 0, :], MUL).then_inc(s["psum_free"], 1)

            def sc_b(at, l, j):
                dve.wait_ge(s["scq_ready"], 8 * l + j + 1)
                ch.link(taps(short_q, short_p, lambda t: col(f"sw{l}", 3 * j + t)))
                dve.wait_ge(s["unit_done"], at.u + 1)
                TT(short_m[:, j % 2, :], short_q, at.bank[:, 0, :], MUL).then_inc(s["psum_free"], 1)

            def z(at, l, j):
                dve.wait_ge(s["zs_ready"], 8 * l + j + 1)
                if j == 0:
                    dve.wait_ge(s["y1_ready"], 8 * l + 8)
                TT(y1[:, j, :], y1[:, j, :], ring[:, j % 2, :], MUL).then_inc(s["psum_free"], 1)

            def group_norm(at, l):
                for q in range(2):
                    dve.wait_ge(s["gssq_ready"], 4 * l + 2 * q + 2)
                    TS(work[:, 2 * q:2 * q + 2, :], bank[4 + (at.cn + q) % 4][:, :, :], 4.0 / D, EPS1,
                       MUL, ADD).then_inc(s["psum_free"], 1)
                for q in range(2):
                    dve.wait_ge(s["groot_ready"], 2 * l + q + 1)
                    ins = nc.vector.reciprocal(work[:, 2 * q:2 * q + 2, :], work[:, 2 * q:2 * q + 2, :])
                ch.link(ins)
                for k in range(KB):
                    STT(y1[:, k, :], y1[:, k, :], col(f"gn{l}", k), work[:, k // 2, :],
                        MUL, MUL).then_inc(s["gy_ready"], 1)
                    if k:
                        mix_rest(16 * l + 7 + k, k - 1, y1[:, k - 1, :])
                mix_rest(16 * l + 15, KB - 1, y1[:, KB - 1, :])

            def residual(u, gate):
                dve.wait_ge(s["unit_done"], u)
                for k in range(KB):
                    if gate is None and k % 2:
                        TT(h[:, k - 1:k + 1, :], bank[k // 2][:, :, :], h[:, k - 1:k + 1, :],
                           ADD).then_inc(s["h_ready"], 1)
                    elif gate is not None:
                        ins = STT(h[:, k, :], bank[k // 2][:, k % 2, :], mod[:, gate + k:gate + k + 1],
                                  h[:, k, :], MUL, ADD)
                        if k % 2:
                            ins.then_inc(s["h_ready"], 1)

            def f_taps(at, l, dst, b):
                taps(dst[:, at.par, :], at.bank[:, 0, :],
                     lambda t: par[:, bass.ds(3 * b + (COLS[f"fw{l}"][0] + t), 1)]).then_inc(s["psum_free"], 1)

            def f_gate(at, l):
                dve.wait_ge(s["flin_ready"], 2 * at.j + 1)
                f_taps(at, l, fg, at.j - NFF * l)

            def f_up(at, l):
                dve.wait_ge(s["flin_ready"], 2 * at.j + 2)
                f_taps(at, l, fu, at.j + (NFF - NFF * l))
                dve.wait_ge(s["silu_ready"], at.j + 1)
                dve.wait_ge(s["psum_free"], at.n + 1)
                TT(fa[:, at.par, :], fs[:, at.par, :], fu[:, at.par, :], MUL).then_inc(s["hid_ready"], 1)

            def hid(at, l):
                rest(alo[:, at.par, :], fa[:, at.par, :], ahi[:, at.par, :], "ahi_ready", at.j + 1, "alo_ready")

            def d_up(at, l):
                dve.wait_ge(s["silu_ready"], at.j + 1)
                dve.wait_ge(s["unit_done"], at.u + 1)
                TT(fa[:, at.par, :], fs[:, at.par, :], at.bank[:, 0, :], MUL).then_inc(s["psum_free"], 2)

            def e_up(at, l):
                d_up(at, l)
                if at.cj == 3 * NFF:
                    dve.wait_ge(s["cw_ready"], 4)
                dve.wait_ge(s["psum_free"], at.n + 1)
                e = (at.j - 3 * NFF) // NFE
                weight = cw[:, e, :] if isinstance(e, int) else cw[:, bass.ds(e, 1), :].rearrange("p a t -> p (a t)")
                TT(fa[:, at.par, :], fa[:, at.par, :], weight, MUL).then_inc(s["hid_ready"], 1)

            def sv(at, l, b):
                if b == 0:
                    ch.link(nc.vector.memset(flat[:, 0:(CB + 1) * PADW], 0.0))
                dve.wait_ge(s["unit_done"], at.u + 1)
                copy(vv[:, b, :], at.bank[:, 0, :]).then_inc(s["psum_free"], 1)

            def squares(at, count, src):
                dve.wait_ge(s["sum_ready"], count)
                ch.link(TS(nmean, at.bank[:, 0, :], -1.0 / (CB * P), None, MUL))
                for b in range(CB):
                    TT(src[:, b, :], src[:, b, :], nmean, ADD).then_inc(s["cen_ready"], 1)
                dve.wait_ge(s["cssq_ready"], count)
                TS(row1[:, :], at.bank[:, 1, :], 1.0 / (CB * P), EPS2, MUL, ADD).then_inc(s["psum_free"], 1)
                dve.wait_ge(s["croot_ready"], count)
                ch.link(nc.vector.reciprocal(rstd[:, :], row1[:, :]))

            def sgu_norm(l):
                for b in range(CB):
                    last = STT(vv[:, b, :], vv[:, b, :], col(f"slg{l}", b), rstd[:, :], MUL, MUL)
                ch.link(last)
                for b in range(CB):
                    last = TS(vv[:, b, :], vv[:, b, :], col(f"slb{l}", b), None, ADD)
                last.then_inc(s["vn_ready"], 1)

            def cval(at, l, b):
                dve.wait_ge(s["gate_ready"], CB * l + b + 1)
                dve.wait_ge(s["unit_done"], at.u + 1)
                TT(glu[:, b, 15:15 + T], sgate[:, b % 2, :], at.bank[:, 0, :], MUL).then_inc(s["psum_free"], 2)
                dve.wait_ge(s["psum_free"], at.n + 1)
                ins = TS(cv[:, b, :], glu[:, b, 0:T], col(f"cw{l}", TAPS * b), col(f"cb{l}", b), MUL, ADD)
                for t in range(1, TAPS):
                    ch.link(ins)
                    ins = STT(cv[:, b, :], glu[:, b, t:t + T], col(f"cw{l}", TAPS * b + t), cv[:, b, :], MUL, ADD)
                if b == CB - 1:
                    ins.then_inc(s["conv_ready"], 1)
                    dve.wait_ge(s["conv_ready"], l + 1)
                else:
                    ch.link(ins)

            def pool(at, l, b):
                x, s2, s4, s8, d = (pl[:, k, :] for k in (0, 1, 2, 3, 4 + b))
                w = slice(16, 16 + T)
                dve.wait_ge(s["unit_done"], at.u + 1)
                if b:
                    dve.wait_ge(s["diff_ready"], 2 * l + b)
                copy(x[:, w], at.bank[:, 0, :]).then_inc(s["psum_free"], 1)
                dve.wait_ge(s["psum_free"], at.n + 1)
                ch.link(TT(s2[:, 1:PADW], x[:, 0:PADW - 1], x[:, 1:PADW], ADD))
                ch.link(TT(s4[:, 2:PADW - 1], s2[:, 1:PADW - 2], s2[:, 3:PADW], ADD))
                low, high = s2, s4
                if b:
                    ch.link(TT(s8[:, 4:PADW - 4], s4[:, 2:PADW - 6], s4[:, 6:PADW - 2], ADD))
                    ch.link(TT(s2[:, w], s8[:, 12:12 + T], s8[:, 20:20 + T], ADD))
                    low, high = s8, s2
                rc = col("rcount", T * b, T)
                TT(d[0:64, w], low[0:64, w], rc[0:64, :], MUL)
                ch.link(TT(d[64:128, w], high[64:128, w], rc[64:128, :], MUL))
                TT(d[:, w], d[:, w], x[:, w], SUB).then_inc(s["diff_ready"], 1)

            def su(at, l, b):
                if b == 0:
                    dve.wait_ge(s["smix_ready"], l + 1)
                    for o, mixed in enumerate((bank[1][:, 0, :], bank[1][:, 1, :], bank[2][:, 0, :])):
                        for c in range(2):
                            w = slice(HALF * c, HALF * c + HALF)
                            ins = TT(gated[:, o, w], mixed[:, w], col(f"sgub{l}", P * o, P), ADD)
                    ch.link(ins)
                dve.wait_ge(s["unit_done"], at.u + 1)
                TT(gated[:, b, :], gated[:, b, :], at.bank[:, 0, :], MUL).then_inc(s["psum_free"], 1)
                mix_rest(MIX2 + 8 * l + 2 * b, 5 + b, gated[:, b, :])
                if b < 2:
                    dve.wait_ge(s["pool_ready"], 2 * l + b + 1)
                    TS(pmix[:, b, :], bank[(3, 0)[b]][:, 0, :], col(f"pscale{l}", b), None, MUL).then_inc(s["poolv_ready"], 1)
                    mix_rest(MIX2 + 8 * l + 2 * b + 1, b, pmix[:, b, :])

            def conv_norm(l):
                for b in range(CB):
                    STT(cv[:, b, :], cv[:, b, :], col(f"clg{l}", b), rstd[:, :], MUL, MUL).then_inc(s["cn_ready"], 1)
                for b in range(CB):
                    mix_rest(MIX2 + 8 * l + 5 + b, 2 + b, cv[:, b, :])

            def route():
                lg, sub, ex, comb, gt, eq, rk = (sml[:, k, :] for k in (1, 2, 3, 6, 8, 9, 10))
                before = cols("before").rearrange("p (e j) -> p e j", e=NEXP)
                dve.wait_ge(s["logit_ready"], 1)
                for c in range(2):
                    w = slice(8 * c, 8 * c + 8)
                    ins = TT(lg[:, w], bank[0][:, 0, w], cols("rb"), ADD)
                ch.link(ins)
                for c in range(2):
                    w = slice(8 * c, 8 * c + 8)
                    own = lg[:, w].rearrange("p (e j) -> p e j", j=1).to_broadcast([P, NEXP, NEXP])
                    other = lg[:, w].rearrange("p (e j) -> p e j", e=1).to_broadcast([P, NEXP, NEXP])
                    g3 = gt.rearrange("p (e j) -> p e j", e=NEXP)
                    e3 = eq.rearrange("p (e j) -> p e j", e=NEXP)
                    TT(g3, other, own, ALU.is_gt)
                    ch.link(TT(e3, other, own, ALU.is_equal))
                    ch.link(TT(e3, e3, before, MUL))
                    ch.link(TT(g3, g3, e3, ADD))
                    nc.vector.tensor_reduce(rk[:, w], g3, AX.X, ADD)
                    ch.link(nc.vector.tensor_reduce(rk[:, 16 + c:17 + c], lg[:, w], AX.X, ALU.max))
                    TS(sub[:, w], lg[:, w], rk[:, 16 + c:17 + c], None, SUB).then_inc(s["rsub_ready"], 1)
                ch.link(TS(rk[:, 32:48], rk[:, 0:16], 1.5, None, ALU.is_lt))
                dve.wait_ge(s["rexp_ready"], 1)
                ch.link(TT(comb[:, 0:16], ex[:, 0:16], rk[:, 32:48], MUL))
                for c in range(2):
                    ins = nc.vector.tensor_reduce(rk[:, 48 + c:49 + c], comb[:, 8 * c:8 * c + 8], AX.X, ADD)
                ch.link(ins)
                ch.link(nc.vector.reciprocal(rk[:, 50:52], rk[:, 48:50]))
                for c in range(2):
                    w = slice(8 * c, 8 * c + 8)
                    ins = TS(comb[:, w], comb[:, w], rk[:, 50 + c:51 + c], None, MUL)
                ins.then_inc(s["comb_ready"], 1)

            def route_spread():
                dve.wait_ge(s["combt_ready"], 1)
                copy(rowF[0:8, 0, :], bank[1][0:8, 0, :]).then_inc(s["combv_ready"], 1)

            dve.wait_ge(s["par_in"], 16)
            dve.wait_ge(s["ada_done"], ADA)
            for l in range(DEPTH):
                ins = TT(mod[:, 48 * l:48 * l + 48], bank[7][:, 0, 48 * l:48 * l + 48], cols(f"adab{l}"), ADD)
            ch.link(ins)
            for l in range(DEPTH):
                for t, name in enumerate(("mixg", "ffng")):
                    a = 48 * l + 24 * t + 8
                    ins = STT(modg[:, 2 * l + t, :], mod[:, a:a + 8], 1.0, cols(f"{name}{l}"), ADD, MUL)
            ins.then_inc(s["mod_ready"], 1)
            walk(dve, split, {
                "norm": norm, "xbc": xbc, "dt": dt, "xbc_last": nothing, "sc_c": sc_c, "sc_v": sc_v,
                "sc_b": sc_b, "z": z, "ssd_scores": ssd_scores, "ssd_out": ssd_out, "mixdown": nothing,
                "group_norm": group_norm, "residual": residual, "f_gate": f_gate, "f_up": f_up, "f_hid": hid,
                "d_gate": nothing, "d_up": d_up, "d_hid": hid, "e_gate": nothing, "e_up": e_up,
                "e_hid": hid, "down": nothing, "sv": sv, "cgate": nothing, "cval": cval, "sums": nothing,
                "squares": squares, "sgu_norm": sgu_norm, "sgu_turn": nothing, "sgu_mix": nothing,
                "pool": pool, "su": su, "conv_norm": conv_norm, "route": route,
                "route_spread": route_spread}, ch)


def _up(w):
    k, n = w.shape
    return w.reshape(k // P, P, n // P, P).transpose(2, 1, 0, 3).reshape(n // P, P, UW)


def _down(w):
    return w.reshape(-1, P, UW)


def _hidden(units, gate, up, down):
    g, u, d = _up(gate), _up(up), _down(down)
    for j in range(len(g)):
        units += [g[j], u[j]] + ([d[j - 1]] if j else [])
    units.append(d[-1])


def _stream(i):
    units = []
    for l in range(DEPTH):
        w = i["w_in"][l]
        xbc, short = _up(w[:, 1024:3072]), [_up(w[:, a:a + D]) for a in (4128, 5152, 3104)]
        units += [xbc[b] for b in [8, 9, 10, 11, 12, 13, 14, 15, 0, 1, 2, 3, 4, 5, 6, 7]]
        units += [short[t][j] for j in range(KB) for t in range(3)]
        units += list(_up(w[:, 0:D]))
        wo = _down(i["w_out"][l])
        units += [wo[(k + 8) % 16] for k in range(16)]
        f = i["w_ffn_up"][l]
        _hidden(units, f[:, 0:NFF * P], f[:, NFF * P:], i["w_ffn_down"][l])
    for l in range(DEPTH):
        w = _up(i["w_in_2"][l])
        order = [11, 12, 13, 5, 2, 6, 3, 7, 4, 0, 1, 8, 9, 10]
        units += [w[b] for b in order]
        wo = _down(i["w_out_2"][l])
        units += [wo[b] for b in [5, 0, 6, 1, 7, 2, 3, 4]]
        if l == 0:
            _hidden(units, i["ffn_w_gate_2"][0], i["ffn_w_up_2"][0], i["ffn_w_down_2"][0])
        else:
            gate, up, down = (np.concatenate(list(i[n][0]), axis=a) for n, a in
                              (("moe_w_gate_2", 1), ("moe_w_up_2", 1), ("moe_w_down_2", 0)))
            _hidden(units, gate, up, down)
    assert len(units) == UNITS
    out = np.empty((UNITS // 2, P, 2 * UW), np.float32)
    for n, a in enumerate(units):
        out[n // 2, :, UW * (n % 2):UW * (n % 2) + UW] = a
    return out


def _params(i):
    par = np.zeros((P, NCOLS), np.float32)

    def put(name, a, rows=P):
        at, width = COLS[name]
        par[0:rows, at:at + width] = a

    def feat(v):
        v = np.asarray(v)
        v = v.reshape(-1, v.shape[-1] // P, P)
        return v.transpose(2, 1, 0).reshape(P, -1)

    def all_rows(v):
        return np.broadcast_to(np.asarray(v).reshape(1, -1), (P, np.size(v)))

    for l in range(DEPTH):
        put(f"norm1{l}", feat(i["norm1_w"][l]))
        put(f"norm2{l}", feat(i["norm2_w"][l]))
        put(f"xw{l}", feat(i["conv_xbc_w"][l]))
        put(f"xb{l}", feat(i["conv_xbc_b"][l]))
        put(f"sw{l}", feat(i["sc_conv_w"][l]))
        put(f"gn{l}", feat(i["ssd_norm_w"][l]))
        put(f"skip{l}", feat(np.repeat(i["d_skip"][l], 64)))
        put(f"fw{l}", feat(i["ffn_conv_w"][l]))
        put(f"fb{l}", feat(i["ffn_conv_b"][l]))
        put(f"dtb{l}", all_rows(np.concatenate([i["dt_bias_f"][l], i["dt_bias_b"][l]])))
        put(f"alog{l}", all_rows(np.concatenate([i["a_log_f"][l], i["a_log_b"][l]])))
        wdt = i["w_in"][l][:, 3072:3104]
        put(f"wdt{l}", wdt.reshape(KB, P, 32).transpose(1, 0, 2).reshape(P, -1))
        put(f"mixg{l}", feat(i["mix_norm_g_2"][l]))
        put(f"ffng{l}", feat(i["ffn_norm_g_2"][l]))
        put(f"pscale{l}", feat(i["pool_scale_2"][l]))
        put(f"cw{l}", feat(i["conv_w_2"][l]))
        for name, key in (("cb", "conv_b_2"), ("clg", "conv_ln_g_2"), ("clb", "conv_ln_b_2"),
                          ("slg", "sgu_ln_g_2"), ("slb", "sgu_ln_b_2"), ("adab", "ada_b_2")):
            put(f"{name}{l}", feat(i[key][l]))
        pw = np.zeros((P, 2, P), np.float32)
        for g in range(4):
            r = slice(64 * (g % 2), 64 * (g % 2) + 64)
            pw[r, g // 2, r] = i["pool_w_2"][l][g]
        put(f"pw{l}", pw.reshape(P, -1))
        put(f"sguw{l}", i["sgu_w_2"][l].transpose(2, 0, 1).reshape(P, -1))
        b = i["sgu_b_2"][l].reshape(CB, 2, P)
        put(f"sgub{l}", np.repeat(b, 64, axis=1).transpose(1, 0, 2).reshape(P, -1))
    put("final1", feat(i["final_norm_w"]))
    put("final2", feat(i["final_norm_g_2"]))
    put("cond", feat(i["c_2"][0]))
    put("rw", i["router_w_2"][0].reshape(KB, P, NEXP).transpose(1, 0, 2).reshape(P, -1))
    put("rb", all_rows(i["router_b_2"][0]))
    put("ident", np.eye(P))
    put("ones", 1.0)
    put("triu", np.triu(np.ones((P, P))))
    put("tril", np.tril(np.ones((P, P))))
    t = np.arange(T)
    rc = np.zeros((P, 2, T))
    for g, w in enumerate((2, 4, 8, 16)):
        count = np.clip(t + w // 2, 0, T) - np.clip(t - w // 2, 0, T)
        rc[64 * (g % 2):64 * (g % 2) + 64, g // 2, :] = 1.0 / count
    put("rcount", rc.reshape(P, -1))
    e = np.arange(NEXP)
    put("before", all_rows((e[None, :] < e[:, None]).astype(np.float32)))
    return par


def kernel(**inputs):
    import concourse.bacc as bacc
    from concourse.bass_utils import run_bass_kernel_spmd as run

    i = {k: np.asarray(v) for k, v in inputs.items()}
    ada = np.concatenate([_up(i["ada_w_2"][l]) for l in range(DEPTH)])
    arrays = {
        "weights": _stream(i),
        "ada": np.ascontiguousarray(ada.reshape(ADA // 2, 2, P, UW).transpose(0, 2, 1, 3)).reshape(ADA // 2, P, 2 * UW),
        "x_t": np.ascontiguousarray(i["x"][0].T.reshape(KB, P, T).transpose(1, 0, 2)).reshape(P, KB * T),
        "params": _params(i),
    }
    nc = bacc.Bacc("TRN2", target_bir_lowering=False, num_devices=1)
    args = [nc.dram_tensor(name, a.shape, F32, kind="ExternalInput").ap() for name, a in arrays.items()]
    out = nc.dram_tensor("out_t", (P, KB * T), F32, kind="ExternalOutput").ap()
    build(nc, *args, out)
    r = run(nc, [arrays], core_ids=[0])
    got = r.results[0]["out_t"].reshape(P, KB, T)
    return got.transpose(2, 1, 0).reshape(1, T, D)
```

```python
from contextlib import ExitStack

import numpy as np

import concourse.bass as bass
from concourse import mybir

F32, F32R = mybir.dt.float32, mybir.dt.float32r
ACT, ALU = mybir.ActivationFunctionType, mybir.AluOpType
AX = mybir.AxisListType

P = 128
T = 256
D = 1024
KB = D // P
DEPTH = 2
HALF = T // 2
HEADS = 16
XBC = 16
NFF = 2816 // P
NEXP = 8
NFE = 3584 // P
GW = 512
GROUPS = NFE * P // GW
GU = 12 * GROUPS
CAP = P
MORE = 3
TAPS = 31
CB = 3
UW = KB * P
SLOTS = 6
PAIRS = SLOTS // 2
LEAD = 4
ADA = DEPTH * 48
DENSE = DEPTH * (48 + 16 + 3 * NFF) + DEPTH * (14 + 8) + 3 * NFF
UNITS = DENSE + NEXP * GU
EPS1, EPS2 = 1e-5, 1e-6

COLS = {}


def _columns():
    at = 0

    def add(name, width):
        nonlocal at
        COLS[name] = (at, width)
        at += width
    for l in range(DEPTH):
        for name, width in (("norm1", 8), ("norm2", 8), ("xw", 3 * XBC), ("xb", XBC), ("sw", 3 * 8),
                            ("gn", 8), ("skip", 8), ("fw", 3 * 2 * NFF), ("fb", 2 * NFF),
                            ("dtb", 32), ("alog", 32), ("wdt", KB * 32)):
            add(f"{name}{l}", width)
        for name, width in (("mixg", 8), ("ffng", 8), ("pscale", 2), ("cw", CB * TAPS), ("cb", CB),
                            ("clg", CB), ("clb", CB), ("slg", CB), ("slb", CB), ("adab", 48),
                            ("pw", 2 * P), ("sguw", 6 * P), ("sgub", CB * P)):
            add(f"{name}{l}", width)
    for name, width in (("final1", 8), ("final2", 8), ("cond", 8), ("rw", 64), ("rb", 8), ("ident", P),
                        ("ones", P), ("triu", P), ("tril", P), ("rcount", 2 * T), ("before", 64),
                        ("iota", P), ("offset", 16)):
        add(name, width)
    return at


NCOLS = _columns()


def build(nc, w_hbm, ada_hbm, x_hbm, par_hbm, out_hbm):
    with ExitStack() as ctx:
        def sb(name, shape, dt=F32):
            return ctx.enter_context(nc.sbuf_tensor(name, shape, dt))

        def sem(name):
            return ctx.enter_context(nc.semaphore(name))

        par = sb("par", [P, NCOLS])
        raw = sb("raw", [P, SLOTS, UW])
        whi = sb("whi", [P, SLOTS, UW], F32R)
        wlo = sb("wlo", [P, SLOTS, UW], F32R)
        h = sb("h", [P, KB, T])
        nhi = sb("nhi", [P, KB, T], F32R)
        nlo = sb("nlo", [P, KB, T], F32R)
        mhi = sb("mhi", [P, 2 * KB, T], F32R)
        mlo = sb("mlo", [P, 2 * KB, T], F32R)
        area = sb("area", [P, 24, T])
        work = sb("work", [P, 15, T])
        ring = sb("ring", [P, 7, T])
        mod = sb("mod", [P, ADA])
        modg = sb("modg", [P, 4, KB])
        cond = sb("cond", [P, KB])
        sml = sb("sml", [P, 12, 64])
        nF = sb("nF", [P, 2, 32])
        itab = sb("itab", [P, 16], mybir.dt.int32)
        rowF = sb("rowF", [HEADS, 2, T])
        row1 = sb("row1", [P, T])
        rstd = sb("rstd", [P, T])
        token = sb("token", [P, 1])
        bank = [ctx.enter_context(nc.psum_tensor(f"bank{b}", [P, 2, T], F32)) for b in range(8)]

        def cols(name):
            a, width = COLS[name]
            return par[:, a:a + width]

        def col(name, k=0, width=1):
            a = COLS[name][0] + k
            return par[:, a:a + width]

        def spreader(rows, k):
            a = COLS["ident"][0] + k
            return par[0:rows, a:a + 1].to_broadcast([rows, P])

        xs, Bt, Ct, nf = area[:, 0:8, :], area[:, 8:12, :], area[:, 12:16, :], area[:, 16:24, :]
        adaring = area[:, :, :].rearrange("p (s a) t -> p s (a t)", s=PAIRS)
        adasum = work[:, 0:12, :].rearrange("p (g a) t -> p g (a t)", g=3)
        y1 = nf
        fg, fu, fs, fa = (area[:, 2 * a:2 * a + 2, :] for a in range(4))
        def halves(a, n):
            return a.rearrange("p a t -> p (a t)").rearrange("p (k t) -> p k t", k=n)
        xgh, xgl = halves(mhi[:, 0:4, :], KB), halves(mlo[:, 0:4, :], KB)
        hth, htl = halves(mhi[:, 4:6, :], 4), halves(mlo[:, 4:6, :], 4)
        place = halves(mhi[:, 6:7, :], 2)
        xth, xtl = halves(nhi[:, :, :], 2), halves(nlo[:, :, :], 2)
        wplace, wplace_t, yg = halves(work[:, 0:1, :], 2), work[:, 1, :], halves(work[:, 2:6, :], 2)
        es, eh = halves(area[:, 0:2, :], 1)[:, 0, :], halves(area[:, 2:4, :], 4)
        ahi, alo = mhi[:, 0:2, :], mlo[:, 0:2, :]
        dec = work[:, 0:6, :].rearrange("p (r a) (b c) -> p r (a b) c", r=2, b=2)
        prod = work[:, 6:12, :].rearrange("p (r a) (b c) -> p r (a b) c", r=2, b=2)
        s6 = work[:, 12:15, :].rearrange("p a (b c) -> p (a b) c", b=2)
        xtok = ring[:, 0:2, :].rearrange("p r (c x) -> p r c x", c=2)
        short_c, short_p, short_q, short_m = ring[:, 2, :], ring[:, 3, :], ring[:, 4, :], ring[:, 5:7, :]
        PADW = T + 32
        flat = area[:, 0:11, :].rearrange("p a t -> p (a t)")
        glu = flat[:, 0:CB * PADW].rearrange("p (b t) -> p b t", b=CB)
        pl = flat[:, CB * PADW:(CB + 6) * PADW].rearrange("p (b t) -> p b t", b=6)
        cv, pmix = area[:, 11:14, :], area[:, 14:16, :]
        vtok = work[:, 0:3, :].rearrange("p a t -> p (a t)").rearrange("p (c x) -> p c x", c=2)
        gated, sq3, sgate, nmean, vv = (work[:, 3:6, :], work[:, 6:9, :], work[:, 9:11, :],
                                        work[:, 11, :], work[:, 12:15, :])

        s = {}
        for name in """par_in x_in cond_ready ada_used ada_done mod_ready hi_ready lo_ready unit_done psum_free
                h_ready sq_ready ssq_ready var_ready root_ready n_ready nhi_ready nlo_ready fin_ready
                flin_ready silu_ready hid_ready ahi_ready alo_ready
                xlin_ready xbc_ready dt_ready dtv_ready dta_ready a_ready cum_ready cumv_ready
                score_ready s6_ready bc_ready clamp_ready xtp_ready xtok_ready dec_ready prod_ready y_ready y1_ready
                scq_ready mhi_ready mlo_ready zs_ready ysq_ready gssq_ready groot_ready gy_ready
                gate_ready conv_ready sum_ready cen_ready csq_ready cssq_ready croot_ready cn_ready
                cs_ready vn_ready vtp_ready vtok_ready smix_ready diff_ready pool_ready poolv_ready
                logit_ready rsub_ready rexp_ready sel_ready count_ready tab_ready xt_ready xth_ready
                xtl_ready place_ready xg_ready xgh_ready xgl_ready wpt_ready wptv_ready ht_ready
                yg_ready ys_ready hadd_ready
                out_stored""".split():
            s[name] = sem(name)
        loaded = [sem(f"loaded{k}") for k in range(PAIRS)]
        ada_in = [sem(f"ada_in{k}") for k in range(PAIRS)]
        block = ctx.enter_context(nc.Block())

        class At:

            def __init__(self, u, n, j, i=0):
                self.cu, self.cn, self.cj, self.i = u, n, j, i
                self.u, self.n, self.j = u + 6 * i, n + 4 * i, j + 2 * i
                self.slot, self.bank, self.par = u % SLOTS, bank[4 + n % 4], j % 2

            def ahead(self, k):
                return At(self.cu + k, self.cn, self.cj, self.i)

        class Chain:

            def __init__(self, eng, name):
                self.eng, self.sem, self.n, self.i, self.step = eng, sem(name), 0, 0, 0

            def mark(self, ins):
                ins.then_inc(self.sem, 1)
                self.n += 1

            def wait(self):
                self.eng.wait_ge(self.sem, self.n + self.step * self.i)

            def link(self, ins):
                self.mark(ins)
                self.wait()

        XBC_ORDER = [8, 9, 10, 11, 12, 13, 14, 15, 0, 1, 2, 3, 4, 5, 6, 7]
        MIX1_ORDER = [(k + 8) % 16 for k in range(16)]
        MIX2_ORDER = [5, 0, 6, 1, 7, 2, 3, 4]
        MIX2 = 16 * DEPTH

        def walk(eng, split, do, chain=None):
            u = n = j = m = 0

            def unit(kind, at, *args):
                split(at.ahead(LEAD))
                do[kind](at, *args)

            def one(kind, *args):
                nonlocal u, n
                unit(kind, At(u, n, 0), *args)
                u, n = u + 1, n + (kind != "mixdown")

            def ffn(kind, count, l, links):
                nonlocal u, n, j

                def pair(i):
                    for k in range(2):
                        a, b, c = u + 3 * k, n + 2 * k, j + k
                        unit(kind + "_gate", At(a, b, c, i), l)
                        unit(kind + "_up", At(a + 1, b + 1, c, i), l)
                        unit("down", At(a + 2, b + 2, c - 1, i), False, False)
                        do[kind + "_hid"](At(a + 2, b + 2, c, i), l)

                unit(kind + "_gate", At(u, n, j), l)
                unit(kind + "_up", At(u + 1, n + 1, j), l)
                do[kind + "_hid"](At(u + 2, n + 2, j), l)
                unit(kind + "_gate", At(u + 2, n + 2, j + 1), l)
                unit(kind + "_up", At(u + 3, n + 3, j + 1), l)
                unit("down", At(u + 4, n + 4, j), True, False)
                do[kind + "_hid"](At(u + 4, n + 4, j + 1), l)
                u, n, j = u + 5, n + 4, j + 2
                loops = (count - 2) // 2
                with eng.Fori(0, loops) as i:
                    if chain is not None:
                        chain.i, chain.step, n0 = i, links, chain.n
                    pair(i)
                if chain is not None:
                    assert chain.n - n0 == links
                    chain.n, chain.i = n0 + links * loops, 0
                u, n, j = u + 6 * loops, n + 4 * loops, j + 2 * loops
                unit("down", At(u, n, j - 1), False, True)
                u += 1

            for v in range(LEAD):
                split(At(v, 0, 0))
            do["norm"](0, EPS1, "first")
            m = 1
            for l in range(DEPTH):
                for k, b in enumerate(XBC_ORDER):
                    one("xbc", l, k, b)
                    if k == 2:
                        do["dt"](l)
                do["xbc_last"](n, l)
                for t in range(KB):
                    one("sc_c", l, t)
                    do["ssd_scores"](l, t)
                    one("sc_v", l, t)
                    one("sc_b", l, t)
                    do["ssd_out"](l, t)
                for t in range(KB):
                    one("z", l, t)
                for k, b in enumerate(MIX1_ORDER):
                    one("mixdown", 16 * l + k, b, k == 0, k == 15)
                    if k == 0:
                        do["group_norm"](At(u, n, 0), l)
                        n += 2
                do["residual"](u, None)
                do["norm"](m, EPS1, "split")
                m += 1
                ffn("f", NFF, l, 4)
                do["residual"](u, None)
                if l < DEPTH - 1:
                    do["norm"](m, EPS1, "split")
                    m += 1
            do["norm"](m, EPS1, "plain")
            m += 1
            for l in range(DEPTH):
                do["norm"](m, EPS2, "shift")
                m += 1
                for b in range(CB):
                    one("sv", l, b)
                ln = At(u, n, 0)
                do["sums"](ln, 2 * l + 1, vv)
                n += 1
                one("cgate", l, 0)
                do["squares"](ln, 2 * l + 1, vv)
                do["sgu_norm"](l)
                one("cval", l, 0)
                do["sgu_turn"](l)
                one("cgate", l, 1)
                do["sgu_mix"](l)
                one("cval", l, 1)
                one("cgate", l, 2)
                one("cval", l, 2)
                for b in range(2):
                    one("pool", l, b)
                for b in range(CB):
                    one("su", l, b)
                for k, b in enumerate(MIX2_ORDER):
                    one("mixdown", MIX2 + 8 * l + k, b, k == 0, k == 7)
                    if k == 0:
                        ln = At(u, n, 0)
                        do["sums"](ln, 2 * l + 2, cv)
                        n += 1
                    if k == 1:
                        do["squares"](ln, 2 * l + 2, cv)
                        do["conv_norm"](l)
                do["residual"](u, 48 * l + 16)
                if l < DEPTH - 1:
                    do["norm"](m, EPS2, "shift")
                    m += 1
                    ffn("d", NFF, l, 0)
                    do["residual"](u, 48 * l + 40)
            do["norm"](m, EPS2, "whole")
            m += 1
            assert u == DENSE, u

            def part(kind, v, i, *args):
                for k in range(4):
                    unit(kind, At(v + k, 0, 0, i), k, *args)

            def group(q, g, first):
                i, t = 14 * q + 2 * (g - 1), GROUPS * q + g
                part("e_gate", u + 8, i, t)
                if first:
                    do["banks_free"](q)
                do["e_turn"](t - 1)
                part("e_up", u + 12, i, t)
                part("e_down", u + 16, i, t - 1, first)

            do["route"](n)
            do["place"](0)
            do["gather"](0)
            do["turn_place"](0)
            passes = eng.value_load(itab[0:1, 15:16], min_val=NEXP, max_val=NEXP + MORE)
            with eng.Fori(0, passes) as q:
                part("e_gate", u, 14 * q, GROUPS * q)
                part("e_up", u + 4, 14 * q, GROUPS * q)
                do["place"](q + 1)
                if do["peels"]:
                    group(q, 1, True)
                    with eng.Fori(2, GROUPS) as g:
                        group(q, g, False)
                else:
                    with eng.Fori(1, GROUPS) as g:
                        group(q, g, False)
                do["e_turn"](GROUPS * q + (GROUPS - 1))
                do["gather"](q + 1)
                part("e_down", u + GU - 4, 14 * q, GROUPS * q + (GROUPS - 1), False)
                do["scatter"](q, u)
                do["turn_place"](q + 1)
            do["experts_done"](passes)
            do["norm"](m, EPS2, "last")

        SPLIT_BEFORE = [0, 1, 2, 3, 4, 4, 5, 6, 7, 7]

        def gain(m, k):
            if m < 5:
                return col(("norm10", "norm20", "norm11", "norm21", "final1")[m], k)
            return col("final2", k) if m == 9 else modg[:, m - 5, k:k + 1]

        def shift(m, k):
            a = 48 * ((m - 5) // 2) + 24 * ((m - 5) % 2) + k
            return mod[:, a:a + 1]

        def nothing(*args):
            pass

        @block.sync
        def _(sp):
            def load(k, src):
                sp.dma_start(raw[:, 2 * k:2 * k + 2, :].rearrange("p a t -> p (a t)"), src).then_inc(loaded[k], 16)

            for k in range(PAIRS):
                load(k, w_hbm[k])
                sp.dma_start(adaring[:, k, :], ada_hbm[k]).then_inc(ada_in[k], 16)
            with sp.Fori(0, ADA // SLOTS - 1) as i:
                for k in range(PAIRS):
                    src = ada_hbm[PAIRS * i + (PAIRS + k)]
                    used = sp.snap(SLOTS * i + (2 * k + 2))
                    sp.wait_ge(s["ada_used"], used)
                    sp.dma_start(adaring[:, k, :], src).then_inc(ada_in[k], 16)
            pairs = DENSE // 2 + PAIRS
            turns = (pairs - PAIRS) // PAIRS
            with sp.Fori(0, turns) as i:
                for k in range(PAIRS):
                    src = w_hbm[PAIRS * i + (PAIRS + k)]
                    used = sp.snap(SLOTS * i + (2 * k + 2))
                    sp.wait_ge(s["lo_ready"], used)
                    load(k, src)
            for p in range(PAIRS * (turns + 1), pairs):
                sp.wait_ge(s["lo_ready"], 2 * (p - PAIRS) + 2)
                load(p % PAIRS, w_hbm[p])
            sp.wait_ge(s["tab_ready"], 1)
            passes = sp.value_load(itab[0:1, 15:16], min_val=NEXP, max_val=NEXP + MORE)
            with sp.Fori(0, passes) as q:
                own = sp.value_load(itab[0:1, bass.ds(q, 1)], min_val=0, max_val=NEXP - 1)
                following = sp.value_load(itab[0:1, bass.ds(q + 1, 1)], min_val=0, max_val=NEXP - 1)
                with sp.Fori(1, GU // SLOTS) as i:
                    for k in range(PAIRS):
                        src = w_hbm[own * (GU // 2) + (PAIRS * i + (DENSE // 2 + k))]
                        used = sp.snap(GU * q + (SLOTS * i + (DENSE - SLOTS + 2 * k + 2)))
                        sp.wait_ge(s["lo_ready"], used)
                        load((DENSE // 2 + k) % PAIRS, src)
                for k in range(PAIRS):
                    src = w_hbm[following * (GU // 2) + (DENSE // 2 + k)]
                    used = sp.snap(GU * q + (GU + DENSE - SLOTS + 2 * k + 2))
                    sp.wait_ge(s["lo_ready"], used)
                    load((DENSE // 2 + k) % PAIRS, src)
            sp.wait_ge(s["fin_ready"], KB)
            sp.dma_start(out_hbm, nf.rearrange("p k t -> p (k t)")).then_inc(s["out_stored"], 16)
            sp.wait_ge(s["out_stored"], 16)

        @block.tensor
        def _(pe):
            mm = nc.tensor.matmul
            fresh = [0]

            def three(out, slot, tile, xh, xl, start, stop):
                w = slice(tile * P, tile * P + P)
                mm(out, whi[:, slot, w], xh, start=start, stop=False, skip_group_check=True)
                mm(out, wlo[:, slot, w], xh, start=False, stop=False, skip_group_check=True)
                return mm(out, whi[:, slot, w], xl, start=False, stop=stop, skip_group_check=True)

            def up(at, *args):
                pe.wait_ge(s["lo_ready"], at.u + 1)
                if at.cn >= 4:
                    pe.wait_ge(s["psum_free"], at.n - 3)
                for k in range(KB):
                    if fresh[0]:
                        pe.wait_ge(s["nlo_ready"], KB * (fresh[0] - 1) + k + 1)
                    last = three(at.bank[:, 0, :], at.slot, k, nhi[:, k, :], nlo[:, k, :],
                                 k == 0, k == KB - 1)
                fresh[0] = 0
                last.then_inc(s["unit_done"], 1)

            def down_tiles(at, xh, xl, first, final):
                for o in range(KB):
                    last = three(bank[o // 2][:, o % 2, :], at.slot, o, xh, xl, first and o % 2 == 0, final)
                last.then_inc(s["unit_done"], 1)

            def mixdown(at, order, b, first, final):
                pe.wait_ge(s["lo_ready"], at.u + 1)
                pe.wait_ge(s["mlo_ready"], order + (4 if first and order >= MIX2 else 1))
                down_tiles(at, mhi[:, b, :], mlo[:, b, :], first, final)

            def down(at, first, final):
                pe.wait_ge(s["lo_ready"], at.u + 1)
                pe.wait_ge(s["alo_ready"], at.j + 1)
                down_tiles(at, ahi[:, at.par, :], alo[:, at.par, :], first, final)

            def norm(m, eps, how):
                for k in range(KB):
                    if k % 2 == 0:
                        pe.wait_ge(s["sq_ready"], 4 * m + k // 2 + 1)
                    last = mm(bank[0][:, 0, :], cols("ones"), nf[:, k, :], start=k == 0, stop=k == KB - 1)
                last.then_inc(s["ssq_ready"], 1)
                if how in ("first", "split", "shift"):
                    fresh[0] = SPLIT_BEFORE[m] + 1

            def dt(l):
                for c in range(2):
                    for k in range(KB):
                        last = mm(bank[0][:, 0, 32 * c:32 * c + 32], nf[:, k, HALF * c:HALF * c + HALF],
                                  col(f"wdt{l}", 32 * k, 32), start=k == 0, stop=k == KB - 1)
                last.then_inc(s["dt_ready"], 1)
                pe.wait_ge(s["a_ready"], l + 1)
                a = sml[:, 0, :].rearrange("p (c h) -> p c h", c=2)
                triu, ones, tril = col("triu", 0, P), cols("ones"), cols("tril")
                o = bank[1][:, 0, 0:64].rearrange("p (c h) -> p c h", c=2)
                mm(o[:, 0, 0:16], triu, a[:, 0, 0:16], start=True, stop=True)
                mm(o[:, 0, 16:32], ones, a[:, 1, 16:32], start=True, stop=False)
                mm(o[:, 0, 16:32], tril, a[:, 0, 16:32], start=False, stop=True)
                mm(o[:, 1, 0:16], ones, a[:, 0, 0:16], start=True, stop=False)
                mm(o[:, 1, 0:16], triu, a[:, 1, 0:16], start=False, stop=True)
                mm(o[:, 1, 16:32], tril, a[:, 1, 16:32], start=True, stop=True)
                f, b = bank[2][0:16, 0, :], bank[3][0:16, 0, :]
                mm(f[:, 0:HALF], a[:, 0, 0:16], triu, start=True, stop=True)
                mm(f[:, HALF:T], a[:, 0, 0:16], ones, start=True, stop=False)
                mm(f[:, HALF:T], a[:, 1, 0:16], triu, start=False, stop=True)
                mm(b[:, 0:HALF], a[:, 1, 16:32], ones, start=True, stop=False)
                mm(b[:, 0:HALF], a[:, 0, 16:32], tril, start=False, stop=True)
                mm(b[:, HALF:T], a[:, 1, 16:32], tril, start=True, stop=True).then_inc(s["cum_ready"], 1)

            def ssd_scores(l, j):
                g, it = j // 2, 8 * l + j
                if j == 0:
                    pe.wait_ge(s["xbc_ready"], 16 * (l + 1))
                    pe.wait_ge(s["cumv_ready"], 3 * (l + 1))
                if j % 2 == 0:
                    if it:
                        pe.wait_ge(s["s6_ready"], 4 * l + g)
                    for c in range(2):
                        last = mm(bank[2][:, c, :], Bt[:, g, HALF * c:HALF * c + HALF], Ct[:, g, :],
                                  start=True, stop=True)
                    last.then_inc(s["score_ready"], 1)
                for r in range(2):
                    if it:
                        pe.wait_ge(s["clamp_ready"], 2 * it + r - 1)
                    for d in range(2):
                        last = mm(bank[r][:, d, :], spreader(16, 2 * j + r), rowF[:, d, :], start=True, stop=True)
                    last.then_inc(s["bc_ready"], 1)
                if it:
                    pe.wait_ge(s["xtok_ready"], it)
                    pe.wait_ge(s["y1_ready"], it)
                for c in range(2):
                    last = nc.tensor.transpose(bank[3][:, 1, HALF * c:HALF * c + HALF],
                                               xs[:, j, HALF * c:HALF * c + HALF], cols("ident"))
                last.then_inc(s["xtp_ready"], 1)

            def ssd_out(l, j):
                it = 8 * l + j
                pe.wait_ge(s["xtok_ready"], it + 1)
                for r in range(2):
                    pe.wait_ge(s["prod_ready"], 2 * it + r + 1)
                    for c in range(2):
                        last = mm(bank[3][64 * r:64 * r + 64, 0, :], xtok[:, it % 2, c, 64 * r:64 * r + 64],
                                  prod[:, r, 2 * c:2 * c + 2, :].rearrange("p a b -> p (a b)"),
                                  start=c == 0, stop=c == 1)
                last.then_inc(s["y_ready"], 1)

            def group_norm(at, l):
                for g in range(4):
                    if g % 2 == 0:
                        pe.wait_ge(s["psum_free"], at.n - 3 + g // 2)
                    pe.wait_ge(s["ysq_ready"], 8 * l + 2 * g + 2)
                    b = bank[4 + (at.cn + g // 2) % 4]
                    for k in range(2):
                        last = mm(b[:, g % 2, :], cols("ones"), xs[:, 2 * g + k, :], start=k == 0, stop=k == 1)
                    last.then_inc(s["gssq_ready"], 1)

            def sums(at, count, src):
                pe.wait_ge(s["psum_free"], at.n - 3)
                if count % 2:
                    pe.wait_ge(s["psum_free"], at.n)
                else:
                    pe.wait_ge(s["conv_ready"], count // 2)
                for b in range(CB):
                    last = mm(at.bank[:, 0, :], cols("ones"), src[:, b, :], start=b == 0, stop=b == CB - 1)
                last.then_inc(s["sum_ready"], 1)

            def squares(at, count, src):
                pe.wait_ge(s["csq_ready"], count)
                for b in range(CB):
                    last = mm(at.bank[:, 1, :], cols("ones"), sq3[:, b, :], start=b == 0, stop=b == CB - 1)
                last.then_inc(s["cssq_ready"], 1)

            def sgu_turn(l):
                pe.wait_ge(s["vn_ready"], l + 1)
                for c in range(2):
                    out = bank[1 + c][:, :, :].rearrange("p a t -> p (a t)")
                    for b in range(CB):
                        last = nc.tensor.transpose(out[:, P * b:P * b + P], vv[:, b, HALF * c:HALF * c + HALF],
                                                   cols("ident"))
                    last.then_inc(s["vtp_ready"], 1)

            def sgu_mix(l):
                pe.wait_ge(s["vtok_ready"], 2 * (l + 1))
                for b in range(CB):
                    o = (bank[1][:, 0, :], bank[1][:, 1, :], bank[2][:, 0, :])[b]
                    for r in range(2):
                        hd = 2 * b + r
                        for c in range(2):
                            last = mm(o[64 * r:64 * r + 64, HALF * c:HALF * c + HALF],
                                      vtok[:, c, 64 * hd:64 * hd + 64], col(f"sguw{l}", P * hd, P),
                                      start=True, stop=True)
                last.then_inc(s["smix_ready"], 1)

            def su(at, l, b):
                up(at)
                if b < 2:
                    pe.wait_ge(s["diff_ready"], 2 * l + b + 1)
                    mm(bank[(3, 0)[b]][:, 0, :], col(f"pw{l}", P * b, P), pl[:, 4 + b, 16:16 + T],
                       start=True, stop=True).then_inc(s["pool_ready"], 1)

            def wide(b):
                return bank[b][:, :, :].rearrange("p a t -> p (a t)")

            def route(n):
                pe.wait_ge(s["n_ready"], KB * 8)
                pe.wait_ge(s["psum_free"], n)
                for c in range(2):
                    for k in range(KB):
                        last = mm(bank[7][:, 0, 8 * c:8 * c + 8], nf[:, k, HALF * c:HALF * c + HALF],
                                  col("rw", 8 * k, 8), start=k == 0, stop=k == KB - 1)
                last.then_inc(s["logit_ready"], 1)
                for c in range(2):
                    for k in range(KB):
                        last = nc.tensor.transpose(wide(2 * c + k // 4)[:, P * (k % 4):P * (k % 4) + P],
                                                   nf[:, k, HALF * c:HALF * c + HALF], cols("ident"))
                        if k % 4 == 3:
                            last.then_inc(s["xt_ready"], 1)
                pe.wait_ge(s["sel_ready"], 1)
                sel, triu, ones = sml[:, 11, 0:16], col("triu", 0, P), cols("ones")
                o = bank[7][:, 1, :]
                mm(o[:, 0:8], triu, sel[:, 0:8], start=True, stop=True)
                mm(o[:, 8:16], ones, sel[:, 0:8], start=True, stop=False)
                mm(o[:, 8:16], triu, sel[:, 8:16], start=False, stop=True)
                mm(o[:, 16:24], ones, sel[:, 0:8], start=True, stop=False)
                mm(o[:, 16:24], ones, sel[:, 8:16], start=False, stop=True).then_inc(s["count_ready"], 1)
                pe.wait_ge(s["xtl_ready"], 4)
                pe.wait_ge(s["tab_ready"], 1)

            def moved(out, xh, xl, slot, w, start, stop):
                mm(out, xh, whi[:, slot, w], start=start, stop=False, skip_group_check=True)
                mm(out, xh, wlo[:, slot, w], start=False, stop=False, skip_group_check=True)
                return mm(out, xl, whi[:, slot, w], start=False, stop=stop, skip_group_check=True)

            def gather(q):
                pe.wait_ge(s["place_ready"], 2 * q + 1)
                for x, b in ((xth, 2), (xtl, 4)):
                    for k in range(KB):
                        for c in range(2):
                            last = mm(wide(b + k // 4)[:, P * (k % 4):P * (k % 4) + P],
                                      x[:, c, P * k:P * k + P], place[:, c, :], start=c == 0, stop=c == 1)
                    last.then_inc(s["xg_ready"], 1)

            def turn_place(q):
                pe.wait_ge(s["place_ready"], 2 * q + 2)
                for c in range(2):
                    last = nc.tensor.transpose(bank[0][:, 0, HALF * c:HALF * c + HALF], wplace[:, c, :], cols("ident"))
                last.then_inc(s["wpt_ready"], 1)
                pe.wait_ge(s["xgh_ready"], q + 1)
                pe.wait_ge(s["xgl_ready"], q + 1)

            def e_hidden(at, k, b):
                pe.wait_ge(s["lo_ready"], at.u + 1)
                for kk in range(2):
                    x = 2 * k + kk
                    last = moved(wide(b), xgh[:, x, :], xgl[:, x, :], at.slot, slice(GW * kk, GW * kk + GW),
                                 x == 0, x == KB - 1)
                last.then_inc(s["unit_done"], 1)

            def e_gate(at, k, t):
                if k == 0:
                    pe.wait_ge(s["silu_ready"], 3 * NFF + t)
                e_hidden(at, k, 4)

            def e_up(at, k, t):
                if k == 0:
                    pe.wait_ge(s["hid_ready"], 2 * NFF + t)
                e_hidden(at, k, 5)

            def banks_free(q):
                pe.wait_ge(s["hadd_ready"], q + 1)
                pe.wait_ge(s["wptv_ready"], q + 1)

            def e_turn(t):
                pe.wait_ge(s["hid_ready"], t + (2 * NFF + 1))
                for b in range(4):
                    last = nc.tensor.transpose(wide(6)[:, P * b:P * b + P], eh[:, b, :], cols("ident"))
                last.then_inc(s["ht_ready"], 1)

            def e_down(at, k, t, first):
                pe.wait_ge(s["lo_ready"], at.u + 1)
                if k == 0:
                    pe.wait_ge(s["alo_ready"], t + (3 * NFF + 1))
                for b in range(2):
                    last = moved(wide(b), hth[:, k, :], htl[:, k, :], at.slot, slice(GW * b, GW * b + GW),
                                 first and k == 0, k == 3)
                last.then_inc(s["unit_done"], 1)

            def scatter(q, u):
                pe.wait_ge(s["yg_ready"], 2 * q + 2)
                for o in range(KB):
                    last = mm(bank[(2, 3, 6, 7)[o // 2]][:, o % 2, :], yg[:, o // 4, P * (o % 4):P * (o % 4) + P],
                              wplace_t, start=True, stop=True)
                last.then_inc(s["ys_ready"], 1)

            pe.wait_ge(s["par_in"], 16)
            pe.sem_inc(s["ada_done"], 3)
            with pe.Fori(0, ADA // (3 * KB)) as i:
                for g in range(3):
                    pe.wait_ge(s["ada_used"], 3 * KB * i + (KB * g + KB))
                    for o in range(KB):
                        last = mm(bank[7][:, 0, bass.ds(3 * KB * i + (KB * g + o), 1)],
                                  adasum[:, g, P * o:P * o + P], col("ones", 0, 1), start=True, stop=True)
                    last.then_inc(s["ada_done"], 1)
            walk(pe, nothing, {
                "norm": norm, "xbc": up, "dt": dt, "xbc_last": nothing, "sc_c": up, "sc_v": up, "sc_b": up,
                "z": up, "ssd_scores": ssd_scores, "ssd_out": ssd_out, "mixdown": mixdown,
                "group_norm": group_norm, "residual": nothing, "f_gate": up, "f_up": up, "f_hid": nothing,
                "d_gate": up, "d_up": up, "d_hid": nothing,
                "down": down, "sv": up, "cgate": up, "cval": up, "sums": sums, "squares": squares,
                "sgu_norm": nothing, "sgu_turn": sgu_turn, "sgu_mix": sgu_mix, "pool": up, "su": su,
                "conv_norm": nothing, "route": route, "place": nothing, "gather": gather,
                "turn_place": turn_place, "e_gate": e_gate, "e_up": e_up, "banks_free": banks_free,
                "e_turn": e_turn, "e_down": e_down, "scatter": scatter, "experts_done": nothing, "peels": True})

        @block.scalar
        def _(act):
            A, copy = nc.scalar.activation, nc.scalar.copy

            act.dma_start(par[:, :], par_hbm).then_inc(s["par_in"], 16)
            act.dma_start(h[:, :, :].rearrange("p k t -> p (k t)"), x_hbm).then_inc(s["x_in"], 16)
            act.wait_ge(s["par_in"], 16)
            A(cond[:, :], cols("cond"), ACT.Silu).then_inc(s["cond_ready"], 1)

            def split(at):
                act.wait_ge(loaded[at.slot // 2], 16 * (at.cu // SLOTS) + 16 + 16 * at.i)
                if at.cu >= SLOTS:
                    act.wait_ge(s["unit_done"], at.u - (SLOTS - 1))
                copy(whi[:, at.slot, :], raw[:, at.slot, :]).then_inc(s["hi_ready"], 1)

            def norm(m, eps, how):
                for q in range(4):
                    if m == 0:
                        act.wait_ge(s["x_in"], 16)
                        act.wait_ge(s["mod_ready"], 1)
                    else:
                        act.wait_ge(s["h_ready"], 4 * (m - 1) + q + 1)
                    A(nf[:, 2 * q:2 * q + 2, :], h[:, 2 * q:2 * q + 2, :], ACT.Square).then_inc(s["sq_ready"], 1)
                act.wait_ge(s["var_ready"], m + 1)
                A(row1[:, :], row1[:, :], ACT.Sqrt).then_inc(s["root_ready"], 1)
                if how in ("first", "split", "shift"):
                    for k in range(KB):
                        act.wait_ge(s["n_ready"], KB * SPLIT_BEFORE[m] + k + 1)
                        copy(nhi[:, k, :], nf[:, k, :]).then_inc(s["nhi_ready"], 1)

            def xbc(at, l, k, b):
                act.wait_ge(s["unit_done"], at.u + 1)
                if k >= 2:
                    act.wait_ge(s["xbc_ready"], 16 * l + k - 1)
                A(ring[:, k % 2, :], at.bank[:, 0, :], ACT.Identity, bias=col(f"xb{l}", b),
                  scale=col(f"xw{l}", 3 * b + 1)).then_inc(s["xlin_ready"], 1)
                if k:
                    xbc_silu(at.n, k - 1)

            def xbc_silu(done, k):
                act.wait_ge(s["psum_free"], done)
                A(area[:, XBC_ORDER[k], :], ring[:, k % 2, :], ACT.Silu).then_inc(s["xbc_ready"], 1)

            def xbc_last(n, l):
                xbc_silu(n, XBC - 1)

            def dt(l):
                act.wait_ge(s["dtv_ready"], 2 * l + 1)
                A(sml[:, 3, :], sml[:, 2, :], ACT.Exp).then_inc(s["dta_ready"], 1)
                A(sml[:, 7, 0:32], cols(f"alog{l}"), ACT.Exp).then_inc(s["dta_ready"], 1)
                act.wait_ge(s["dtv_ready"], 2 * l + 2)
                A(sml[:, 5, :], sml[:, 4, :], ACT.Ln).then_inc(s["dta_ready"], 1)

            def ssd_scores(l, j):
                it = 8 * l + j
                act.wait_ge(s["xtp_ready"], it + 1)
                copy(xtok[:, it % 2, :, :].rearrange("p c x -> p (c x)"),
                     bank[3][:, 1, :]).then_inc(s["xtok_ready"], 1)
                for r in range(2):
                    act.wait_ge(s["clamp_ready"], 2 * it + r + 1)
                    A(dec[:, r, :, :], dec[:, r, :, :], ACT.Exp).then_inc(s["dec_ready"], 1)

            def sc_v(at, l, j):
                act.wait_ge(s["psum_free"], at.n + 1)
                A(short_q, short_p, ACT.Copy, scale=col(f"sw{l}", 3 * j + 1)).then_inc(s["scq_ready"], 1)

            def sc_b(at, l, j):
                act.wait_ge(s["psum_free"], at.n + 1)
                copy(mhi[:, 8 + j, :], short_m[:, j % 2, :]).then_inc(s["mhi_ready"], 1)

            def z(at, l, j):
                act.wait_ge(s["unit_done"], at.u + 1)
                A(ring[:, j % 2, :], at.bank[:, 0, :], ACT.Silu).then_inc(s["zs_ready"], 1)
                act.wait_ge(s["psum_free"], at.n + 1)
                A(xs[:, j, :], y1[:, j, :], ACT.Square).then_inc(s["ysq_ready"], 1)

            def group_norm(at, l):
                for q in range(2):
                    act.wait_ge(s["psum_free"], at.n + q + 1)
                    A(work[:, 2 * q:2 * q + 2, :], work[:, 2 * q:2 * q + 2, :],
                      ACT.Sqrt).then_inc(s["groot_ready"], 1)
                for k in range(KB):
                    act.wait_ge(s["gy_ready"], 8 * l + k + 1)
                    copy(mhi[:, k, :], y1[:, k, :]).then_inc(s["mhi_ready"], 1)

            def f_lin(at, l, dst, b):
                act.wait_ge(s["unit_done"], at.u + 1)
                A(dst[:, at.par, :], at.bank[:, 0, :], ACT.Identity,
                  bias=par[:, bass.ds(b + COLS[f"fb{l}"][0], 1)],
                  scale=par[:, bass.ds(3 * b + (COLS[f"fw{l}"][0] + 1), 1)]).then_inc(s["flin_ready"], 1)

            def f_gate(at, l):
                f_lin(at, l, fg, at.j - NFF * l)

            def f_up(at, l):
                f_lin(at, l, fu, at.j + (NFF - NFF * l))
                act.wait_ge(s["psum_free"], at.n)
                A(fs[:, at.par, :], fg[:, at.par, :], ACT.Silu).then_inc(s["silu_ready"], 1)

            def f_hid(at, l):
                act.wait_ge(s["hid_ready"], at.j + 1)
                copy(ahi[:, at.par, :], fa[:, at.par, :]).then_inc(s["ahi_ready"], 1)

            def d_gate(at, l):
                act.wait_ge(s["unit_done"], at.u + 1)
                A(fs[:, at.par, :], at.bank[:, 0, :], ACT.Silu).then_inc(s["silu_ready"], 1)

            def d_hid(at, l):
                act.wait_ge(s["psum_free"], at.n)
                copy(ahi[:, at.par, :], fa[:, at.par, :]).then_inc(s["ahi_ready"], 1)

            def squares(at, count, src):
                for b in range(CB):
                    act.wait_ge(s["cen_ready"], CB * (count - 1) + b + 1)
                    last = A(sq3[:, b, :], src[:, b, :], ACT.Square)
                last.then_inc(s["csq_ready"], 1)
                act.wait_ge(s["psum_free"], at.n + 1)
                A(row1[:, :], row1[:, :], ACT.Sqrt).then_inc(s["croot_ready"], 1)

            def sgu_turn(l):
                for c in range(2):
                    act.wait_ge(s["vtp_ready"], 2 * l + c + 1)
                    copy(vtok[:, c, :], bank[1 + c][:, :, :].rearrange("p a t -> p (a t)")[:, 0:CB * P]
                         ).then_inc(s["vtok_ready"], 1)

            def cgate(at, l, b):
                act.wait_ge(s["unit_done"], at.u + 1)
                if b == 2:
                    act.wait_ge(s["psum_free"], at.n - 2)
                A(sgate[:, b % 2, :], at.bank[:, 0, :], ACT.Sigmoid).then_inc(s["gate_ready"], 1)

            def su(at, l, b):
                act.wait_ge(s["psum_free"], at.n + 1)
                copy(mhi[:, 5 + b, :], gated[:, b, :]).then_inc(s["mhi_ready"], 1)
                if b < 2:
                    act.wait_ge(s["poolv_ready"], 2 * l + b + 1)
                    copy(mhi[:, b, :], pmix[:, b, :]).then_inc(s["mhi_ready"], 1)

            def conv_norm(l):
                for b in range(CB):
                    act.wait_ge(s["cn_ready"], CB * l + b + 1)
                    A(cv[:, b, :], cv[:, b, :], ACT.Silu, bias=col(f"clb{l}", b)).then_inc(s["cs_ready"], 1)
                for b in range(CB):
                    act.wait_ge(s["cs_ready"], CB * l + b + 1)
                    copy(mhi[:, 2 + b, :], cv[:, b, :]).then_inc(s["mhi_ready"], 1)

            def wide(b):
                return bank[b][:, :, :].rearrange("p a t -> p (a t)")

            def route(n):
                for b in range(4):
                    act.wait_ge(s["xt_ready"], b + 1)
                    copy(xth[:, b // 2, GW * (b % 2):GW * (b % 2) + GW], wide(b)).then_inc(s["xth_ready"], 1)
                act.wait_ge(s["rsub_ready"], 2)
                A(sml[:, 3, 0:16], sml[:, 2, 0:16], ACT.Exp).then_inc(s["rexp_ready"], 1)
                act.wait_ge(s["tab_ready"], 1)

            def gather(q):
                act.wait_ge(s["xg_ready"], 2 * q + 1)
                for b in range(2):
                    last = copy(xgh[:, 4 * b:4 * b + 4, :].rearrange("p k t -> p (k t)"), wide(2 + b))
                last.then_inc(s["xgh_ready"], 1)

            def turn_place(q):
                act.wait_ge(s["wpt_ready"], q + 1)
                copy(wplace_t, bank[0][:, 0, :]).then_inc(s["wptv_ready"], 1)

            def e_gate(at, k, t):
                if k == 3:
                    act.wait_ge(s["unit_done"], at.u + 1)
                    act.wait_ge(s["hid_ready"], t + 2 * NFF)
                    A(es, wide(4), ACT.Silu).then_inc(s["silu_ready"], 1)

            def e_turn(t):
                act.wait_ge(s["ht_ready"], t + 1)
                copy(hth.rearrange("p k t -> p (k t)"), wide(6)).then_inc(s["ahi_ready"], 1)

            def scatter(q, u):
                act.wait_ge(s["unit_done"], GU * q + (u + GU))
                for b in range(2):
                    copy(yg[:, b, :], wide(b)).then_inc(s["yg_ready"], 1)

            walk(act, split, {
                "norm": norm, "xbc": xbc, "dt": dt, "xbc_last": xbc_last, "sc_c": nothing, "sc_v": sc_v,
                "sc_b": sc_b, "z": z, "ssd_scores": ssd_scores, "ssd_out": nothing, "mixdown": nothing,
                "group_norm": group_norm, "residual": nothing, "f_gate": f_gate, "f_up": f_up, "f_hid": f_hid,
                "d_gate": d_gate, "d_up": nothing, "d_hid": d_hid, "down": nothing, "sv": nothing, "cgate": cgate, "cval": nothing,
                "sums": nothing, "squares": squares, "sgu_norm": nothing, "sgu_turn": sgu_turn,
                "sgu_mix": nothing, "pool": nothing, "su": su, "conv_norm": conv_norm, "route": route,
                "place": nothing, "gather": gather, "turn_place": turn_place, "e_gate": e_gate,
                "e_up": nothing, "e_turn": e_turn, "e_down": nothing,
                "scatter": scatter, "experts_done": nothing, "peels": False})

        @block.vector
        def _(dve):
            TT, TS, STT, copy = (nc.vector.tensor_tensor, nc.vector.tensor_scalar,
                                 nc.vector.scalar_tensor_tensor, nc.vector.tensor_copy)
            MUL, ADD, SUB = ALU.mult, ALU.add, ALU.subtract
            ch = Chain(dve, "vchain")

            def split(at):
                dve.wait_ge(s["hi_ready"], at.u + 1)
                TT(wlo[:, at.slot, :], raw[:, at.slot, :], whi[:, at.slot, :].bitcast(F32),
                   SUB).then_inc(s["lo_ready"], 1)

            def rest(dst, src, hi, ready, count, done):
                dve.wait_ge(s[ready], count)
                TT(dst, src, hi.bitcast(F32), SUB).then_inc(s[done], 1)

            def mix_rest(order, b, src):
                rest(mlo[:, b, :], src, mhi[:, b, :], "mhi_ready", order + 1, "mlo_ready")

            def taps(dst, src, w):
                ch.link(STT(dst[:, 1:T], src[:, 0:T - 1], w(0), dst[:, 1:T], MUL, ADD))
                return STT(dst[:, 0:T - 1], src[:, 1:T], w(2), dst[:, 0:T - 1], MUL, ADD)

            def norm(m, eps, how):
                dve.wait_ge(s["ssq_ready"], m + 1)
                TS(row1[:, :], bank[0][:, 0, :], 1.0 / D, eps, MUL, ADD).then_inc(s["var_ready"], 1)
                dve.wait_ge(s["root_ready"], m + 1)
                ch.link(nc.vector.reciprocal(rstd[:, :], row1[:, :]))
                for k in range(KB):
                    dst = h if how == "plain" else nf
                    ins = STT(dst[:, k, :], h[:, k, :], gain(m, k), rstd[:, :], MUL, MUL)
                    if how == "plain":
                        if k % 2:
                            ins.then_inc(s["h_ready"], 1)
                    elif how == "last":
                        ins.then_inc(s["fin_ready"], 1)
                    else:
                        if how in ("shift", "whole"):
                            ch.link(ins)
                            ins = TS(nf[:, k, :], nf[:, k, :], shift(m, k), None, ADD)
                        ins.then_inc(s["n_ready"], 1)
                        if k and how != "whole":
                            norm_rest(m, k - 1)
                if how in ("first", "split", "shift"):
                    norm_rest(m, KB - 1)

            def norm_rest(m, k):
                rest(nlo[:, k, :], nf[:, k, :], nhi[:, k, :], "nhi_ready", KB * SPLIT_BEFORE[m] + k + 1, "nlo_ready")

            def xbc(at, l, k, b):
                dve.wait_ge(s["xlin_ready"], 16 * l + k + 1)
                taps(ring[:, k % 2, :], at.bank[:, 0, :],
                     lambda t: col(f"xw{l}", 3 * b + t)).then_inc(s["psum_free"], 1)

            def dt(l):
                a, x, nx, e, u, lnu, ea, t, r, d = (sml[:, k, :] for k in (0, 1, 2, 3, 4, 5, 7, 8, 9, 10))
                dve.wait_ge(s["dt_ready"], l + 1)
                for c in range(2):
                    w = slice(32 * c, 32 * c + 32)
                    ins = TT(x[:, w], bank[0][:, 0, w], cols(f"dtb{l}"), ADD)
                ch.link(ins)
                STT(nx, x, -1.0, x, MUL, ALU.min).then_inc(s["dtv_ready"], 1)
                dve.wait_ge(s["dta_ready"], 3 * l + 1)
                TS(u, e, 1.0, None, ADD).then_inc(s["dtv_ready"], 1)
                dve.wait_ge(s["dtv_ready"], 2 * l + 2)
                ch.link(TS(t, u, -1.0, 1.0, MUL, ADD))
                TT(t, t, e, ADD)
                ch.link(nc.vector.reciprocal(r, u))
                ch.link(TT(t, t, r, MUL))
                dve.wait_ge(s["dta_ready"], 3 * l + 3)
                ch.link(STT(d, x, 0.0, lnu, ALU.max, ADD))
                ch.link(TT(d, d, t, ADD))
                for c in range(2):
                    w = slice(32 * c, 32 * c + 32)
                    ins = STT(a[:, w], d[:, w], -1.0, ea[:, 0:32], MUL, MUL)
                ins.then_inc(s["a_ready"], 1)
                dve.wait_ge(s["cum_ready"], l + 1)
                TS(nF[:, :, :].rearrange("p c h -> p (c h)"), bank[1][:, 0, 0:64], -1.0, None,
                   MUL).then_inc(s["cumv_ready"], 1)
                copy(rowF[:, 0, :], bank[2][0:16, 0, :]).then_inc(s["cumv_ready"], 1)
                copy(rowF[:, 1, :], bank[3][0:16, 0, :]).then_inc(s["cumv_ready"], 1)

            def ssd_scores(l, j):
                g, it = j // 2, 8 * l + j
                triu, tril = col("triu", 0, P), cols("tril")
                if j % 2 == 0:
                    sc = bank[2][:, :, :].rearrange("p c (b t) -> p (c b) t", b=2)
                    dve.wait_ge(s["score_ready"], 4 * l + g + 1)
                    TT(s6[:, 0, :], sc[:, 0, :], triu, MUL)
                    copy(s6[:, 1:3, :], sc[:, 1:3, :])
                    TT(s6[:, 3, :], sc[:, 3, :], tril, MUL)
                    TT(s6[:, 4, :], sc[:, 0, :], tril, MUL)
                    TT(s6[:, 5, :], sc[:, 3, :], triu, MUL).then_inc(s["s6_ready"], 1)
                    dve.wait_ge(s["s6_ready"], 4 * l + g + 1)
                parts = ((0, 2, 0, 0, 0), (2, 4, 1, 1, 0), (4, 5, 0, 1, 0), (5, 6, 1, 0, HALF))
                dts = sml[:, 10, :].rearrange("p (c h) -> p c h", c=2)
                for r in range(2):
                    hd = 2 * j + r
                    dve.wait_ge(s["bc_ready"], 2 * it + r + 1)
                    if it:
                        dve.wait_ge(s["prod_ready"], 2 * it + r - 1)
                    for a, b, c, d, t in parts:
                        ins = TS(dec[:, r, a:b, :].rearrange("p a b -> p (a b)"),
                                 bank[r][:, d, t:t + HALF * (b - a)], nF[:, c, 16 * d + hd:16 * d + hd + 1],
                                 0.0, ADD, ALU.min)
                    ins.then_inc(s["clamp_ready"], 1)
                for r in range(2):
                    hd = 2 * j + r
                    dve.wait_ge(s["dec_ready"], 2 * it + r + 1)
                    for a, b, c, d, t in parts:
                        ins = STT(prod[:, r, a:b, :], dec[:, r, a:b, :], dts[:, c, 16 * d + hd:16 * d + hd + 1],
                                  s6[:, a:b, :], MUL, MUL)
                    ch.link(ins)
                    TT(prod[:, r, 0:4:3, :], prod[:, r, 0:4:3, :], prod[:, r, 4:6, :], ADD).then_inc(s["prod_ready"], 1)

            def ssd_out(l, j):
                it = 8 * l + j
                mix_rest(16 * l + j, 8 + j, short_m[:, j % 2, :])
                dve.wait_ge(s["y_ready"], it + 1)
                STT(y1[:, j, :], xs[:, j, :], col(f"skip{l}", j), bank[3][:, 0, :], MUL, ADD).then_inc(s["y1_ready"], 1)

            def sc_c(at, l, j):
                dve.wait_ge(s["unit_done"], at.u + 1)
                copy(short_c, at.bank[:, 0, :]).then_inc(s["psum_free"], 1)

            def sc_v(at, l, j):
                dve.wait_ge(s["unit_done"], at.u + 1)
                dve.wait_ge(s["psum_free"], at.n)
                TT(short_p, short_c, at.bank[:, 0, :], MUL).then_inc(s["psum_free"], 1)

            def sc_b(at, l, j):
                dve.wait_ge(s["scq_ready"], 8 * l + j + 1)
                ch.link(taps(short_q, short_p, lambda t: col(f"sw{l}", 3 * j + t)))
                dve.wait_ge(s["unit_done"], at.u + 1)
                TT(short_m[:, j % 2, :], short_q, at.bank[:, 0, :], MUL).then_inc(s["psum_free"], 1)

            def z(at, l, j):
                dve.wait_ge(s["zs_ready"], 8 * l + j + 1)
                if j == 0:
                    dve.wait_ge(s["y1_ready"], 8 * l + 8)
                TT(y1[:, j, :], y1[:, j, :], ring[:, j % 2, :], MUL).then_inc(s["psum_free"], 1)

            def group_norm(at, l):
                for q in range(2):
                    dve.wait_ge(s["gssq_ready"], 4 * l + 2 * q + 2)
                    TS(work[:, 2 * q:2 * q + 2, :], bank[4 + (at.cn + q) % 4][:, :, :], 4.0 / D, EPS1,
                       MUL, ADD).then_inc(s["psum_free"], 1)
                for q in range(2):
                    dve.wait_ge(s["groot_ready"], 2 * l + q + 1)
                    ins = nc.vector.reciprocal(work[:, 2 * q:2 * q + 2, :], work[:, 2 * q:2 * q + 2, :])
                ch.link(ins)
                for k in range(KB):
                    STT(y1[:, k, :], y1[:, k, :], col(f"gn{l}", k), work[:, k // 2, :],
                        MUL, MUL).then_inc(s["gy_ready"], 1)
                    if k:
                        mix_rest(16 * l + 7 + k, k - 1, y1[:, k - 1, :])
                mix_rest(16 * l + 15, KB - 1, y1[:, KB - 1, :])

            def residual(u, gate):
                dve.wait_ge(s["unit_done"], u)
                for k in range(KB):
                    if gate is None and k % 2:
                        TT(h[:, k - 1:k + 1, :], bank[k // 2][:, :, :], h[:, k - 1:k + 1, :],
                           ADD).then_inc(s["h_ready"], 1)
                    elif gate is not None:
                        ins = STT(h[:, k, :], bank[k // 2][:, k % 2, :], mod[:, gate + k:gate + k + 1],
                                  h[:, k, :], MUL, ADD)
                        if k % 2:
                            ins.then_inc(s["h_ready"], 1)

            def f_taps(at, l, dst, b):
                taps(dst[:, at.par, :], at.bank[:, 0, :],
                     lambda t: par[:, bass.ds(3 * b + (COLS[f"fw{l}"][0] + t), 1)]).then_inc(s["psum_free"], 1)

            def f_gate(at, l):
                dve.wait_ge(s["flin_ready"], 2 * at.j + 1)
                f_taps(at, l, fg, at.j - NFF * l)

            def f_up(at, l):
                dve.wait_ge(s["flin_ready"], 2 * at.j + 2)
                f_taps(at, l, fu, at.j + (NFF - NFF * l))
                dve.wait_ge(s["silu_ready"], at.j + 1)
                dve.wait_ge(s["psum_free"], at.n + 1)
                TT(fa[:, at.par, :], fs[:, at.par, :], fu[:, at.par, :], MUL).then_inc(s["hid_ready"], 1)

            def hid(at, l):
                rest(alo[:, at.par, :], fa[:, at.par, :], ahi[:, at.par, :], "ahi_ready", at.j + 1, "alo_ready")

            def d_up(at, l):
                dve.wait_ge(s["silu_ready"], at.j + 1)
                dve.wait_ge(s["unit_done"], at.u + 1)
                TT(fa[:, at.par, :], fs[:, at.par, :], at.bank[:, 0, :], MUL).then_inc(s["psum_free"], 2)

            def sv(at, l, b):
                if b == 0:
                    ch.link(nc.vector.memset(flat[:, 0:(CB + 1) * PADW], 0.0))
                dve.wait_ge(s["unit_done"], at.u + 1)
                copy(vv[:, b, :], at.bank[:, 0, :]).then_inc(s["psum_free"], 1)

            def squares(at, count, src):
                dve.wait_ge(s["sum_ready"], count)
                ch.link(TS(nmean, at.bank[:, 0, :], -1.0 / (CB * P), None, MUL))
                for b in range(CB):
                    TT(src[:, b, :], src[:, b, :], nmean, ADD).then_inc(s["cen_ready"], 1)
                dve.wait_ge(s["cssq_ready"], count)
                TS(row1[:, :], at.bank[:, 1, :], 1.0 / (CB * P), EPS2, MUL, ADD).then_inc(s["psum_free"], 1)
                dve.wait_ge(s["croot_ready"], count)
                ch.link(nc.vector.reciprocal(rstd[:, :], row1[:, :]))

            def sgu_norm(l):
                for b in range(CB):
                    last = STT(vv[:, b, :], vv[:, b, :], col(f"slg{l}", b), rstd[:, :], MUL, MUL)
                ch.link(last)
                for b in range(CB):
                    last = TS(vv[:, b, :], vv[:, b, :], col(f"slb{l}", b), None, ADD)
                last.then_inc(s["vn_ready"], 1)

            def cval(at, l, b):
                dve.wait_ge(s["gate_ready"], CB * l + b + 1)
                dve.wait_ge(s["unit_done"], at.u + 1)
                TT(glu[:, b, 15:15 + T], sgate[:, b % 2, :], at.bank[:, 0, :], MUL).then_inc(s["psum_free"], 2)
                dve.wait_ge(s["psum_free"], at.n + 1)
                ins = TS(cv[:, b, :], glu[:, b, 0:T], col(f"cw{l}", TAPS * b), col(f"cb{l}", b), MUL, ADD)
                for t in range(1, TAPS):
                    ch.link(ins)
                    ins = STT(cv[:, b, :], glu[:, b, t:t + T], col(f"cw{l}", TAPS * b + t), cv[:, b, :], MUL, ADD)
                if b == CB - 1:
                    ins.then_inc(s["conv_ready"], 1)
                    dve.wait_ge(s["conv_ready"], l + 1)
                else:
                    ch.link(ins)

            def pool(at, l, b):
                x, s2, s4, s8, d = (pl[:, k, :] for k in (0, 1, 2, 3, 4 + b))
                w = slice(16, 16 + T)
                dve.wait_ge(s["unit_done"], at.u + 1)
                if b:
                    dve.wait_ge(s["diff_ready"], 2 * l + b)
                copy(x[:, w], at.bank[:, 0, :]).then_inc(s["psum_free"], 1)
                dve.wait_ge(s["psum_free"], at.n + 1)
                ch.link(TT(s2[:, 1:PADW], x[:, 0:PADW - 1], x[:, 1:PADW], ADD))
                ch.link(TT(s4[:, 2:PADW - 1], s2[:, 1:PADW - 2], s2[:, 3:PADW], ADD))
                low, high = s2, s4
                if b:
                    ch.link(TT(s8[:, 4:PADW - 4], s4[:, 2:PADW - 6], s4[:, 6:PADW - 2], ADD))
                    ch.link(TT(s2[:, w], s8[:, 12:12 + T], s8[:, 20:20 + T], ADD))
                    low, high = s8, s2
                rc = col("rcount", T * b, T)
                TT(d[0:64, w], low[0:64, w], rc[0:64, :], MUL)
                ch.link(TT(d[64:128, w], high[64:128, w], rc[64:128, :], MUL))
                TT(d[:, w], d[:, w], x[:, w], SUB).then_inc(s["diff_ready"], 1)

            def su(at, l, b):
                if b == 0:
                    dve.wait_ge(s["smix_ready"], l + 1)
                    for o, mixed in enumerate((bank[1][:, 0, :], bank[1][:, 1, :], bank[2][:, 0, :])):
                        for c in range(2):
                            w = slice(HALF * c, HALF * c + HALF)
                            ins = TT(gated[:, o, w], mixed[:, w], col(f"sgub{l}", P * o, P), ADD)
                    ch.link(ins)
                dve.wait_ge(s["unit_done"], at.u + 1)
                TT(gated[:, b, :], gated[:, b, :], at.bank[:, 0, :], MUL).then_inc(s["psum_free"], 1)
                mix_rest(MIX2 + 8 * l + 2 * b, 5 + b, gated[:, b, :])
                if b < 2:
                    dve.wait_ge(s["pool_ready"], 2 * l + b + 1)
                    TS(pmix[:, b, :], bank[(3, 0)[b]][:, 0, :], col(f"pscale{l}", b), None, MUL).then_inc(s["poolv_ready"], 1)
                    mix_rest(MIX2 + 8 * l + 2 * b + 1, b, pmix[:, b, :])

            def conv_norm(l):
                for b in range(CB):
                    STT(cv[:, b, :], cv[:, b, :], col(f"clg{l}", b), rstd[:, :], MUL, MUL).then_inc(s["cn_ready"], 1)
                for b in range(CB):
                    mix_rest(MIX2 + 8 * l + 5 + b, 2 + b, cv[:, b, :])

            def wide(b):
                return bank[b][:, :, :].rearrange("p a t -> p (a t)")

            def route(n):
                lg, sub, ex, gt, eq, rk = (sml[:, k, :] for k in (1, 2, 3, 8, 9, 10))
                comb, sel, tab = sml[:, 6, :], sml[:, 11, 0:16], sml[:, 4, :]
                pos, cnt, over, before_me = sml[:, 5, 0:16], sml[:, 5, 16:24], sml[:, 5, 24:32], sml[:, 5, 32:40]
                g3, e3 = (a.rearrange("p (e j) -> p e j", e=NEXP) for a in (gt, eq))
                before = cols("before").rearrange("p (e j) -> p e j", e=NEXP)

                def across(a):
                    return a.rearrange("p (e j) -> p e j", e=1).to_broadcast([P, NEXP, NEXP])
                dve.wait_ge(s["logit_ready"], 1)
                for c in range(2):
                    w = slice(8 * c, 8 * c + 8)
                    ins = TT(lg[:, w], bank[7][:, 0, w], cols("rb"), ADD)
                ch.link(ins)
                for c in range(2):
                    w = slice(8 * c, 8 * c + 8)
                    own = lg[:, w].rearrange("p (e j) -> p e j", j=1).to_broadcast([P, NEXP, NEXP])
                    TT(g3, across(lg[:, w]), own, ALU.is_gt)
                    ch.link(TT(e3, across(lg[:, w]), own, ALU.is_equal))
                    ch.link(TT(e3, e3, before, MUL))
                    ch.link(TT(g3, g3, e3, ADD))
                    nc.vector.tensor_reduce(rk[:, w], g3, AX.X, ADD)
                    ch.link(nc.vector.tensor_reduce(rk[:, 16 + c:17 + c], lg[:, w], AX.X, ALU.max))
                    TS(sub[:, w], lg[:, w], rk[:, 16 + c:17 + c], None, SUB).then_inc(s["rsub_ready"], 1)
                TS(sel, rk[:, 0:16], 1.5, None, ALU.is_lt).then_inc(s["sel_ready"], 1)
                for b in range(4):
                    w = slice(GW * (b % 2), GW * (b % 2) + GW)
                    dve.wait_ge(s["xth_ready"], b + 1)
                    TT(xtl[:, b // 2, w], wide(b), xth[:, b // 2, w].bitcast(F32), SUB).then_inc(s["xtl_ready"], 1)
                dve.wait_ge(s["rexp_ready"], 1)
                dve.wait_ge(s["sel_ready"], 1)
                ch.link(TT(comb[:, 0:16], ex[:, 0:16], sel, MUL))
                for c in range(2):
                    ins = nc.vector.tensor_reduce(rk[:, 48 + c:49 + c], comb[:, 8 * c:8 * c + 8], AX.X, ADD)
                ch.link(ins)
                ch.link(nc.vector.reciprocal(rk[:, 50:52], rk[:, 48:50]))
                for c in range(2):
                    w = slice(8 * c, 8 * c + 8)
                    TS(comb[:, w], comb[:, w], rk[:, 50 + c:51 + c], None, MUL)
                dve.wait_ge(s["count_ready"], 1)
                ch.link(TT(pos, bank[7][:, 1, 0:16], sel, MUL))
                TS(pos, pos, -1.0, None, ADD)
                ch.link(TS(over, bank[7][:, 1, 16:24], CAP + 0.5, None, ALU.is_gt))
                ch.link(TT(e3, across(over), before, MUL))
                ch.link(nc.vector.tensor_reduce(before_me, e3, AX.X, ADD))
                ch.link(nc.vector.memset(tab[:, 0:16], 0.0))
                copy(tab[:, 0:NEXP], col("iota", 0, NEXP))
                for x in range(MORE):
                    ch.link(TS(cnt, before_me, float(x), None, ALU.is_equal))
                    ch.link(TT(cnt, cnt, over, MUL))
                    ch.link(TT(cnt, cnt, col("iota", 0, NEXP), MUL))
                    ch.link(nc.vector.tensor_reduce(tab[:, NEXP + x:NEXP + x + 1], cnt, AX.X, ADD))
                ch.link(nc.vector.tensor_reduce(tab[:, 15:16], over, AX.X, ADD))
                ch.link(TS(tab[:, 15:16], tab[:, 15:16], float(NEXP), None, ADD))
                copy(itab[:, :], tab[:, 0:16]).then_inc(s["tab_ready"], 1)
                dve.wait_ge(s["xtl_ready"], 4)
                dve.wait_ge(s["tab_ready"], 1)
                nc.vector.memset(token[:, :], 0.0).then_inc(s["hadd_ready"], 1)

            def place_tokens(q):
                e = dve.value_load(itab[0:1, bass.ds(q, 1)], min_val=0, max_val=NEXP - 1)
                off = col("offset", 0, 16)[:, bass.ds(q, 1)]
                for c in range(2):
                    pos = sml[:, 5, bass.ds(e + 8 * c, 1)]
                    ins = TS(place[:, c, :], cols("iota"), off, pos, ADD, ALU.is_equal)
                ins.then_inc(s["place_ready"], 1)
                dve.wait_ge(s["place_ready"], 2 * q + 1)
                for c in range(2):
                    ins = TS(wplace[:, c, :], place[:, c, :].bitcast(F32), sml[:, 6, bass.ds(e + 8 * c, 1)], None, MUL)
                ins.then_inc(s["place_ready"], 1)

            def gather(q):
                dve.wait_ge(s["xg_ready"], 2 * q + 2)
                for b in range(2):
                    last = copy(xgl[:, 4 * b:4 * b + 4, :].rearrange("p k t -> p (k t)"), wide(4 + b))
                last.then_inc(s["xgl_ready"], 1)

            def e_up(at, k, t):
                if k == 3:
                    dve.wait_ge(s["silu_ready"], 3 * NFF + 1 + t)
                    dve.wait_ge(s["unit_done"], at.u + 1)
                    TT(eh.rearrange("p k t -> p (k t)"), es, wide(5), MUL).then_inc(s["hid_ready"], 1)

            def e_turn(t):
                dve.wait_ge(s["ahi_ready"], 3 * NFF + 1 + t)
                TT(htl.rearrange("p k t -> p (k t)"), wide(6), hth.rearrange("p k t -> p (k t)").bitcast(F32),
                   SUB).then_inc(s["alo_ready"], 1)

            def scatter(q, u):
                dve.wait_ge(s["ys_ready"], q + 1)
                gate = 48 * (DEPTH - 1) + 40
                for k in range(KB):
                    last = STT(h[:, k, :], bank[(2, 3, 6, 7)[k // 2]][:, k % 2, :], mod[:, gate + k:gate + k + 1],
                               h[:, k, :], MUL, ADD)
                last.then_inc(s["hadd_ready"], 1)

            def experts_done(passes):
                dve.wait_ge(s["hadd_ready"], passes + 1)
                nc.vector.memset(token[:, :], 0.0).then_inc(s["h_ready"], 4)

            dve.wait_ge(s["cond_ready"], 1)
            with dve.Fori(0, ADA // (3 * KB)) as i:
                for g in range(3):
                    for k in range(KB):
                        n = KB * g + k
                        w = adaring[:, n // 2 % PAIRS, UW * (n % 2):UW * (n % 2) + UW]
                        if n % 2 == 0:
                            dve.wait_ge(ada_in[n // 2 % PAIRS], 64 * i + 16 * (n // SLOTS) + 16)
                        if k == 0:
                            dve.wait_ge(s["ada_done"], 3 * i + (g + 1))
                            ins = TS(adasum[:, g, :], w, cond[:, 0:1], None, MUL)
                        else:
                            dve.wait_ge(s["ada_used"], 3 * KB * i + n)
                            ins = STT(adasum[:, g, :], w, cond[:, k:k + 1], adasum[:, g, :], MUL, ADD)
                        ins.then_inc(s["ada_used"], 1)
            dve.wait_ge(s["par_in"], 16)
            dve.wait_ge(s["ada_done"], ADA // KB + 3)
            for l in range(DEPTH):
                ins = TT(mod[:, 48 * l:48 * l + 48], bank[7][:, 0, 48 * l:48 * l + 48], cols(f"adab{l}"), ADD)
            ch.link(ins)
            for l in range(DEPTH):
                for t, name in enumerate(("mixg", "ffng")):
                    a = 48 * l + 24 * t + 8
                    ins = STT(modg[:, 2 * l + t, :], mod[:, a:a + 8], 1.0, cols(f"{name}{l}"), ADD, MUL)
            ins.then_inc(s["mod_ready"], 1)
            walk(dve, split, {
                "norm": norm, "xbc": xbc, "dt": dt, "xbc_last": nothing, "sc_c": sc_c, "sc_v": sc_v,
                "sc_b": sc_b, "z": z, "ssd_scores": ssd_scores, "ssd_out": ssd_out, "mixdown": nothing,
                "group_norm": group_norm, "residual": residual, "f_gate": f_gate, "f_up": f_up, "f_hid": hid,
                "d_gate": nothing, "d_up": d_up, "d_hid": hid, "down": nothing, "sv": sv,
                "cgate": nothing, "cval": cval, "sums": nothing, "squares": squares,
                "sgu_norm": sgu_norm, "sgu_turn": nothing, "sgu_mix": nothing, "pool": pool, "su": su,
                "conv_norm": conv_norm, "route": route, "place": place_tokens, "gather": gather,
                "turn_place": nothing, "e_gate": nothing, "e_up": e_up,
                "e_turn": e_turn, "e_down": nothing, "scatter": scatter, "experts_done": experts_done,
                "peels": False}, ch)


def _up(w):
    k, n = w.shape
    return w.reshape(k // P, P, n // P, P).transpose(2, 1, 0, 3).reshape(n // P, P, UW)


def _down(w):
    return w.reshape(-1, P, UW)


def _hidden(units, gate, up, down):
    g, u, d = _up(gate), _up(up), _down(down)
    for j in range(len(g)):
        units += [g[j], u[j]] + ([d[j - 1]] if j else [])
    units.append(d[-1])


def _stream(i):
    units = []
    for l in range(DEPTH):
        w = i["w_in"][l]
        xbc, short = _up(w[:, 1024:3072]), [_up(w[:, a:a + D]) for a in (4128, 5152, 3104)]
        units += [xbc[b] for b in [8, 9, 10, 11, 12, 13, 14, 15, 0, 1, 2, 3, 4, 5, 6, 7]]
        units += [short[t][j] for j in range(KB) for t in range(3)]
        units += list(_up(w[:, 0:D]))
        wo = _down(i["w_out"][l])
        units += [wo[(k + 8) % 16] for k in range(16)]
        f = i["w_ffn_up"][l]
        _hidden(units, f[:, 0:NFF * P], f[:, NFF * P:], i["w_ffn_down"][l])
    for l in range(DEPTH):
        w = _up(i["w_in_2"][l])
        order = [11, 12, 13, 5, 2, 6, 3, 7, 4, 0, 1, 8, 9, 10]
        units += [w[b] for b in order]
        wo = _down(i["w_out_2"][l])
        units += [wo[b] for b in [5, 0, 6, 1, 7, 2, 3, 4]]
        if l == 0:
            _hidden(units, i["ffn_w_gate_2"][0], i["ffn_w_up_2"][0], i["ffn_w_down_2"][0])
        else:
            for e in range(NEXP):
                g, u = (i[name][0, e].reshape(4, 2, P, GROUPS, GW).transpose(3, 0, 2, 1, 4)
                        .reshape(GROUPS, 4, P, UW) for name in ("moe_w_gate_2", "moe_w_up_2"))
                d = _down(i["moe_w_down_2"][0, e]).reshape(GROUPS, 4, P, UW)
                for k in range(GROUPS):
                    units += [*g[k], *u[k]] + ([*d[k - 1]] if k else [])
                units += [*d[-1]]
    assert len(units) == UNITS
    out = np.empty((UNITS // 2, P, 2 * UW), np.float32)
    for n, a in enumerate(units):
        out[n // 2, :, UW * (n % 2):UW * (n % 2) + UW] = a
    return out


def _params(i):
    par = np.zeros((P, NCOLS), np.float32)

    def put(name, a, rows=P):
        at, width = COLS[name]
        par[0:rows, at:at + width] = a

    def feat(v):
        v = np.asarray(v)
        v = v.reshape(-1, v.shape[-1] // P, P)
        return v.transpose(2, 1, 0).reshape(P, -1)

    def all_rows(v):
        return np.broadcast_to(np.asarray(v).reshape(1, -1), (P, np.size(v)))

    for l in range(DEPTH):
        put(f"norm1{l}", feat(i["norm1_w"][l]))
        put(f"norm2{l}", feat(i["norm2_w"][l]))
        put(f"xw{l}", feat(i["conv_xbc_w"][l]))
        put(f"xb{l}", feat(i["conv_xbc_b"][l]))
        put(f"sw{l}", feat(i["sc_conv_w"][l]))
        put(f"gn{l}", feat(i["ssd_norm_w"][l]))
        put(f"skip{l}", feat(np.repeat(i["d_skip"][l], 64)))
        put(f"fw{l}", feat(i["ffn_conv_w"][l]))
        put(f"fb{l}", feat(i["ffn_conv_b"][l]))
        put(f"dtb{l}", all_rows(np.concatenate([i["dt_bias_f"][l], i["dt_bias_b"][l]])))
        put(f"alog{l}", all_rows(np.concatenate([i["a_log_f"][l], i["a_log_b"][l]])))
        wdt = i["w_in"][l][:, 3072:3104]
        put(f"wdt{l}", wdt.reshape(KB, P, 32).transpose(1, 0, 2).reshape(P, -1))
        put(f"mixg{l}", feat(i["mix_norm_g_2"][l]))
        put(f"ffng{l}", feat(i["ffn_norm_g_2"][l]))
        put(f"pscale{l}", feat(i["pool_scale_2"][l]))
        put(f"cw{l}", feat(i["conv_w_2"][l]))
        for name, key in (("cb", "conv_b_2"), ("clg", "conv_ln_g_2"), ("clb", "conv_ln_b_2"),
                          ("slg", "sgu_ln_g_2"), ("slb", "sgu_ln_b_2"), ("adab", "ada_b_2")):
            put(f"{name}{l}", feat(i[key][l]))
        pw = np.zeros((P, 2, P), np.float32)
        for g in range(4):
            r = slice(64 * (g % 2), 64 * (g % 2) + 64)
            pw[r, g // 2, r] = i["pool_w_2"][l][g]
        put(f"pw{l}", pw.reshape(P, -1))
        put(f"sguw{l}", i["sgu_w_2"][l].transpose(2, 0, 1).reshape(P, -1))
        b = i["sgu_b_2"][l].reshape(CB, 2, P)
        put(f"sgub{l}", np.repeat(b, 64, axis=1).transpose(1, 0, 2).reshape(P, -1))
    put("final1", feat(i["final_norm_w"]))
    put("final2", feat(i["final_norm_g_2"]))
    put("cond", feat(i["c_2"][0]))
    put("rw", i["router_w_2"][0].reshape(KB, P, NEXP).transpose(1, 0, 2).reshape(P, -1))
    put("rb", all_rows(i["router_b_2"][0]))
    put("ident", np.eye(P))
    put("ones", 1.0)
    put("triu", np.triu(np.ones((P, P))))
    put("tril", np.tril(np.ones((P, P))))
    t = np.arange(T)
    rc = np.zeros((P, 2, T))
    for g, w in enumerate((2, 4, 8, 16)):
        count = np.clip(t + w // 2, 0, T) - np.clip(t - w // 2, 0, T)
        rc[64 * (g % 2):64 * (g % 2) + 64, g // 2, :] = 1.0 / count
    put("rcount", rc.reshape(P, -1))
    e = np.arange(NEXP)
    put("before", all_rows((e[None, :] < e[:, None]).astype(np.float32)))
    put("iota", np.arange(P))
    put("offset", np.where(np.arange(16) < NEXP, 0.0, CAP))
    return par


def kernel(**inputs):
    import concourse.bacc as bacc
    from concourse.bass_utils import run_bass_kernel_spmd as run

    i = {k: np.asarray(v) for k, v in inputs.items()}
    ada = i["ada_w_2"].reshape(DEPTH, KB, P, 6, UW).transpose(0, 3, 1, 2, 4).reshape(ADA, P, UW)
    arrays = {
        "weights": _stream(i),
        "ada": np.ascontiguousarray(ada.reshape(ADA // 2, 2, P, UW).transpose(0, 2, 1, 3)).reshape(ADA // 2, P, 2 * UW),
        "x_t": np.ascontiguousarray(i["x"][0].T.reshape(KB, P, T).transpose(1, 0, 2)).reshape(P, KB * T),
        "params": _params(i),
    }
    nc = bacc.Bacc("TRN2", target_bir_lowering=False, num_devices=1)
    args = [nc.dram_tensor(name, a.shape, F32, kind="ExternalInput").ap() for name, a in arrays.items()]
    out = nc.dram_tensor("out_t", (P, KB * T), F32, kind="ExternalOutput").ap()
    build(nc, *args, out)
    r = run(nc, [arrays], core_ids=[0])
    got = r.results[0]["out_t"].reshape(P, KB, T)
    return got.transpose(2, 1, 0).reshape(1, T, D)
```

```python
from contextlib import ExitStack

import numpy as np

import concourse.bass as bass
from concourse import mybir

F32, F32R = mybir.dt.float32, mybir.dt.float32r
ACT, ALU = mybir.ActivationFunctionType, mybir.AluOpType
AX = mybir.AxisListType

P = 128
T = 256
D = 1024
KB = D // P
DEPTH = 2
HALF = T // 2
HEADS = 16
XBC = 16
NFF = 2816 // P
NEXP = 8
NFE = 3584 // P
GW = 512
GROUPS = NFE * P // GW
GU = 12 * GROUPS
CAP = P
MORE = 3
TAPS = 31
PE_TAPS = 14
CB = 3
UW = KB * P
SLOTS = 6
PAIRS = SLOTS // 2
TURNS = GU // SLOTS
LEAD = 4
ADA = DEPTH * 48
WINDOWS = 3
WIN = ADA // WINDOWS
ASLOTS = 4
DENSE = DEPTH * (48 + 16 + 3 * NFF) + DEPTH * (14 + 8) + 3 * NFF
UNITS = DENSE + NEXP * GU
EPS1, EPS2 = 1e-5, 1e-6

COLS = {}


def _columns():
    at = 0

    def add(name, width):
        nonlocal at
        COLS[name] = (at, width)
        at += width
    add("ones", P)
    add("eps", 2)
    for l in range(DEPTH):
        for name, width in (("norm1", 8), ("norm2", 8), ("xw", 3 * XBC), ("xb", XBC), ("sw", 3 * 8),
                            ("gn", 8), ("skip", 8), ("fw", 3 * 2 * NFF), ("fb", 2 * NFF),
                            ("dtb", 32), ("alog", 32), ("wdt", KB * 32)):
            add(f"{name}{l}", width)
        for name, width in (("mixg", 8), ("ffng", 8), ("pscale", 2), ("cw", CB * TAPS), ("cb", CB),
                            ("clg", CB), ("clb", CB), ("slg", CB), ("slb", CB),
                            ("pw", 2 * P), ("sguw", 6 * P), ("sgub", CB * P)):
            add(f"{name}{l}", width)
    for name, width in (("adab", ADA), ("final1", 8), ("final2", 8), ("rw", 64), ("rb", 8), ("ident", P),
                        ("triu", P), ("tril", P), ("rcount", 2 * T), ("before", 64),
                        ("iota", P), ("offset", 16)):
        add(name, width)
    return at


NCOLS = _columns()
EARLY = COLS["sw0"][0]


def build(nc, w_hbm, ada_hbm, cond_hbm, x_hbm, par_hbm, out_hbm):
    with ExitStack() as ctx:
        def sb(name, shape, dt=F32):
            return ctx.enter_context(nc.sbuf_tensor(name, shape, dt))

        def sem(name):
            return ctx.enter_context(nc.semaphore(name))

        par = sb("par", [P, NCOLS])
        raw = sb("raw", [P, SLOTS, UW])
        whi = sb("whi", [P, SLOTS, UW], F32R)
        wlo = sb("wlo", [P, SLOTS, UW], F32R)
        h = sb("h", [P, KB, T])
        nhi = sb("nhi", [P, KB, T], F32R)
        nlo = sb("nlo", [P, KB, T], F32R)
        mhi = sb("mhi", [P, 2 * KB, T], F32R)
        mlo = sb("mlo", [P, 2 * KB, T], F32R)
        area = sb("area", [P, 24, T])
        work = sb("work", [P, 15, T])
        ring = sb("ring", [P, 7, T])
        mod = sb("mod", [P, ADA])
        modg = sb("modg", [P, 4, KB])
        cond = sb("cond", [P, D])
        sml = sb("sml", [P, 12, 64])
        tokF = sb("tokF", [P, 2, 32])
        itab = sb("itab", [P, 16], mybir.dt.int32)
        rows = sb("rows", [P, 2, T])
        row1, rstd = rows[:, 0, :], rows[:, 1, :]
        rowF = rows[0:HEADS, :, :]
        token = sb("token", [P, 1])
        bank = [ctx.enter_context(nc.psum_tensor(f"bank{b}", [P, 2, T], F32)) for b in range(8)]

        def cols(name):
            a, width = COLS[name]
            return par[:, a:a + width]

        def col(name, k=0, width=1):
            a = COLS[name][0] + k
            return par[:, a:a + width]

        def spreader(rows, k):
            a = COLS["ident"][0] + k
            return par[0:rows, a:a + 1].to_broadcast([rows, P])

        def halves(a, n):
            return a.rearrange("p a t -> p (a t)").rearrange("p (k t) -> p k t", k=n)

        xs, Bt, Ct, nf = area[:, 0:8, :], area[:, 8:12, :], area[:, 12:16, :], area[:, 16:24, :]
        adaring = [halves(area[:, a:a + 4, :], 1)[:, 0, :] for a in (8, 12, 16, 20)]
        y1 = nf
        fg, fu, fs, fa = (area[:, 2 * a:2 * a + 2, :] for a in range(4))
        xgh, xgl = halves(mhi[:, 0:4, :], KB), halves(mlo[:, 0:4, :], KB)
        hth, htl = halves(mhi[:, 4:6, :], 4), halves(mlo[:, 4:6, :], 4)
        place = halves(mhi[:, 6:7, :], 2)
        xth, xtl = halves(nhi[:, :, :], 2), halves(nlo[:, :, :], 2)
        wplace, wplace_t, yg = halves(work[:, 0:1, :], 2), work[:, 1, :], halves(work[:, 2:6, :], 2)
        es, eh = halves(area[:, 0:2, :], 1)[:, 0, :], halves(area[:, 2:4, :], 4)
        ahi, alo = mhi[:, 0:2, :], mlo[:, 0:2, :]
        dec = work[:, 0:6, :].rearrange("p (r a) (b c) -> p r (a b) c", r=2, b=2)
        prod = work[:, 6:12, :].rearrange("p (r a) (b c) -> p r (a b) c", r=2, b=2)
        s6 = work[:, 12:15, :].rearrange("p a (b c) -> p (a b) c", b=2)
        xtok = ring[:, 0:2, :].rearrange("p r (c x) -> p r c x", c=2)
        short_c, short_p, short_q, short_m = ring[:, 2, :], ring[:, 3, :], ring[:, 4, :], ring[:, 5:7, :]
        PADW = T + 32
        flat = area[:, 0:11, :].rearrange("p a t -> p (a t)")
        glu = flat[:, 0:CB * PADW].rearrange("p (b t) -> p b t", b=CB)
        pl = flat[:, CB * PADW:(CB + 6) * PADW].rearrange("p (b t) -> p b t", b=6)
        cv, pmix = area[:, 11:14, :], area[:, 14:16, :]
        diag = [halves(a[:, 0:PE_TAPS // 2, :], PE_TAPS) for a in (nf, ring, nf)]
        vtok = work[:, 0:3, :].rearrange("p a t -> p (a t)").rearrange("p (c x) -> p c x", c=2)
        gated, sq3, sgate, nmean, vv = (work[:, 3:6, :], work[:, 6:9, :], work[:, 9:11, :],
                                        work[:, 11, :], work[:, 12:15, :])

        s = {}
        for name in """par_in late_in x_in cond_in cond_ready ada_used hi_ready lo_ready unit_done bank_done psum_free
                h_ready sq_ready ssq_ready root_ready n_ready nhi_ready nlo_ready fin_ready
                flin_ready silu_ready hid_ready ahi_ready alo_ready
                xlin_ready xbc_ready dt_ready dtv_ready dta_ready a_ready cum_ready cumv_ready
                score_ready s6_ready bc_ready clamp_ready xtp_ready xtok_ready dec_ready prod_ready y_ready y1_ready
                shortc_ready scq_ready mhi_ready mlo_ready zs_ready ysq_ready gssq_ready groot_ready gy_ready
                gate_ready sum_ready cen_ready csq_ready cssq_ready croot_ready cn_ready
                cs_ready vn_ready vtp_ready vtok_ready smix_ready diff_ready diag_ready taps_ready taps_added
                pool_ready poolv_ready
                logit_ready rsub_ready rexp_ready sel_ready count_ready tab_ready xt_ready xth_ready
                xtl_ready place_ready xg_ready xgh_ready xgl_ready wpt_ready wptv_ready ht_ready
                yg_ready ys_ready hadd_ready
                out_stored""".split():
            s[name] = sem(name)
        loaded = [sem(f"loaded{k}") for k in range(PAIRS)]
        ada_in = [sem(f"ada_in{k}") for k in range(ASLOTS)]
        block = ctx.enter_context(nc.Block())

        class At:

            def __init__(self, u, n, j, i=0):
                self.cu, self.cn, self.cj, self.i = u, n, j, i
                self.u, self.n, self.j = u + 6 * i, n + 4 * i, j + 2 * i
                self.slot, self.bank, self.par = u % SLOTS, bank[4 + n % 4], j % 2

            def ahead(self, k):
                return At(self.cu + k, self.cn, self.cj, self.i)

        class Chain:

            def __init__(self, eng, name):
                self.eng, self.sem, self.n, self.i, self.step = eng, sem(name), 0, 0, 0

            def mark(self, ins):
                ins.then_inc(self.sem, 1)
                self.n += 1

            def wait(self):
                self.eng.wait_ge(self.sem, self.n + self.step * self.i)

            def link(self, ins):
                self.mark(ins)
                self.wait()

        XBC_ORDER = [8, 9, 10, 11, 12, 13, 14, 15, 0, 1, 2, 3, 4, 5, 6, 7]
        MIX1_ORDER = [(k + 8) % 16 for k in range(16)]
        MIX2_ORDER = [5, 0, 6, 1, 7, 2, 3, 4]
        MIX2 = 16 * DEPTH

        def walk(eng, split, do, chain=None):
            u = n = j = m = 0

            def unit(kind, at, *args):
                split(at.ahead(LEAD))
                do[kind](at, *args)

            def one(kind, *args):
                nonlocal u, n
                unit(kind, At(u, n, 0), *args)
                u, n = u + 1, n + (kind != "mixdown")

            def ffn(kind, count, l, links):
                nonlocal u, n, j

                def pair(i, w, modulate):
                    for k in range(2):
                        a, b, c = u + 3 * k, n + 2 * k, j + k
                        unit(kind + "_gate", At(a, b, c, i), l)
                        if modulate:
                            do["modulate"](w, i, 2 * k)
                        unit(kind + "_up", At(a + 1, b + 1, c, i), l)
                        if modulate:
                            do["modulate"](w, i, 2 * k + 1)
                        unit("down", At(a + 2, b + 2, c - 1, i), False, False)
                        do[kind + "_hid"](At(a + 2, b + 2, c, i), l)

                unit(kind + "_gate", At(u, n, j), l)
                unit(kind + "_up", At(u + 1, n + 1, j), l)
                do[kind + "_hid"](At(u + 2, n + 2, j), l)
                unit(kind + "_gate", At(u + 2, n + 2, j + 1), l)
                unit(kind + "_up", At(u + 3, n + 3, j + 1), l)
                unit("down", At(u + 4, n + 4, j), True, False)
                do[kind + "_hid"](At(u + 4, n + 4, j + 1), l)
                u, n, j = u + 5, n + 4, j + 2
                loops, n0 = (count - 2) // 2, chain and chain.n
                turns = WIN // ASLOTS
                ends = [0, turns, loops] if do["modulate"] is not nothing else [0, loops]
                for first, end in zip(ends, ends[1:]):
                    with eng.Fori(first, end) as i:
                        if chain is not None:
                            chain.i, chain.step, chain.n = i, links, n0
                        pair(i, l if kind == "f" else DEPTH, end == turns)
                if chain is not None:
                    assert chain.n - n0 == links
                    chain.n, chain.i = n0 + links * loops, 0
                u, n, j = u + 6 * loops, n + 4 * loops, j + 2 * loops
                unit("down", At(u, n, j - 1), False, True)
                u += 1

            for v in range(2):
                split(At(v, 0, 0))
            do["norm"](0, EPS1, "split")
            for v in range(2, LEAD):
                split(At(v, 0, 0))
            m = 1
            for l in range(DEPTH):
                for k, b in enumerate(XBC_ORDER):
                    one("xbc", l, k, b)
                    if k == 2:
                        do["dt"](l)
                    if k == 6:
                        do["cum"](l)
                do["xbc_last"](n, l)
                for t in range(KB):
                    one("sc_c", l, t)
                    do["ssd_scores"](l, t)
                    one("sc_v", l, t)
                    one("sc_b", l, t)
                    do["ssd_out"](l, t)
                for t in range(KB):
                    one("z", l, t)
                for k, b in enumerate(MIX1_ORDER):
                    one("mixdown", 16 * l + k, b, k == 0, k == 15)
                    if k == 0:
                        do["group_norm"](At(u, n, 0), l)
                        n += 2
                do["residual"](u, None)
                do["norm"](m, EPS1, "split")
                m += 1
                ffn("f", NFF, l, 4)
                do["residual"](u, None)
                if l < DEPTH - 1:
                    do["norm"](m, EPS1, "split")
                    m += 1
            do["norm"](m, EPS1, "plain")
            m += 1
            for l in range(DEPTH):
                do["norm"](m, EPS2, "shift")
                m += 1
                for b in range(CB):
                    one("sv", l, b)
                ln = At(u, n, 0)
                do["sums"](ln, 2 * l + 1, vv)
                n += 1
                one("cgate", l, 0)
                do["squares"](ln, 2 * l + 1, vv)
                do["sgu_norm"](l)
                one("cval", l, 0)
                do["sgu_turn"](l)
                glu_done = n
                one("cgate", l, 1)
                do["conv"](glu_done, l, 0)
                do["sgu_mix"](l)
                one("cval", l, 1)
                glu_done = n
                one("cgate", l, 2)
                do["conv"](glu_done, l, 1)
                one("cval", l, 2)
                glu_done = n
                one("pool", l, 0)
                do["conv"](glu_done, l, 2)
                one("pool", l, 1)
                do["conv_last"](l)
                for b in range(CB):
                    one("su", l, b)
                for k, b in enumerate(MIX2_ORDER):
                    one("mixdown", MIX2 + 8 * l + k, b, k == 0, k == 7)
                    if k == 0:
                        ln = At(u, n, 0)
                        do["sums"](ln, 2 * l + 2, cv)
                        n += 1
                    if k == 1:
                        do["squares"](ln, 2 * l + 2, cv)
                        do["conv_norm"](l)
                do["residual"](u, 48 * l + 16)
                if l < DEPTH - 1:
                    do["norm"](m, EPS2, "shift")
                    m += 1
                    ffn("d", NFF, l, 0)
                    do["residual"](u, 48 * l + 40)
            do["norm"](m, EPS2, "whole")
            m += 1
            assert u == DENSE, u

            def part(kind, v, i, *args):
                for k in range(4):
                    unit(kind, At(v + k, 0, 0, i), k, *args)

            def split_more(v, i):
                for k in range(LEAD, SLOTS):
                    split(At(v + k, 0, 0, i))

            def group(q, g, first):
                i, t = TURNS * q + 12 // SLOTS * (g - 1), GROUPS * q + g
                part("e_gate", u + 8, i, t)
                if first:
                    do["banks_free"](q)
                do["e_turn"](t - 1)
                part("e_up", u + 12, i, t)
                part("e_down", u + 16, i, t - 1, first)

            do["route"](n)
            do["place"](0)
            do["gather"](0)
            do["turn_place"](0)
            passes = eng.value_load(itab[0:1, 15:16], min_val=NEXP, max_val=NEXP + MORE)
            split_more(u, 0)
            with eng.Fori(0, passes) as q:
                for k in range(4):
                    at = At(u + k, 0, 0, TURNS * q)
                    if k >= SLOTS - LEAD:
                        split(at.ahead(LEAD))
                    do["e_gate"](at, k, GROUPS * q)
                part("e_up", u + 4, TURNS * q, GROUPS * q)
                do["place"](q + 1)
                if do["peels"]:
                    group(q, 1, True)
                    with eng.Fori(2, GROUPS) as g:
                        group(q, g, False)
                else:
                    with eng.Fori(1, GROUPS) as g:
                        group(q, g, False)
                do["e_turn"](GROUPS * q + (GROUPS - 1))
                do["gather"](q + 1)
                part("e_down", u + GU - 4, TURNS * q, GROUPS * q + (GROUPS - 1), False)
                do["scatter"](q, u)
                split_more(u + GU, TURNS * q)
                do["scatter_add"](q)
                do["turn_place"](q + 1)
            do["experts_done"](passes)
            do["norm"](m, EPS2, "last")

        OPENS = (1, 3, 6)
        WINDOW_OF = {2: 0, 4: 1, 7: 2}

        DECAYS = ((0, 2, 0, 0, 0), (2, 4, 1, 1, 0), (4, 5, 0, 1, 0), (5, 6, 1, 0, HALF))

        SPLIT_BEFORE = [0, 1, 2, 3, 4, 4, 5, 6, 7, 7]

        def gain(m, k):
            if m < 5:
                return col(("norm10", "norm20", "norm11", "norm21", "final1")[m], k)
            return col("final2", k) if m == 9 else modg[:, m - 5, k:k + 1]

        def shift(m, k):
            a = 48 * ((m - 5) // 2) + 24 * ((m - 5) % 2) + k
            return mod[:, a:a + 1]

        def epsilon(eps):
            return col("eps", (EPS1, EPS2).index(eps))

        def conv_bank(b):
            return bank[(0, 3, 0)[b]][:, b // 2, :]

        def nothing(*args):
            pass

        @block.sync
        def _(sp):
            def load(k, src):
                sp.dma_start(raw[:, 2 * k:2 * k + 2, :].rearrange("p a t -> p (a t)"), src).then_inc(loaded[k], 16)

            load(0, w_hbm[0])
            sp.dma_start(h[:, :, :].rearrange("p k t -> p (k t)"), x_hbm).then_inc(s["x_in"], 16)
            sp.dma_start(par[:, 0:EARLY], par_hbm[:, 0:EARLY]).then_inc(s["par_in"], 16)
            for k in range(1, PAIRS):
                load(k, w_hbm[k])
            sp.dma_start(par[:, EARLY:], par_hbm[:, EARLY:]).then_inc(s["late_in"], 16)
            pairs = DENSE // 2 + PAIRS
            turns = (pairs - PAIRS) // PAIRS
            with sp.Fori(0, turns) as i:
                for k in range(PAIRS):
                    src = w_hbm[PAIRS * i + (PAIRS + k)]
                    used = sp.snap(SLOTS * i + (2 * k + 2))
                    sp.wait_ge(s["lo_ready"], used)
                    load(k, src)
            for p in range(PAIRS * (turns + 1), pairs):
                sp.wait_ge(s["lo_ready"], 2 * (p - PAIRS) + 2)
                load(p % PAIRS, w_hbm[p])
            sp.wait_ge(s["tab_ready"], 1)
            passes = sp.value_load(itab[0:1, 15:16], min_val=NEXP, max_val=NEXP + MORE)
            with sp.Fori(0, passes) as q:
                own = sp.value_load(itab[0:1, bass.ds(q, 1)], min_val=0, max_val=NEXP - 1)
                following = sp.value_load(itab[0:1, bass.ds(q + 1, 1)], min_val=0, max_val=NEXP - 1)
                with sp.Fori(1, GU // SLOTS) as i:
                    for k in range(PAIRS):
                        src = w_hbm[own * (GU // 2) + (PAIRS * i + (DENSE // 2 + k))]
                        used = sp.snap(GU * q + (SLOTS * i + (DENSE - SLOTS + 2 * k + 2)))
                        sp.wait_ge(s["lo_ready"], used)
                        load((DENSE // 2 + k) % PAIRS, src)
                for k in range(PAIRS):
                    src = w_hbm[following * (GU // 2) + (DENSE // 2 + k)]
                    used = sp.snap(GU * q + (GU + DENSE - SLOTS + 2 * k + 2))
                    sp.wait_ge(s["lo_ready"], used)
                    load((DENSE // 2 + k) % PAIRS, src)
            sp.wait_ge(s["fin_ready"], KB)
            sp.dma_start(out_hbm, nf.rearrange("p k t -> p (k t)")).then_inc(s["out_stored"], 16)
            sp.wait_ge(s["out_stored"], 16)

        @block.tensor
        def _(pe):
            mm = nc.tensor.matmul
            fresh = [0]

            def three(out, slot, tile, xh, xl, start, stop):
                w = slice(tile * P, tile * P + P)
                mm(out, whi[:, slot, w], xh, start=start, stop=False, skip_group_check=True)
                mm(out, wlo[:, slot, w], xh, start=False, stop=False, skip_group_check=True)
                return mm(out, whi[:, slot, w], xl, start=False, stop=stop, skip_group_check=True)

            def up(at, *args):
                pe.wait_ge(s["lo_ready"], at.u + 1)
                if at.cn >= 4:
                    pe.wait_ge(s["psum_free"], at.n - 3)
                for k in range(KB):
                    if fresh[0]:
                        pe.wait_ge(s["nlo_ready"], KB * (fresh[0] - 1) + k + 1)
                    last = three(at.bank[:, 0, :], at.slot, k, nhi[:, k, :], nlo[:, k, :],
                                 k == 0, k == KB - 1)
                fresh[0] = 0
                last.then_inc(s["unit_done"], 1)

            def down_tiles(at, xh, xl, first, final):
                for o in range(KB):
                    last = three(bank[o // 2][:, o % 2, :], at.slot, o, xh, xl, first and o % 2 == 0, final)
                    if final and o in (1, 3, 5):
                        last.then_inc(s["bank_done"], 1)
                last.then_inc(s["unit_done"], 1)

            def mixdown(at, order, b, first, final):
                pe.wait_ge(s["lo_ready"], at.u + 1)
                pe.wait_ge(s["mlo_ready"], order + (4 if first and order >= MIX2 else 1))
                down_tiles(at, mhi[:, b, :], mlo[:, b, :], first, final)

            def down(at, first, final):
                pe.wait_ge(s["lo_ready"], at.u + 1)
                pe.wait_ge(s["alo_ready"], at.j + 1)
                down_tiles(at, ahi[:, at.par, :], alo[:, at.par, :], first, final)

            def norm(m, eps, how):
                for k in range(KB):
                    if k % 2 == 0:
                        pe.wait_ge(s["sq_ready"], 4 * m + k // 2 + 1)
                    last = mm(bank[0][:, 0, :], cols("ones"), nf[:, k, :], start=k == 0, stop=k == KB - 1)
                last.then_inc(s["ssq_ready"], 1)
                if how in ("split", "shift"):
                    fresh[0] = SPLIT_BEFORE[m] + 1

            def dt(l):
                if l == 0:
                    pe.wait_ge(s["late_in"], 16)
                for c in range(2):
                    for k in range(KB):
                        last = mm(bank[0][:, 0, 32 * c:32 * c + 32], nf[:, k, HALF * c:HALF * c + HALF],
                                  col(f"wdt{l}", 32 * k, 32), start=k == 0, stop=k == KB - 1)
                last.then_inc(s["dt_ready"], 1)

            def cum(l):
                pe.wait_ge(s["a_ready"], l + 1)
                a = sml[:, 0, :].rearrange("p (c h) -> p c h", c=2)
                triu, ones, tril = col("triu", 0, P), cols("ones"), cols("tril")
                o = bank[1][:, 0, 0:64].rearrange("p (c h) -> p c h", c=2)
                mm(o[:, 0, 0:16], triu, a[:, 0, 0:16], start=True, stop=True)
                mm(o[:, 0, 16:32], ones, a[:, 1, 16:32], start=True, stop=False)
                mm(o[:, 0, 16:32], tril, a[:, 0, 16:32], start=False, stop=True)
                mm(o[:, 1, 0:16], ones, a[:, 0, 0:16], start=True, stop=False)
                mm(o[:, 1, 0:16], triu, a[:, 1, 0:16], start=False, stop=True)
                mm(o[:, 1, 16:32], tril, a[:, 1, 16:32], start=True, stop=True)
                f, b = bank[2][0:16, 0, :], bank[3][0:16, 0, :]
                mm(f[:, 0:HALF], a[:, 0, 0:16], triu, start=True, stop=True)
                mm(f[:, HALF:T], a[:, 0, 0:16], ones, start=True, stop=False)
                mm(f[:, HALF:T], a[:, 1, 0:16], triu, start=False, stop=True)
                mm(b[:, 0:HALF], a[:, 1, 16:32], ones, start=True, stop=False)
                mm(b[:, 0:HALF], a[:, 0, 16:32], tril, start=False, stop=True)
                mm(b[:, HALF:T], a[:, 1, 16:32], tril, start=True, stop=True).then_inc(s["cum_ready"], 1)

            def ssd_scores(l, j):
                g, it = j // 2, 8 * l + j
                if j == 0:
                    pe.wait_ge(s["xbc_ready"], 16 * (l + 1))
                    pe.wait_ge(s["cumv_ready"], 3 * (l + 1))
                if j % 2 == 0:
                    if it:
                        pe.wait_ge(s["s6_ready"], 4 * l + g)
                    for c in range(2):
                        last = mm(bank[2][:, c, :], Bt[:, g, HALF * c:HALF * c + HALF], Ct[:, g, :],
                                  start=True, stop=True)
                    last.then_inc(s["score_ready"], 1)
                for r in range(2):
                    if it:
                        pe.wait_ge(s["clamp_ready"], 2 * it + r - 1)
                    for d in range(2):
                        last = mm(bank[r][:, d, :], spreader(16, 2 * j + r), rowF[:, d, :], start=True, stop=True)
                    last.then_inc(s["bc_ready"], 1)
                if it:
                    pe.wait_ge(s["xtok_ready"], it)
                    pe.wait_ge(s["y1_ready"], it)
                for c in range(2):
                    last = nc.tensor.transpose(bank[3][:, 1, HALF * c:HALF * c + HALF],
                                               xs[:, j, HALF * c:HALF * c + HALF], cols("ident"))
                last.then_inc(s["xtp_ready"], 1)

            def ssd_out(l, j):
                it = 8 * l + j
                pe.wait_ge(s["xtok_ready"], it + 1)
                for r in range(2):
                    pe.wait_ge(s["prod_ready"], 2 * it + r + 1)
                    for c in range(2):
                        last = mm(bank[3][64 * r:64 * r + 64, 0, :], xtok[:, it % 2, c, 64 * r:64 * r + 64],
                                  prod[:, r, 2 * c:2 * c + 2, :].rearrange("p a b -> p (a b)"),
                                  start=c == 0, stop=c == 1)
                last.then_inc(s["y_ready"], 1)

            def group_norm(at, l):
                for g in range(4):
                    if g % 2 == 0:
                        pe.wait_ge(s["psum_free"], at.n - 3 + g // 2)
                    pe.wait_ge(s["ysq_ready"], 8 * l + 2 * g + 2)
                    b = bank[4 + (at.cn + g // 2) % 4]
                    for k in range(2):
                        last = mm(b[:, g % 2, :], cols("ones"), xs[:, 2 * g + k, :], start=k == 0, stop=k == 1)
                    last.then_inc(s["gssq_ready"], 1)

            def sums(at, count, src):
                pe.wait_ge(s["psum_free"], at.n - 3)
                if count % 2:
                    pe.wait_ge(s["psum_free"], at.n)
                else:
                    pe.wait_ge(s["taps_added"], CB * (count // 2))
                for b in range(CB):
                    last = mm(at.bank[:, 0, :], cols("ones"), src[:, b, :], start=b == 0, stop=b == CB - 1)
                last.then_inc(s["sum_ready"], 1)

            def squares(at, count, src):
                pe.wait_ge(s["csq_ready"], count)
                for b in range(CB):
                    last = mm(at.bank[:, 1, :], cols("ones"), sq3[:, b, :], start=b == 0, stop=b == CB - 1)
                last.then_inc(s["cssq_ready"], 1)

            def sgu_turn(l):
                pe.wait_ge(s["vn_ready"], l + 1)
                for c in range(2):
                    out = bank[1 + c][:, :, :].rearrange("p a t -> p (a t)")
                    for b in range(CB):
                        last = nc.tensor.transpose(out[:, P * b:P * b + P], vv[:, b, HALF * c:HALF * c + HALF],
                                                   cols("ident"))
                    last.then_inc(s["vtp_ready"], 1)

            def sgu_mix(l):
                pe.wait_ge(s["vtok_ready"], 2 * (l + 1))
                for b in range(CB):
                    o = (bank[1][:, 0, :], bank[1][:, 1, :], bank[2][:, 0, :])[b]
                    for r in range(2):
                        hd = 2 * b + r
                        for c in range(2):
                            last = mm(o[64 * r:64 * r + 64, HALF * c:HALF * c + HALF],
                                      vtok[:, c, 64 * hd:64 * hd + 64], col(f"sguw{l}", P * hd, P),
                                      start=True, stop=True)
                last.then_inc(s["smix_ready"], 1)

            def conv(glu_done, l, b):
                pe.wait_ge(s["psum_free"], glu_done)
                pe.wait_ge(s["diag_ready"], CB * l + b + 1)
                if b == 2:
                    pe.wait_ge(s["taps_added"], CB * l + 1)
                for k in range(PE_TAPS):
                    t = TAPS - PE_TAPS + k
                    last = mm(conv_bank(b), diag[b][:, k, :], glu[:, b, t:t + T], start=k == 0, stop=k == PE_TAPS - 1)
                last.then_inc(s["taps_ready"], 1)

            def su(at, l, b):
                up(at)
                if b < 2:
                    pe.wait_ge(s["taps_added"], CB * l + b + 2)
                    pe.wait_ge(s["diff_ready"], 2 * l + b + 1)
                    mm(bank[(3, 0)[b]][:, 0, :], col(f"pw{l}", P * b, P), pl[:, 4 + b, 16:16 + T],
                       start=True, stop=True).then_inc(s["pool_ready"], 1)

            def wide(b):
                return bank[b][:, :, :].rearrange("p a t -> p (a t)")

            def route(n):
                pe.wait_ge(s["n_ready"], KB * 8)
                pe.wait_ge(s["psum_free"], n)
                for c in range(2):
                    for k in range(KB):
                        last = mm(bank[7][:, 0, 8 * c:8 * c + 8], nf[:, k, HALF * c:HALF * c + HALF],
                                  col("rw", 8 * k, 8), start=k == 0, stop=k == KB - 1)
                last.then_inc(s["logit_ready"], 1)
                for c in range(2):
                    for k in range(KB):
                        last = nc.tensor.transpose(wide(2 * c + k // 4)[:, P * (k % 4):P * (k % 4) + P],
                                                   nf[:, k, HALF * c:HALF * c + HALF], cols("ident"))
                        if k % 4 == 3:
                            last.then_inc(s["xt_ready"], 1)
                pe.wait_ge(s["sel_ready"], 1)
                sel, triu, ones = sml[:, 11, 0:16], col("triu", 0, P), cols("ones")
                o = bank[7][:, 1, :]
                mm(o[:, 0:8], triu, sel[:, 0:8], start=True, stop=True)
                mm(o[:, 8:16], ones, sel[:, 0:8], start=True, stop=False)
                mm(o[:, 8:16], triu, sel[:, 8:16], start=False, stop=True)
                mm(o[:, 16:24], ones, sel[:, 0:8], start=True, stop=False)
                mm(o[:, 16:24], ones, sel[:, 8:16], start=False, stop=True).then_inc(s["count_ready"], 1)
                pe.wait_ge(s["xtl_ready"], 4)
                pe.wait_ge(s["tab_ready"], 1)

            def moved(out, xh, xl, slot, w, start, stop):
                mm(out, xh, whi[:, slot, w], start=start, stop=False, skip_group_check=True)
                mm(out, xh, wlo[:, slot, w], start=False, stop=False, skip_group_check=True)
                return mm(out, xl, whi[:, slot, w], start=False, stop=stop, skip_group_check=True)

            def gather(q):
                pe.wait_ge(s["place_ready"], 2 * q + 1)
                for x, b in ((xth, 2), (xtl, 4)):
                    for k in range(KB):
                        for c in range(2):
                            last = mm(wide(b + k // 4)[:, P * (k % 4):P * (k % 4) + P],
                                      x[:, c, P * k:P * k + P], place[:, c, :], start=c == 0, stop=c == 1)
                    last.then_inc(s["xg_ready"], 1)

            def turn_place(q):
                pe.wait_ge(s["place_ready"], 2 * q + 2)
                for c in range(2):
                    last = nc.tensor.transpose(bank[0][:, 0, HALF * c:HALF * c + HALF], wplace[:, c, :], cols("ident"))
                last.then_inc(s["wpt_ready"], 1)
                pe.wait_ge(s["xgh_ready"], q + 1)
                pe.wait_ge(s["xgl_ready"], q + 1)

            def e_hidden(at, k, b):
                pe.wait_ge(s["lo_ready"], at.u + 1)
                for kk in range(2):
                    x = 2 * k + kk
                    last = moved(wide(b), xgh[:, x, :], xgl[:, x, :], at.slot, slice(GW * kk, GW * kk + GW),
                                 x == 0, x == KB - 1)
                last.then_inc(s["unit_done"], 1)

            def e_gate(at, k, t):
                if k == 0:
                    pe.wait_ge(s["silu_ready"], 3 * NFF + t)
                e_hidden(at, k, 4)

            def e_up(at, k, t):
                if k == 0:
                    pe.wait_ge(s["hid_ready"], 2 * NFF + t)
                e_hidden(at, k, 5)

            def banks_free(q):
                pe.wait_ge(s["hadd_ready"], q + 1)
                pe.wait_ge(s["wptv_ready"], q + 1)

            def e_turn(t):
                pe.wait_ge(s["hid_ready"], t + (2 * NFF + 1))
                for b in range(4):
                    last = nc.tensor.transpose(wide(6)[:, P * b:P * b + P], eh[:, b, :], cols("ident"))
                last.then_inc(s["ht_ready"], 1)

            def e_down(at, k, t, first):
                pe.wait_ge(s["lo_ready"], at.u + 1)
                if k == 0:
                    pe.wait_ge(s["alo_ready"], t + (3 * NFF + 1))
                for b in range(2):
                    last = moved(wide(b), hth[:, k, :], htl[:, k, :], at.slot, slice(GW * b, GW * b + GW),
                                 first and k == 0, k == 3)
                last.then_inc(s["unit_done"], 1)

            def scatter(q, u):
                pe.wait_ge(s["yg_ready"], 2 * q + 2)
                for o in range(KB):
                    last = mm(bank[(2, 3, 6, 7)[o // 2]][:, o % 2, :], yg[:, o // 4, P * (o % 4):P * (o % 4) + P],
                              wplace_t, start=True, stop=True)
                last.then_inc(s["ys_ready"], 1)

            pe.wait_ge(s["par_in"], 16)
            walk(pe, nothing, {
                "norm": norm, "xbc": up, "dt": dt, "cum": cum, "xbc_last": nothing, "sc_c": up, "sc_v": up, "sc_b": up,
                "z": up, "ssd_scores": ssd_scores, "ssd_out": ssd_out, "mixdown": mixdown,
                "group_norm": group_norm, "residual": nothing, "f_gate": up, "f_up": up, "f_hid": nothing,
                "d_gate": up, "d_up": up, "d_hid": nothing,
                "down": down, "sv": up, "cgate": up, "cval": up, "sums": sums, "squares": squares,
                "sgu_norm": nothing, "sgu_turn": sgu_turn, "sgu_mix": sgu_mix, "pool": up, "su": su,
                "conv_norm": nothing, "conv": conv, "conv_last": nothing, "route": route, "modulate": nothing, "place": nothing, "gather": gather,
                "turn_place": turn_place, "e_gate": e_gate, "e_up": e_up, "banks_free": banks_free,
                "e_turn": e_turn, "e_down": e_down, "scatter": scatter, "scatter_add": nothing, "experts_done": nothing, "peels": True})

        @block.scalar
        def _(act):
            A, copy = nc.scalar.activation, nc.scalar.copy

            act.wait_ge(s["par_in"], 16)

            def split(at):
                act.wait_ge(loaded[at.slot // 2], 16 * (at.cu // SLOTS) + 16 + 16 * at.i)
                if at.cu >= SLOTS:
                    act.wait_ge(s["unit_done"], at.u - (SLOTS - 1))
                copy(whi[:, at.slot, :], raw[:, at.slot, :]).then_inc(s["hi_ready"], 1)

            def norm(m, eps, how):
                for q in range(4):
                    if m == 0:
                        act.wait_ge(s["x_in"], 16)
                    else:
                        act.wait_ge(s["h_ready"], 4 * (m - 1) + q + 1)
                    A(nf[:, 2 * q:2 * q + 2, :], h[:, 2 * q:2 * q + 2, :], ACT.Square).then_inc(s["sq_ready"], 1)
                act.wait_ge(s["ssq_ready"], m + 1)
                A(row1, bank[0][:, 0, :], ACT.Sqrt, scale=1.0 / D, bias=epsilon(eps)).then_inc(s["root_ready"], 1)
                if how in ("split", "shift"):
                    for k in range(KB):
                        act.wait_ge(s["n_ready"], KB * SPLIT_BEFORE[m] + k + 1)
                        if how == "shift":
                            ins = A(nhi[:, k, :], nf[:, k, :], ACT.Identity, bias=shift(m, k))
                        else:
                            ins = copy(nhi[:, k, :], nf[:, k, :])
                        ins.then_inc(s["nhi_ready"], 1)

            def xbc(at, l, k, b):
                act.wait_ge(s["unit_done"], at.u + 1)
                if k >= 2:
                    act.wait_ge(s["xbc_ready"], 16 * l + k - 1)
                A(ring[:, k % 2, :], at.bank[:, 0, :], ACT.Identity, bias=col(f"xb{l}", b),
                  scale=col(f"xw{l}", 3 * b + 1)).then_inc(s["xlin_ready"], 1)
                if k:
                    xbc_silu(at.n, k - 1)

            def xbc_silu(done, k):
                act.wait_ge(s["psum_free"], done)
                A(area[:, XBC_ORDER[k], :], ring[:, k % 2, :], ACT.Silu).then_inc(s["xbc_ready"], 1)

            def xbc_last(n, l):
                xbc_silu(n, XBC - 1)
                if l == 0:
                    act.wait_ge(s["cond_in"], 16)
                    A(cond[:, :], cond[:, :], ACT.Silu).then_inc(s["cond_ready"], 1)

            def dt(l):
                if l == 0:
                    act.wait_ge(s["late_in"], 16)
                act.wait_ge(s["dtv_ready"], 2 * l + 1)
                A(sml[:, 3, :], sml[:, 2, :], ACT.Exp).then_inc(s["dta_ready"], 1)
                A(sml[:, 7, 0:32], cols(f"alog{l}"), ACT.Exp).then_inc(s["dta_ready"], 1)
                act.wait_ge(s["dtv_ready"], 2 * l + 2)
                A(sml[:, 5, :], sml[:, 4, :], ACT.Ln).then_inc(s["dta_ready"], 1)

            def ssd_scores(l, j):
                it = 8 * l + j
                if j == 0:
                    act.wait_ge(s["cumv_ready"], 3 * (l + 1))
                for r in range(2):
                    hd = 2 * j + r
                    act.wait_ge(s["bc_ready"], 2 * it + r + 1)
                    if it:
                        act.wait_ge(s["prod_ready"], 2 * it + r - 1)
                    for a, b, c, d, t in DECAYS:
                        ins = A(dec[:, r, a:b, :].rearrange("p a b -> p (a b)"),
                                bank[r][:, d, t:t + HALF * (b - a)], ACT.Relu, scale=-1.0,
                                bias=tokF[:, c, 16 * d + hd:16 * d + hd + 1])
                    ins.then_inc(s["clamp_ready"], 1)
                act.wait_ge(s["xtp_ready"], it + 1)
                copy(xtok[:, it % 2, :, :].rearrange("p c x -> p (c x)"),
                     bank[3][:, 1, :]).then_inc(s["xtok_ready"], 1)
                for r in range(2):
                    act.wait_ge(s["clamp_ready"], 2 * it + r + 1)
                    A(dec[:, r, :, :], dec[:, r, :, :], ACT.Exp, scale=-1.0).then_inc(s["dec_ready"], 1)

            def sc_c(at, l, j):
                act.wait_ge(s["psum_free"], at.n)
                act.wait_ge(s["unit_done"], at.u + 1)
                copy(short_c, at.bank[:, 0, :]).then_inc(s["shortc_ready"], 1)

            def sc_v(at, l, j):
                act.wait_ge(s["psum_free"], at.n + 1)
                A(short_q, short_p, ACT.Copy, scale=col(f"sw{l}", 3 * j + 1)).then_inc(s["scq_ready"], 1)

            def sc_b(at, l, j):
                act.wait_ge(s["psum_free"], at.n + 1)
                copy(mhi[:, 8 + j, :], short_m[:, j % 2, :]).then_inc(s["mhi_ready"], 1)

            def z(at, l, j):
                act.wait_ge(s["unit_done"], at.u + 1)
                A(ring[:, j % 2, :], at.bank[:, 0, :], ACT.Silu).then_inc(s["zs_ready"], 1)
                act.wait_ge(s["psum_free"], at.n + 1)
                A(xs[:, j, :], y1[:, j, :], ACT.Square).then_inc(s["ysq_ready"], 1)

            def group_norm(at, l):
                for q in range(2):
                    act.wait_ge(s["psum_free"], at.n + q + 1)
                    A(work[:, 2 * q:2 * q + 2, :], work[:, 2 * q:2 * q + 2, :],
                      ACT.Sqrt).then_inc(s["groot_ready"], 1)
                for k in range(KB):
                    act.wait_ge(s["gy_ready"], 8 * l + k + 1)
                    copy(mhi[:, k, :], y1[:, k, :]).then_inc(s["mhi_ready"], 1)

            def f_lin(at, l, dst, b):
                act.wait_ge(s["unit_done"], at.u + 1)
                A(dst[:, at.par, :], at.bank[:, 0, :], ACT.Identity,
                  bias=par[:, bass.ds(b + COLS[f"fb{l}"][0], 1)],
                  scale=par[:, bass.ds(3 * b + (COLS[f"fw{l}"][0] + 1), 1)]).then_inc(s["flin_ready"], 1)

            def f_gate(at, l):
                f_lin(at, l, fg, at.j - NFF * l)

            def f_up(at, l):
                f_lin(at, l, fu, at.j + (NFF - NFF * l))
                act.wait_ge(s["psum_free"], at.n)
                A(fs[:, at.par, :], fg[:, at.par, :], ACT.Silu).then_inc(s["silu_ready"], 1)

            def f_hid(at, l):
                act.wait_ge(s["hid_ready"], at.j + 1)
                copy(ahi[:, at.par, :], fa[:, at.par, :]).then_inc(s["ahi_ready"], 1)

            def d_gate(at, l):
                act.wait_ge(s["unit_done"], at.u + 1)
                A(fs[:, at.par, :], at.bank[:, 0, :], ACT.Silu).then_inc(s["silu_ready"], 1)

            def d_hid(at, l):
                act.wait_ge(s["psum_free"], at.n)
                copy(ahi[:, at.par, :], fa[:, at.par, :]).then_inc(s["ahi_ready"], 1)

            def squares(at, count, src):
                for b in range(CB):
                    act.wait_ge(s["cen_ready"], CB * (count - 1) + b + 1)
                    last = A(sq3[:, b, :], src[:, b, :], ACT.Square)
                last.then_inc(s["csq_ready"], 1)
                act.wait_ge(s["cssq_ready"], count)
                A(row1, at.bank[:, 1, :], ACT.Sqrt, scale=1.0 / (CB * P), bias=epsilon(EPS2)
                  ).then_inc(s["croot_ready"], 1)

            def sv(at, l, b):
                if b == 0:
                    act.wait_ge(s["nlo_ready"], KB * (SPLIT_BEFORE[2 * DEPTH + 1 + 2 * l] + 1))
                if b < 2:
                    diagonals(l, b)

            def conv(glu_done, l, b):
                if b == 1:
                    act.wait_ge(s["taps_ready"], CB * l + 1)
                    diagonals(l, 2)

            def diagonals(l, b):
                for k in range(PE_TAPS):
                    last = A(diag[b][:, k, :], cols("ident"), ACT.Copy,
                             scale=col(f"cw{l}", TAPS * b + TAPS - PE_TAPS + k))
                last.then_inc(s["diag_ready"], 1)

            def sgu_turn(l):
                for c in range(2):
                    act.wait_ge(s["vtp_ready"], 2 * l + c + 1)
                    copy(vtok[:, c, :], bank[1 + c][:, :, :].rearrange("p a t -> p (a t)")[:, 0:CB * P]
                         ).then_inc(s["vtok_ready"], 1)

            def cgate(at, l, b):
                act.wait_ge(s["unit_done"], at.u + 1)
                if b == 2:
                    act.wait_ge(s["psum_free"], at.n - 2)
                A(sgate[:, b % 2, :], at.bank[:, 0, :], ACT.Sigmoid).then_inc(s["gate_ready"], 1)

            def su(at, l, b):
                act.wait_ge(s["psum_free"], at.n + 1)
                copy(mhi[:, 5 + b, :], gated[:, b, :]).then_inc(s["mhi_ready"], 1)
                if b < 2:
                    act.wait_ge(s["poolv_ready"], 2 * l + b + 1)
                    copy(mhi[:, b, :], pmix[:, b, :]).then_inc(s["mhi_ready"], 1)

            def conv_norm(l):
                for b in range(CB):
                    act.wait_ge(s["cn_ready"], CB * l + b + 1)
                    A(cv[:, b, :], cv[:, b, :], ACT.Silu, bias=col(f"clb{l}", b)).then_inc(s["cs_ready"], 1)
                for b in range(CB):
                    act.wait_ge(s["cs_ready"], CB * l + b + 1)
                    copy(mhi[:, 2 + b, :], cv[:, b, :]).then_inc(s["mhi_ready"], 1)

            def wide(b):
                return bank[b][:, :, :].rearrange("p a t -> p (a t)")

            def route(n):
                for b in range(4):
                    act.wait_ge(s["xt_ready"], b + 1)
                    copy(xth[:, b // 2, GW * (b % 2):GW * (b % 2) + GW], wide(b)).then_inc(s["xth_ready"], 1)
                act.wait_ge(s["rsub_ready"], 2)
                A(sml[:, 3, 0:16], sml[:, 2, 0:16], ACT.Exp).then_inc(s["rexp_ready"], 1)
                act.wait_ge(s["tab_ready"], 1)

            def gather(q):
                act.wait_ge(s["xg_ready"], 2 * q + 1)
                for b in range(2):
                    last = copy(xgh[:, 4 * b:4 * b + 4, :].rearrange("p k t -> p (k t)"), wide(2 + b))
                last.then_inc(s["xgh_ready"], 1)

            def turn_place(q):
                act.wait_ge(s["wpt_ready"], q + 1)
                copy(wplace_t, bank[0][:, 0, :]).then_inc(s["wptv_ready"], 1)

            def e_gate(at, k, t):
                if k == 3:
                    act.wait_ge(s["unit_done"], at.u + 1)
                    act.wait_ge(s["hid_ready"], t + 2 * NFF)
                    A(es, wide(4), ACT.Silu).then_inc(s["silu_ready"], 1)

            def e_turn(t):
                act.wait_ge(s["ht_ready"], t + 1)
                copy(hth.rearrange("p k t -> p (k t)"), wide(6)).then_inc(s["ahi_ready"], 1)

            def scatter(q, u):
                act.wait_ge(s["unit_done"], GU * q + (u + GU))
                for b in range(2):
                    copy(yg[:, b, :], wide(b)).then_inc(s["yg_ready"], 1)

            walk(act, split, {
                "norm": norm, "xbc": xbc, "dt": dt, "cum": nothing, "xbc_last": xbc_last, "sc_c": sc_c, "sc_v": sc_v,
                "sc_b": sc_b, "z": z, "ssd_scores": ssd_scores, "ssd_out": nothing, "mixdown": nothing,
                "group_norm": group_norm, "residual": nothing, "f_gate": f_gate, "f_up": f_up, "f_hid": f_hid,
                "d_gate": d_gate, "d_up": nothing, "d_hid": d_hid, "down": nothing, "sv": sv, "cgate": cgate, "cval": nothing,
                "sums": nothing, "squares": squares, "sgu_norm": nothing, "sgu_turn": sgu_turn,
                "sgu_mix": nothing, "pool": nothing, "su": su, "conv_norm": conv_norm, "route": route,
                "conv": conv, "conv_last": nothing,
                "modulate": nothing, "place": nothing, "gather": gather, "turn_place": turn_place, "e_gate": e_gate,
                "e_up": nothing, "e_turn": e_turn, "e_down": nothing,
                "scatter": scatter, "scatter_add": nothing, "experts_done": nothing, "peels": False})

        @block.gpsimd
        def _(pool):
            def load(g, u):
                pool.dma_start(adaring[g], ada_hbm[u]).then_inc(ada_in[g], 16)

            pool.wait_ge(s["late_in"], 16)
            pool.dma_start(cond[:, :], cond_hbm).then_inc(s["cond_in"], 16)
            for w in range(WINDOWS):
                pool.wait_ge(s["nlo_ready"], KB * (SPLIT_BEFORE[OPENS[w]] + 1))
                for g in range(ASLOTS):
                    load(g, WIN * w + g)
                with pool.Fori(0, WIN // ASLOTS - 1) as k:
                    for g in range(ASLOTS):
                        pool.wait_ge(s["ada_used"], ASLOTS * k + (WIN * w + g + 1))
                        load(g, ASLOTS * k + (WIN * w + ASLOTS + g))

        @block.vector
        def _(dve):
            TT, TS, STT, copy = (nc.vector.tensor_tensor, nc.vector.tensor_scalar,
                                 nc.vector.scalar_tensor_tensor, nc.vector.tensor_copy)
            MUL, ADD, SUB = ALU.mult, ALU.add, ALU.subtract
            ch = Chain(dve, "vchain")

            def split(at):
                dve.wait_ge(s["hi_ready"], at.u + 1)
                TT(wlo[:, at.slot, :], raw[:, at.slot, :], whi[:, at.slot, :].bitcast(F32),
                   SUB).then_inc(s["lo_ready"], 1)

            def rest(dst, src, hi, ready, count, done):
                dve.wait_ge(s[ready], count)
                TT(dst, src, hi.bitcast(F32), SUB).then_inc(s[done], 1)

            def mix_rest(order, b, src):
                rest(mlo[:, b, :], src, mhi[:, b, :], "mhi_ready", order + 1, "mlo_ready")

            def taps(dst, src, w):
                ch.link(STT(dst[:, 1:T], src[:, 0:T - 1], w(0), dst[:, 1:T], MUL, ADD))
                return STT(dst[:, 0:T - 1], src[:, 1:T], w(2), dst[:, 0:T - 1], MUL, ADD)

            def modulation(w):
                a = WIN * w
                dve.wait_ge(s["ada_used"], WIN * (w + 1))
                ch.link(TT(mod[:, a:a + WIN], mod[:, a:a + WIN], col("adab", a, WIN), ADD))
                for g in range(a // KB, (a + WIN) // KB):
                    if g % 3 == 1:
                        name = ("mixg", "ffng")[g // 3 % 2]
                        ins = STT(modg[:, g // 3, :], mod[:, KB * g:KB * g + KB], 1.0, cols(f"{name}{g // 6}"), ADD, MUL)
                ch.link(ins)

            def norm(m, eps, how):
                if m in WINDOW_OF:
                    modulation(WINDOW_OF[m])
                dve.wait_ge(s["root_ready"], m + 1)
                ch.link(nc.vector.reciprocal(rstd[:, :], row1[:, :]))
                for k in range(KB):
                    dst = h if how == "plain" else nf
                    ins = STT(dst[:, k, :], h[:, k, :], gain(m, k), rstd[:, :], MUL, MUL)
                    if how == "plain":
                        if k % 2:
                            ins.then_inc(s["h_ready"], 1)
                    elif how == "last":
                        ins.then_inc(s["fin_ready"], 1)
                    else:
                        if how == "whole":
                            ch.link(ins)
                            ins = TS(nf[:, k, :], nf[:, k, :], shift(m, k), None, ADD)
                        ins.then_inc(s["n_ready"], 1)
                        if k and how != "whole":
                            norm_rest(m, k - 1, how)
                if how in ("split", "shift"):
                    norm_rest(m, KB - 1, how)

            def norm_rest(m, k, how):
                dve.wait_ge(s["nhi_ready"], KB * SPLIT_BEFORE[m] + k + 1)
                hi = nhi[:, k, :].bitcast(F32)
                if how == "shift":
                    ins = STT(nlo[:, k, :], nf[:, k, :], shift(m, k), hi, ADD, SUB)
                else:
                    ins = TT(nlo[:, k, :], nf[:, k, :], hi, SUB)
                ins.then_inc(s["nlo_ready"], 1)

            def xbc(at, l, k, b):
                dve.wait_ge(s["xlin_ready"], 16 * l + k + 1)
                taps(ring[:, k % 2, :], at.bank[:, 0, :],
                     lambda t: col(f"xw{l}", 3 * b + t)).then_inc(s["psum_free"], 1)

            def dt(l):
                if l == 0:
                    dve.wait_ge(s["late_in"], 16)
                a, x, nx, e, u, lnu, ea, t, r, d = (sml[:, k, :] for k in (0, 1, 2, 3, 4, 5, 7, 8, 9, 10))
                dve.wait_ge(s["dt_ready"], l + 1)
                for c in range(2):
                    w = slice(32 * c, 32 * c + 32)
                    ins = TT(x[:, w], bank[0][:, 0, w], cols(f"dtb{l}"), ADD)
                ch.link(ins)
                STT(nx, x, -1.0, x, MUL, ALU.min).then_inc(s["dtv_ready"], 1)
                dve.wait_ge(s["dta_ready"], 3 * l + 1)
                TS(u, e, 1.0, None, ADD).then_inc(s["dtv_ready"], 1)
                dve.wait_ge(s["dtv_ready"], 2 * l + 2)
                ch.link(TS(t, u, -1.0, 1.0, MUL, ADD))
                TT(t, t, e, ADD)
                ch.link(nc.vector.reciprocal(r, u))
                ch.link(TT(t, t, r, MUL))
                dve.wait_ge(s["dta_ready"], 3 * l + 3)
                ch.link(STT(d, x, 0.0, lnu, ALU.max, ADD))
                ch.link(TT(d, d, t, ADD))
                for c in range(2):
                    w = slice(32 * c, 32 * c + 32)
                    ins = STT(a[:, w], d[:, w], -1.0, ea[:, 0:32], MUL, MUL)
                ins.then_inc(s["a_ready"], 1)

            def cum(l):
                dve.wait_ge(s["cum_ready"], l + 1)
                copy(tokF[:, :, :].rearrange("p c h -> p (c h)"), bank[1][:, 0, 0:64]).then_inc(s["cumv_ready"], 1)
                copy(rowF[:, 0, :], bank[2][0:16, 0, :]).then_inc(s["cumv_ready"], 1)
                copy(rowF[:, 1, :], bank[3][0:16, 0, :]).then_inc(s["cumv_ready"], 1)

            def ssd_scores(l, j):
                g, it = j // 2, 8 * l + j
                triu, tril = col("triu", 0, P), cols("tril")
                if j % 2 == 0:
                    sc = bank[2][:, :, :].rearrange("p c (b t) -> p (c b) t", b=2)
                    dve.wait_ge(s["score_ready"], 4 * l + g + 1)
                    TT(s6[:, 0, :], sc[:, 0, :], triu, MUL)
                    copy(s6[:, 1:3, :], sc[:, 1:3, :])
                    TT(s6[:, 3, :], sc[:, 3, :], tril, MUL)
                    TT(s6[:, 4, :], sc[:, 0, :], tril, MUL)
                    TT(s6[:, 5, :], sc[:, 3, :], triu, MUL).then_inc(s["s6_ready"], 1)
                    dve.wait_ge(s["s6_ready"], 4 * l + g + 1)
                dts = sml[:, 10, :].rearrange("p (c h) -> p c h", c=2)
                for r in range(2):
                    hd = 2 * j + r
                    dve.wait_ge(s["dec_ready"], 2 * it + r + 1)
                    for a, b, c, d, t in DECAYS:
                        ins = STT(prod[:, r, a:b, :], dec[:, r, a:b, :], dts[:, c, 16 * d + hd:16 * d + hd + 1],
                                  s6[:, a:b, :], MUL, MUL)
                    ch.link(ins)
                    TT(prod[:, r, 0:4:3, :], prod[:, r, 0:4:3, :], prod[:, r, 4:6, :], ADD).then_inc(s["prod_ready"], 1)

            def ssd_out(l, j):
                it = 8 * l + j
                dve.wait_ge(s["y_ready"], it + 1)
                STT(y1[:, j, :], xs[:, j, :], col(f"skip{l}", j), bank[3][:, 0, :], MUL, ADD).then_inc(s["y1_ready"], 1)
                mix_rest(16 * l + j, 8 + j, short_m[:, j % 2, :])

            def sc_v(at, l, j):
                dve.wait_ge(s["unit_done"], at.u + 1)
                dve.wait_ge(s["shortc_ready"], 8 * l + j + 1)
                TT(short_p, short_c, at.bank[:, 0, :], MUL).then_inc(s["psum_free"], 2)

            def sc_b(at, l, j):
                dve.wait_ge(s["scq_ready"], 8 * l + j + 1)
                ch.link(taps(short_q, short_p, lambda t: col(f"sw{l}", 3 * j + t)))
                dve.wait_ge(s["unit_done"], at.u + 1)
                TT(short_m[:, j % 2, :], short_q, at.bank[:, 0, :], MUL).then_inc(s["psum_free"], 1)

            def z(at, l, j):
                dve.wait_ge(s["zs_ready"], 8 * l + j + 1)
                if j == 0:
                    dve.wait_ge(s["y1_ready"], 8 * l + 8)
                TT(y1[:, j, :], y1[:, j, :], ring[:, j % 2, :], MUL).then_inc(s["psum_free"], 1)

            def group_norm(at, l):
                for q in range(2):
                    dve.wait_ge(s["gssq_ready"], 4 * l + 2 * q + 2)
                    TS(work[:, 2 * q:2 * q + 2, :], bank[4 + (at.cn + q) % 4][:, :, :], 4.0 / D, EPS1,
                       MUL, ADD).then_inc(s["psum_free"], 1)
                for q in range(2):
                    dve.wait_ge(s["groot_ready"], 2 * l + q + 1)
                    ins = nc.vector.reciprocal(work[:, 2 * q:2 * q + 2, :], work[:, 2 * q:2 * q + 2, :])
                ch.link(ins)
                for k in range(KB):
                    STT(y1[:, k, :], y1[:, k, :], col(f"gn{l}", k), work[:, k // 2, :],
                        MUL, MUL).then_inc(s["gy_ready"], 1)
                    if k:
                        mix_rest(16 * l + 7 + k, k - 1, y1[:, k - 1, :])
                mix_rest(16 * l + 15, KB - 1, y1[:, KB - 1, :])

            residuals = [0]

            def residual(u, gate):
                for k in range(KB):
                    if k % 2 == 0 and k < KB - 2:
                        dve.wait_ge(s["bank_done"], 3 * residuals[0] + k // 2 + 1)
                    elif k == KB - 2:
                        dve.wait_ge(s["unit_done"], u)
                    if gate is None and k % 2:
                        TT(h[:, k - 1:k + 1, :], bank[k // 2][:, :, :], h[:, k - 1:k + 1, :],
                           ADD).then_inc(s["h_ready"], 1)
                    elif gate is not None:
                        ins = STT(h[:, k, :], bank[k // 2][:, k % 2, :], mod[:, gate + k:gate + k + 1],
                                  h[:, k, :], MUL, ADD)
                        if k % 2:
                            ins.then_inc(s["h_ready"], 1)
                residuals[0] += 1

            def f_taps(at, l, dst, b):
                taps(dst[:, at.par, :], at.bank[:, 0, :],
                     lambda t: par[:, bass.ds(3 * b + (COLS[f"fw{l}"][0] + t), 1)]).then_inc(s["psum_free"], 1)

            def f_gate(at, l):
                dve.wait_ge(s["flin_ready"], 2 * at.j + 1)
                f_taps(at, l, fg, at.j - NFF * l)

            def f_up(at, l):
                dve.wait_ge(s["flin_ready"], 2 * at.j + 2)
                f_taps(at, l, fu, at.j + (NFF - NFF * l))
                dve.wait_ge(s["silu_ready"], at.j + 1)
                dve.wait_ge(s["psum_free"], at.n + 1)
                TT(fa[:, at.par, :], fs[:, at.par, :], fu[:, at.par, :], MUL).then_inc(s["hid_ready"], 1)

            def modulate(w, i, g):
                if g == 0:
                    dve.wait_ge(s["cond_ready"], 1)
                dve.wait_ge(ada_in[g], 16 * i + (16 * (WIN // ASLOTS) * w + 16))
                STT(adaring[g], adaring[g], 1.0, cond[:, :], MUL, MUL,
                    accum_out=mod[:, bass.ds(ASLOTS * i + (WIN * w + g), 1)]).then_inc(s["ada_used"], 1)

            def hid(at, l):
                rest(alo[:, at.par, :], fa[:, at.par, :], ahi[:, at.par, :], "ahi_ready", at.j + 1, "alo_ready")

            def d_up(at, l):
                dve.wait_ge(s["silu_ready"], at.j + 1)
                dve.wait_ge(s["unit_done"], at.u + 1)
                TT(fa[:, at.par, :], fs[:, at.par, :], at.bank[:, 0, :], MUL).then_inc(s["psum_free"], 2)

            def sv(at, l, b):
                if b == 0:
                    ch.link(nc.vector.memset(flat[:, 0:(CB + 1) * PADW], 0.0))
                dve.wait_ge(s["unit_done"], at.u + 1)
                copy(vv[:, b, :], at.bank[:, 0, :]).then_inc(s["psum_free"], 1)

            def squares(at, count, src):
                dve.wait_ge(s["sum_ready"], count)
                ch.link(TS(nmean, at.bank[:, 0, :], -1.0 / (CB * P), None, MUL))
                for b in range(CB):
                    TT(src[:, b, :], src[:, b, :], nmean, ADD).then_inc(s["cen_ready"], 1)
                dve.wait_ge(s["croot_ready"], count)
                nc.vector.reciprocal(rstd, row1).then_inc(s["psum_free"], 1)
                dve.wait_ge(s["psum_free"], at.n + 1)

            def sgu_norm(l):
                for b in range(CB):
                    last = STT(vv[:, b, :], vv[:, b, :], col(f"slg{l}", b), rstd[:, :], MUL, MUL)
                ch.link(last)
                for b in range(CB):
                    last = TS(vv[:, b, :], vv[:, b, :], col(f"slb{l}", b), None, ADD)
                last.then_inc(s["vn_ready"], 1)

            def cval(at, l, b):
                dve.wait_ge(s["gate_ready"], CB * l + b + 1)
                dve.wait_ge(s["unit_done"], at.u + 1)
                TT(glu[:, b, 15:15 + T], sgate[:, b % 2, :], at.bank[:, 0, :], MUL).then_inc(s["psum_free"], 2)

            def conv(glu_done, l, b):
                if b:
                    conv_add(l, b - 1)
                dve.wait_ge(s["psum_free"], glu_done)
                ins = TS(cv[:, b, :], glu[:, b, 0:T], col(f"cw{l}", TAPS * b), col(f"cb{l}", b), MUL, ADD)
                for t in range(1, TAPS - PE_TAPS):
                    ch.link(ins)
                    ins = STT(cv[:, b, :], glu[:, b, t:t + T], col(f"cw{l}", TAPS * b + t), cv[:, b, :], MUL, ADD)
                ch.mark(ins)

            def conv_add(l, b):
                ch.wait()
                dve.wait_ge(s["taps_ready"], CB * l + b + 1)
                TT(cv[:, b, :], conv_bank(b), cv[:, b, :], ADD).then_inc(s["taps_added"], 1)

            def conv_last(l):
                conv_add(l, CB - 1)
                dve.wait_ge(s["taps_added"], CB * (l + 1))

            def pool(at, l, b):
                x, s2, s4, s8, d = (pl[:, k, :] for k in (0, 1, 2, 3, 4 + b))
                w = slice(16, 16 + T)
                dve.wait_ge(s["unit_done"], at.u + 1)
                if b:
                    dve.wait_ge(s["diff_ready"], 2 * l + b)
                copy(x[:, w], at.bank[:, 0, :]).then_inc(s["psum_free"], 1)
                dve.wait_ge(s["psum_free"], at.n + 1)
                ch.link(TT(s2[:, 1:PADW], x[:, 0:PADW - 1], x[:, 1:PADW], ADD))
                ch.link(TT(s4[:, 2:PADW - 1], s2[:, 1:PADW - 2], s2[:, 3:PADW], ADD))
                low, high = s2, s4
                if b:
                    ch.link(TT(s8[:, 4:PADW - 4], s4[:, 2:PADW - 6], s4[:, 6:PADW - 2], ADD))
                    ch.link(TT(s2[:, w], s8[:, 12:12 + T], s8[:, 20:20 + T], ADD))
                    low, high = s8, s2
                rc = col("rcount", T * b, T)
                TT(d[0:64, w], low[0:64, w], rc[0:64, :], MUL)
                ch.link(TT(d[64:128, w], high[64:128, w], rc[64:128, :], MUL))
                TT(d[:, w], d[:, w], x[:, w], SUB).then_inc(s["diff_ready"], 1)

            def su(at, l, b):
                if b == 0:
                    dve.wait_ge(s["smix_ready"], l + 1)
                    for o, mixed in enumerate((bank[1][:, 0, :], bank[1][:, 1, :], bank[2][:, 0, :])):
                        for c in range(2):
                            w = slice(HALF * c, HALF * c + HALF)
                            ins = TT(gated[:, o, w], mixed[:, w], col(f"sgub{l}", P * o, P), ADD)
                    ch.link(ins)
                dve.wait_ge(s["unit_done"], at.u + 1)
                TT(gated[:, b, :], gated[:, b, :], at.bank[:, 0, :], MUL).then_inc(s["psum_free"], 1)
                mix_rest(MIX2 + 8 * l + 2 * b, 5 + b, gated[:, b, :])
                if b < 2:
                    dve.wait_ge(s["pool_ready"], 2 * l + b + 1)
                    TS(pmix[:, b, :], bank[(3, 0)[b]][:, 0, :], col(f"pscale{l}", b), None,
                       MUL).then_inc(s["poolv_ready"], 1)
                    mix_rest(MIX2 + 8 * l + 2 * b + 1, b, pmix[:, b, :])

            def conv_norm(l):
                for b in range(CB):
                    STT(cv[:, b, :], cv[:, b, :], col(f"clg{l}", b), rstd[:, :], MUL, MUL).then_inc(s["cn_ready"], 1)
                for b in range(CB):
                    mix_rest(MIX2 + 8 * l + 5 + b, 2 + b, cv[:, b, :])

            def wide(b):
                return bank[b][:, :, :].rearrange("p a t -> p (a t)")

            def route(n):
                lg, sub, ex, gt, eq, rk = (sml[:, k, :] for k in (1, 2, 3, 8, 9, 10))
                comb, sel, tab = sml[:, 6, :], sml[:, 11, 0:16], sml[:, 4, :]
                pos, cnt, over, before_me = sml[:, 5, 0:16], sml[:, 5, 16:24], sml[:, 5, 24:32], sml[:, 5, 32:40]
                g3, e3 = (a.rearrange("p (e j) -> p e j", e=NEXP) for a in (gt, eq))
                before = cols("before").rearrange("p (e j) -> p e j", e=NEXP)

                def across(a):
                    return a.rearrange("p (e j) -> p e j", e=1).to_broadcast([P, NEXP, NEXP])
                dve.wait_ge(s["logit_ready"], 1)
                for c in range(2):
                    w = slice(8 * c, 8 * c + 8)
                    ins = TT(lg[:, w], bank[7][:, 0, w], cols("rb"), ADD)
                ch.link(ins)
                for c in range(2):
                    w = slice(8 * c, 8 * c + 8)
                    own = lg[:, w].rearrange("p (e j) -> p e j", j=1).to_broadcast([P, NEXP, NEXP])
                    TT(g3, across(lg[:, w]), own, ALU.is_gt)
                    ch.link(TT(e3, across(lg[:, w]), own, ALU.is_equal))
                    ch.link(TT(e3, e3, before, MUL))
                    ch.link(TT(g3, g3, e3, ADD))
                    nc.vector.tensor_reduce(rk[:, w], g3, AX.X, ADD)
                    ch.link(nc.vector.tensor_reduce(rk[:, 16 + c:17 + c], lg[:, w], AX.X, ALU.max))
                    TS(sub[:, w], lg[:, w], rk[:, 16 + c:17 + c], None, SUB).then_inc(s["rsub_ready"], 1)
                TS(sel, rk[:, 0:16], 1.5, None, ALU.is_lt).then_inc(s["sel_ready"], 1)
                for b in range(4):
                    w = slice(GW * (b % 2), GW * (b % 2) + GW)
                    dve.wait_ge(s["xth_ready"], b + 1)
                    TT(xtl[:, b // 2, w], wide(b), xth[:, b // 2, w].bitcast(F32), SUB).then_inc(s["xtl_ready"], 1)
                dve.wait_ge(s["rexp_ready"], 1)
                dve.wait_ge(s["sel_ready"], 1)
                ch.link(TT(comb[:, 0:16], ex[:, 0:16], sel, MUL))
                for c in range(2):
                    ins = nc.vector.tensor_reduce(rk[:, 48 + c:49 + c], comb[:, 8 * c:8 * c + 8], AX.X, ADD)
                ch.link(ins)
                ch.link(nc.vector.reciprocal(rk[:, 50:52], rk[:, 48:50]))
                for c in range(2):
                    w = slice(8 * c, 8 * c + 8)
                    TS(comb[:, w], comb[:, w], rk[:, 50 + c:51 + c], None, MUL)
                dve.wait_ge(s["count_ready"], 1)
                ch.link(TT(pos, bank[7][:, 1, 0:16], sel, MUL))
                TS(pos, pos, -1.0, None, ADD)
                ch.link(TS(over, bank[7][:, 1, 16:24], CAP + 0.5, None, ALU.is_gt))
                ch.link(TT(e3, across(over), before, MUL))
                ch.link(nc.vector.tensor_reduce(before_me, e3, AX.X, ADD))
                ch.link(nc.vector.memset(tab[:, 0:16], 0.0))
                copy(tab[:, 0:NEXP], col("iota", 0, NEXP))
                for x in range(MORE):
                    ch.link(TS(cnt, before_me, float(x), None, ALU.is_equal))
                    ch.link(TT(cnt, cnt, over, MUL))
                    ch.link(TT(cnt, cnt, col("iota", 0, NEXP), MUL))
                    ch.link(nc.vector.tensor_reduce(tab[:, NEXP + x:NEXP + x + 1], cnt, AX.X, ADD))
                ch.link(nc.vector.tensor_reduce(tab[:, 15:16], over, AX.X, ADD))
                ch.link(TS(tab[:, 15:16], tab[:, 15:16], float(NEXP), None, ADD))
                copy(itab[:, :], tab[:, 0:16]).then_inc(s["tab_ready"], 1)
                dve.wait_ge(s["xtl_ready"], 4)
                dve.wait_ge(s["tab_ready"], 1)
                nc.vector.memset(token[:, :], 0.0).then_inc(s["hadd_ready"], 1)

            def place_tokens(q):
                e = dve.value_load(itab[0:1, bass.ds(q, 1)], min_val=0, max_val=NEXP - 1)
                off = col("offset", 0, 16)[:, bass.ds(q, 1)]
                for c in range(2):
                    pos = sml[:, 5, bass.ds(e + 8 * c, 1)]
                    ins = TS(place[:, c, :], cols("iota"), off, pos, ADD, ALU.is_equal)
                ins.then_inc(s["place_ready"], 1)
                dve.wait_ge(s["place_ready"], 2 * q + 1)
                for c in range(2):
                    ins = TS(wplace[:, c, :], place[:, c, :].bitcast(F32), sml[:, 6, bass.ds(e + 8 * c, 1)], None, MUL)
                ins.then_inc(s["place_ready"], 1)

            def gather(q):
                dve.wait_ge(s["xg_ready"], 2 * q + 2)
                for b in range(2):
                    last = copy(xgl[:, 4 * b:4 * b + 4, :].rearrange("p k t -> p (k t)"), wide(4 + b))
                last.then_inc(s["xgl_ready"], 1)

            def e_up(at, k, t):
                if k == 3:
                    dve.wait_ge(s["silu_ready"], 3 * NFF + 1 + t)
                    dve.wait_ge(s["unit_done"], at.u + 1)
                    TT(eh.rearrange("p k t -> p (k t)"), es, wide(5), MUL).then_inc(s["hid_ready"], 1)

            def e_turn(t):
                dve.wait_ge(s["ahi_ready"], 3 * NFF + 1 + t)
                TT(htl.rearrange("p k t -> p (k t)"), wide(6), hth.rearrange("p k t -> p (k t)").bitcast(F32),
                   SUB).then_inc(s["alo_ready"], 1)

            def scatter_add(q):
                dve.wait_ge(s["ys_ready"], q + 1)
                gate = 48 * (DEPTH - 1) + 40
                for k in range(KB):
                    last = STT(h[:, k, :], bank[(2, 3, 6, 7)[k // 2]][:, k % 2, :], mod[:, gate + k:gate + k + 1],
                               h[:, k, :], MUL, ADD)
                last.then_inc(s["hadd_ready"], 1)

            def experts_done(passes):
                dve.wait_ge(s["hadd_ready"], passes + 1)
                nc.vector.memset(token[:, :], 0.0).then_inc(s["h_ready"], 4)

            dve.wait_ge(s["par_in"], 16)
            walk(dve, split, {
                "norm": norm, "xbc": xbc, "dt": dt, "cum": cum, "xbc_last": nothing, "sc_c": nothing, "sc_v": sc_v,
                "sc_b": sc_b, "z": z, "ssd_scores": ssd_scores, "ssd_out": ssd_out, "mixdown": nothing,
                "group_norm": group_norm, "residual": residual, "f_gate": f_gate, "f_up": f_up, "f_hid": hid,
                "d_gate": nothing, "d_up": d_up, "d_hid": hid, "down": nothing, "sv": sv,
                "cgate": nothing, "cval": cval, "sums": nothing, "squares": squares,
                "sgu_norm": sgu_norm, "sgu_turn": nothing, "sgu_mix": nothing, "pool": pool, "su": su,
                "conv_norm": conv_norm, "conv": conv, "conv_last": conv_last, "route": route, "modulate": modulate, "place": place_tokens, "gather": gather,
                "turn_place": nothing, "e_gate": nothing, "e_up": e_up,
                "e_turn": e_turn, "e_down": nothing, "scatter": nothing, "scatter_add": scatter_add, "experts_done": experts_done,
                "peels": False}, ch)


def _up(w):
    k, n = w.shape
    return w.reshape(k // P, P, n // P, P).transpose(2, 1, 0, 3).reshape(n // P, P, UW)


def _down(w):
    return w.reshape(-1, P, UW)


def _hidden(units, gate, up, down):
    g, u, d = _up(gate), _up(up), _down(down)
    for j in range(len(g)):
        units += [g[j], u[j]] + ([d[j - 1]] if j else [])
    units.append(d[-1])


def _stream(i):
    units = []
    for l in range(DEPTH):
        w = i["w_in"][l]
        xbc, short = _up(w[:, 1024:3072]), [_up(w[:, a:a + D]) for a in (4128, 5152, 3104)]
        units += [xbc[b] for b in [8, 9, 10, 11, 12, 13, 14, 15, 0, 1, 2, 3, 4, 5, 6, 7]]
        units += [short[t][j] for j in range(KB) for t in range(3)]
        units += list(_up(w[:, 0:D]))
        wo = _down(i["w_out"][l])
        units += [wo[(k + 8) % 16] for k in range(16)]
        f = i["w_ffn_up"][l]
        _hidden(units, f[:, 0:NFF * P], f[:, NFF * P:], i["w_ffn_down"][l])
    for l in range(DEPTH):
        w = _up(i["w_in_2"][l])
        order = [11, 12, 13, 5, 2, 6, 3, 7, 4, 0, 1, 8, 9, 10]
        units += [w[b] for b in order]
        wo = _down(i["w_out_2"][l])
        units += [wo[b] for b in [5, 0, 6, 1, 7, 2, 3, 4]]
        if l == 0:
            _hidden(units, i["ffn_w_gate_2"][0], i["ffn_w_up_2"][0], i["ffn_w_down_2"][0])
        else:
            for e in range(NEXP):
                g, u = (i[name][0, e].reshape(4, 2, P, GROUPS, GW).transpose(3, 0, 2, 1, 4)
                        .reshape(GROUPS, 4, P, UW) for name in ("moe_w_gate_2", "moe_w_up_2"))
                d = _down(i["moe_w_down_2"][0, e]).reshape(GROUPS, 4, P, UW)
                for k in range(GROUPS):
                    units += [*g[k], *u[k]] + ([*d[k - 1]] if k else [])
                units += [*d[-1]]
    assert len(units) == UNITS
    out = np.empty((UNITS // 2, P, 2 * UW), np.float32)
    for n, a in enumerate(units):
        out[n // 2, :, UW * (n % 2):UW * (n % 2) + UW] = a
    return out


def _params(i):
    par = np.zeros((P, NCOLS), np.float32)

    def put(name, a, rows=P):
        at, width = COLS[name]
        par[0:rows, at:at + width] = a

    def feat(v):
        v = np.asarray(v)
        v = v.reshape(-1, v.shape[-1] // P, P)
        return v.transpose(2, 1, 0).reshape(P, -1)

    def all_rows(v):
        return np.broadcast_to(np.asarray(v).reshape(1, -1), (P, np.size(v)))

    for l in range(DEPTH):
        put(f"norm1{l}", feat(i["norm1_w"][l]))
        put(f"norm2{l}", feat(i["norm2_w"][l]))
        put(f"xw{l}", feat(i["conv_xbc_w"][l]))
        put(f"xb{l}", feat(i["conv_xbc_b"][l]))
        put(f"sw{l}", feat(i["sc_conv_w"][l]))
        put(f"gn{l}", feat(i["ssd_norm_w"][l]))
        put(f"skip{l}", feat(np.repeat(i["d_skip"][l], 64)))
        put(f"fw{l}", feat(i["ffn_conv_w"][l]))
        put(f"fb{l}", feat(i["ffn_conv_b"][l]))
        put(f"dtb{l}", all_rows(np.concatenate([i["dt_bias_f"][l], i["dt_bias_b"][l]])))
        put(f"alog{l}", all_rows(np.concatenate([i["a_log_f"][l], i["a_log_b"][l]])))
        wdt = i["w_in"][l][:, 3072:3104]
        put(f"wdt{l}", wdt.reshape(KB, P, 32).transpose(1, 0, 2).reshape(P, -1))
        put(f"mixg{l}", feat(i["mix_norm_g_2"][l]))
        put(f"ffng{l}", feat(i["ffn_norm_g_2"][l]))
        put(f"pscale{l}", feat(i["pool_scale_2"][l]))
        put(f"cw{l}", feat(i["conv_w_2"][l]))
        for name, key in (("cb", "conv_b_2"), ("clg", "conv_ln_g_2"), ("clb", "conv_ln_b_2"),
                          ("slg", "sgu_ln_g_2"), ("slb", "sgu_ln_b_2"), ):
            put(f"{name}{l}", feat(i[key][l]))
        pw = np.zeros((P, 2, P), np.float32)
        for g in range(4):
            r = slice(64 * (g % 2), 64 * (g % 2) + 64)
            pw[r, g // 2, r] = i["pool_w_2"][l][g]
        put(f"pw{l}", pw.reshape(P, -1))
        put(f"sguw{l}", i["sgu_w_2"][l].transpose(2, 0, 1).reshape(P, -1))
        b = i["sgu_b_2"][l].reshape(CB, 2, P)
        put(f"sgub{l}", np.repeat(b, 64, axis=1).transpose(1, 0, 2).reshape(P, -1))
    put("adab", feat(i["ada_b_2"].reshape(-1)))
    put("final1", feat(i["final_norm_w"]))
    put("final2", feat(i["final_norm_g_2"]))
    put("rw", i["router_w_2"][0].reshape(KB, P, NEXP).transpose(1, 0, 2).reshape(P, -1))
    put("rb", all_rows(i["router_b_2"][0]))
    put("ident", np.eye(P))
    put("ones", 1.0)
    put("eps", [EPS1, EPS2])
    put("triu", np.triu(np.ones((P, P))))
    put("tril", np.tril(np.ones((P, P))))
    t = np.arange(T)
    rc = np.zeros((P, 2, T))
    for g, w in enumerate((2, 4, 8, 16)):
        count = np.clip(t + w // 2, 0, T) - np.clip(t - w // 2, 0, T)
        rc[64 * (g % 2):64 * (g % 2) + 64, g // 2, :] = 1.0 / count
    put("rcount", rc.reshape(P, -1))
    e = np.arange(NEXP)
    put("before", all_rows((e[None, :] < e[:, None]).astype(np.float32)))
    put("iota", np.arange(P))
    put("offset", np.where(np.arange(16) < NEXP, 0.0, CAP))
    return par


def kernel(**inputs):
    import concourse.bacc as bacc
    from concourse.bass_utils import run_bass_kernel_spmd as run

    i = {k: np.asarray(v) for k, v in inputs.items()}
    ada = i["ada_w_2"].reshape(DEPTH, D, 48, P).transpose(0, 2, 3, 1).reshape(ADA, P, UW)
    arrays = {
        "weights": _stream(i),
        "ada": np.ascontiguousarray(ada),
        "cond_rows": np.ascontiguousarray(np.broadcast_to(i["c_2"].reshape(1, D), (P, D))),
        "x_t": np.ascontiguousarray(i["x"][0].T.reshape(KB, P, T).transpose(1, 0, 2)).reshape(P, KB * T),
        "params": _params(i),
    }
    nc = bacc.Bacc("TRN2", target_bir_lowering=False, num_devices=1)
    args = [nc.dram_tensor(name, a.shape, F32, kind="ExternalInput").ap() for name, a in arrays.items()]
    out = nc.dram_tensor("out_t", (P, KB * T), F32, kind="ExternalOutput").ap()
    build(nc, *args, out)
    r = run(nc, [arrays], core_ids=[0])
    got = r.results[0]["out_t"].reshape(P, KB, T)
    return got.transpose(2, 1, 0).reshape(1, T, D)
```
